# Optimizing a Trainium2 kernel written in Bass

```python
import math
import jax, jax.numpy as jnp
from jax import lax
import numpy as np

D_MODEL = 1024
BATCH = 1
SEQ = 1024
DEPTH = 1

CHUNK = 64
GDN_DK = 128
GDN_DV = 128
GDN_HEADS = D_MODEL // (2 * GDN_DV)
GDN_CONV = 4
SWA_HEAD_DIM = 64
SWA_HEADS = D_MODEL // (2 * SWA_HEAD_DIM)
SWA_KV_HEADS = 2
SWA_GROUP = SWA_HEADS // SWA_KV_HEADS
WINDOW = 128
WINDOW_CHUNKS = WINDOW // CHUNK
ROPE_THETA = 500000.0
ROT_DIM = SWA_HEAD_DIM // 4
D_FF = 2816
FFN_CONV = 3
EPS = 1e-6

MIX_A = GDN_HEADS * GDN_DV
MIX_B = SWA_HEADS * SWA_HEAD_DIM
MIX_WIDTH = MIX_A + MIX_B
GDN_CONV_CH = 2 * GDN_HEADS * GDN_DK + GDN_HEADS * GDN_DV
IN_SPLITS = (GDN_HEADS * GDN_DK, GDN_HEADS * GDN_DK, GDN_HEADS * GDN_DV, GDN_HEADS * GDN_DV,
             GDN_HEADS, GDN_HEADS,
             SWA_HEADS * SWA_HEAD_DIM, SWA_KV_HEADS * SWA_HEAD_DIM, SWA_KV_HEADS * SWA_HEAD_DIM)
IN_WIDTH = sum(IN_SPLITS)

kernel_name = "hybrid_gdn_swa_sink_convffn_block"

def _split_points(sizes):
    return [int(v) for v in np.cumsum(np.array(sizes))[:-1]]

def rms_norm(x, w):
    xf = x.astype(jnp.float32)
    y = xf * lax.rsqrt(jnp.mean(xf * xf, axis=-1, keepdims=True) + EPS)
    return (y * w.astype(jnp.float32)).astype(x.dtype)

def l2_normalize(x):
    xf = x.astype(jnp.float32)
    return xf * lax.rsqrt(jnp.sum(xf * xf, axis=-1, keepdims=True) + EPS)

def causal_depthwise_conv(x, w):
    k_width = w.shape[0]
    s = x.shape[1]
    xp = jnp.pad(x, ((0, 0), (k_width - 1, 0), (0, 0)))
    y = xp[:, 0:s, :] * w[0].astype(x.dtype)
    for k in range(1, k_width):
        y = y + xp[:, k:k + s, :] * w[k].astype(x.dtype)
    return y

def partial_rope(x, cos, sin):
    xr = x[..., :ROT_DIM].astype(jnp.float32)
    x1, x2 = jnp.split(xr, 2, axis=-1)
    c = cos[None, :, None, :]
    s = sin[None, :, None, :]
    rot = jnp.concatenate([x1 * c - x2 * s, x2 * c + x1 * s], axis=-1).astype(x.dtype)
    return jnp.concatenate([rot, x[..., ROT_DIM:]], axis=-1)

def chunk_band(t):
    b, s, h, d = t.shape
    n = s // CHUNK
    tc = t.reshape(b, n, CHUNK, h, d)
    padded = jnp.pad(tc, ((0, 0), (WINDOW_CHUNKS - 1, 0), (0, 0), (0, 0), (0, 0)))
    parts = [padded[:, j:j + n] for j in range(WINDOW_CHUNKS)]
    return jnp.concatenate(parts, axis=2)

def sliding_window_sink_attention(q, k, v, sinks):
    b, s = q.shape[0], q.shape[1]
    n = s // CHUNK
    qc = q.reshape(b, n, CHUNK, SWA_KV_HEADS, SWA_GROUP, SWA_HEAD_DIM)
    kb = chunk_band(k)
    vb = chunk_band(v)
    scores = jnp.einsum('bnqhgd,bnkhd->bnhgqk', qc, kb).astype(jnp.float32) * (SWA_HEAD_DIM ** -0.5)
    key_chunk = (jnp.arange(n)[:, None] - (WINDOW_CHUNKS - 1)
                 + (jnp.arange(WINDOW_CHUNKS * CHUNK)[None, :] // CHUNK))
    valid = key_chunk >= 0
    scores = jnp.where(valid[None, :, None, None, None, :], scores, -jnp.inf)
    sink = jnp.broadcast_to(sinks.astype(jnp.float32).reshape(1, 1, SWA_KV_HEADS, SWA_GROUP, 1, 1),
                            scores.shape[:-1] + (1,))
    probs = jax.nn.softmax(jnp.concatenate([scores, sink], axis=-1), axis=-1)[..., :-1]
    out = jnp.einsum('bnhgqk,bnkhd->bnqhgd', probs.astype(v.dtype), vb)
    return out.reshape(b, s, SWA_HEADS * SWA_HEAD_DIM)

def gated_delta_rule(q, k, v, g, beta):
    b, s, h, dk = q.shape
    dv = v.shape[-1]
    n = s // CHUNK
    q = q * (dk ** -0.5)

    def to_chunks(t):
        return t.reshape(b, n, CHUNK, h, -1).transpose(0, 1, 3, 2, 4)

    qc, kc, vc = to_chunks(q), to_chunks(k), to_chunks(v)
    gc = g.reshape(b, n, CHUNK, h).transpose(0, 1, 3, 2)
    bc = beta.reshape(b, n, CHUNK, h).transpose(0, 1, 3, 2)
    gcum = jnp.cumsum(gc, axis=-1)
    idx = jnp.arange(CHUNK)
    lower_incl = idx[:, None] >= idx[None, :]
    strict = idx[:, None] > idx[None, :]
    decay = jnp.exp(jnp.where(lower_incl, gcum[..., :, None] - gcum[..., None, :], -jnp.inf))
    kbeta = kc * bc[..., None]
    l_mat = jnp.where(strict, jnp.einsum('bnhid,bnhjd->bnhij', kbeta, kc) * decay, 0.0)
    a_mat = jnp.eye(CHUNK, dtype=jnp.float32) + l_mat
    rhs = jnp.concatenate([vc * bc[..., None], kbeta * jnp.exp(gcum)[..., None]], axis=-1)
    sol = lax.linalg.triangular_solve(a_mat, rhs, left_side=True, lower=True, unit_diagonal=True)
    u, w = sol[..., :dv], sol[..., dv:]
    qk = jnp.where(lower_incl, jnp.einsum('bnhid,bnhjd->bnhij', qc, kc) * decay, 0.0)
    q_dec = qc * jnp.exp(gcum)[..., None]
    k_dec = kc * jnp.exp(gcum[..., -1:] - gcum)[..., None]
    g_last = jnp.exp(gcum[..., -1])

    def step(state, xs):
        qk_n, q_dec_n, k_dec_n, u_n, w_n, g_last_n = xs
        v_new = u_n - jnp.einsum('bhck,bhkv->bhcv', w_n, state)
        o = (jnp.einsum('bhck,bhkv->bhcv', q_dec_n, state)
             + jnp.einsum('bhij,bhjv->bhiv', qk_n, v_new))
        state = state * g_last_n[..., None, None] + jnp.einsum('bhck,bhcv->bhkv', k_dec_n, v_new)
        return state, o

    xs = tuple(jnp.moveaxis(t, 1, 0) for t in (qk, q_dec, k_dec, u, w, g_last))
    state0 = jnp.zeros((b, h, dk, dv), jnp.float32)
    _, o = lax.scan(step, state0, xs)
    return o.transpose(1, 0, 3, 2, 4).reshape(b, s, h, dv)

def hybrid_layer(x, g_pre_mix, w_in, gdn_conv_w, gdn_A_log, gdn_dt_bias, gdn_norm_w, attn_sinks,
                 w_out, g_post_mix, g_pre_ffn, w_up, ffn_conv_w, ffn_conv_b, w_down, g_post_ffn):
    b, s, _ = x.shape
    h = rms_norm(x, g_pre_mix)
    proj = h @ w_in.astype(x.dtype)
    qa, ka, va, za, aa, ba, qb, kb, vb = jnp.split(proj, _split_points(IN_SPLITS), axis=-1)

    qkv = jax.nn.silu(causal_depthwise_conv(jnp.concatenate([qa, ka, va], axis=-1), gdn_conv_w))
    qa, ka, va = jnp.split(qkv, _split_points((GDN_HEADS * GDN_DK, GDN_HEADS * GDN_DK, GDN_HEADS * GDN_DV)), axis=-1)
    qa = l2_normalize(qa.reshape(b, s, GDN_HEADS, GDN_DK))
    ka = l2_normalize(ka.reshape(b, s, GDN_HEADS, GDN_DK))
    va = va.reshape(b, s, GDN_HEADS, GDN_DV).astype(jnp.float32)
    beta = jax.nn.sigmoid(ba.astype(jnp.float32))
    g = -jnp.exp(gdn_A_log.astype(jnp.float32)) * jax.nn.softplus(aa.astype(jnp.float32) + gdn_dt_bias.astype(jnp.float32))
    o_a = gated_delta_rule(qa, ka, va, g, beta)
    o_a = rms_norm(o_a, gdn_norm_w) * jax.nn.silu(za.reshape(b, s, GDN_HEADS, GDN_DV).astype(jnp.float32))
    o_a = o_a.reshape(b, s, MIX_A).astype(x.dtype)

    pos = jnp.arange(s, dtype=jnp.float32)
    inv_freq = ROPE_THETA ** (-jnp.arange(0, ROT_DIM, 2, dtype=jnp.float32) / ROT_DIM)
    ang = pos[:, None] * inv_freq[None, :]
    cos, sin = jnp.cos(ang), jnp.sin(ang)
    qb = partial_rope(qb.reshape(b, s, SWA_HEADS, SWA_HEAD_DIM), cos, sin)
    kb = partial_rope(kb.reshape(b, s, SWA_KV_HEADS, SWA_HEAD_DIM), cos, sin)
    vb = vb.reshape(b, s, SWA_KV_HEADS, SWA_HEAD_DIM)
    o_b = sliding_window_sink_attention(qb, kb, vb, attn_sinks).astype(x.dtype)

    mix = jnp.concatenate([o_a, o_b], axis=-1) @ w_out.astype(x.dtype)
    x = x + rms_norm(mix, g_post_mix)

    h = rms_norm(x, g_pre_ffn)
    u = causal_depthwise_conv(h @ w_up.astype(x.dtype), ffn_conv_w) + ffn_conv_b.astype(x.dtype)
    gate, val = jnp.split(u, 2, axis=-1)
    y = (jax.nn.gelu(gate, approximate=True) * val) @ w_down.astype(x.dtype)
    return x + rms_norm(y, g_post_ffn)

def setup_inputs(seed: int = 0) -> dict:
    key = jax.random.key(seed)
    ks = jax.random.split(key, 17)
    L = DEPTH

    def nrm(k, shape, scale):
        return jax.random.normal(k, shape, jnp.float32) * scale

    def gain(k, dim):
        return 1.0 + 0.05 * jax.random.normal(k, (L, dim), jnp.float32)

    dt = jnp.exp(jax.random.uniform(ks[5], (L, GDN_HEADS), jnp.float32) * (math.log(0.1) - math.log(0.001)) + math.log(0.001))
    return {
        "x": nrm(ks[0], (BATCH, SEQ, D_MODEL), 1.0),
        "g_pre_mix": gain(ks[1], D_MODEL),
        "w_in": nrm(ks[2], (L, D_MODEL, IN_WIDTH), D_MODEL ** -0.5),
        "gdn_conv_w": nrm(ks[3], (L, GDN_CONV, GDN_CONV_CH), GDN_CONV ** -0.5),
        "gdn_A_log": jnp.log(jax.random.uniform(ks[4], (L, GDN_HEADS), jnp.float32, 1.0, 16.0)),
        "gdn_dt_bias": dt + jnp.log(-jnp.expm1(-dt)),
        "gdn_norm_w": gain(ks[6], GDN_DV),
        "attn_sinks": nrm(ks[7], (L, SWA_HEADS), 0.5),
        "w_out": nrm(ks[8], (L, MIX_WIDTH, D_MODEL), MIX_WIDTH ** -0.5),
        "g_post_mix": gain(ks[9], D_MODEL),
        "g_pre_ffn": gain(ks[10], D_MODEL),
        "w_up": nrm(ks[11], (L, D_MODEL, 2 * D_FF), D_MODEL ** -0.5),
        "ffn_conv_w": nrm(ks[12], (L, FFN_CONV, 2 * D_FF), FFN_CONV ** -0.5),
        "ffn_conv_b": nrm(ks[13], (L, 2 * D_FF), 0.01),
        "w_down": nrm(ks[14], (L, D_FF, D_MODEL), D_FF ** -0.5),
        "g_post_ffn": gain(ks[15], D_MODEL),
    }

def reference(x, g_pre_mix, w_in, gdn_conv_w, gdn_A_log, gdn_dt_bias, gdn_norm_w, attn_sinks,
              w_out, g_post_mix, g_pre_ffn, w_up, ffn_conv_w, ffn_conv_b, w_down, g_post_ffn):
    for layer in range(DEPTH):
        x = hybrid_layer(x, g_pre_mix[layer], w_in[layer], gdn_conv_w[layer], gdn_A_log[layer],
                         gdn_dt_bias[layer], gdn_norm_w[layer], attn_sinks[layer], w_out[layer],
                         g_post_mix[layer], g_pre_ffn[layer], w_up[layer], ffn_conv_w[layer],
                         ffn_conv_b[layer], w_down[layer], g_post_ffn[layer])
    return x


_drawn_inputs = setup_inputs


def setup_inputs(seed=0):
    import zlib

    import numpy as np

    out = dict(_drawn_inputs(seed))
    spreads = {}
    factors = {'attn_sinks': 64.0, 'ffn_conv_b': 6.911}
    for name, (base, spread) in spreads.items():
        noise = np.random.default_rng([zlib.crc32(name.encode()), seed]).standard_normal(out[name].shape)
        drawn = base * np.exp(spread * noise) if base else spread * noise
        out[name] = __import__('jax').numpy.asarray(drawn.astype(out[name].dtype))
    for name, factor in factors.items():
        out[name] = (out[name] * factor).astype(out[name].dtype)
    return out
```

```python
from contextlib import ExitStack

import numpy as np

import concourse.bass as bass
from concourse import mybir

P = 128
F32 = mybir.dt.float32
F32R = mybir.dt.float32r
BF16 = mybir.dt.bfloat16
ALU = mybir.AluOpType
ACT = mybir.ActivationFunctionType
AX_X = mybir.AxisListType.X

EPS = 1e-6
D = 1024
S = 1024
T = S // P
KD = D // P
HALF = 512
GH, DK = 4, 128
QH, KVH, HD = 8, 2, 64
GROUP = QH // KVH
CHUNK = 64
ROT = HD // 4
ROPE_THETA = 500000.0
GTAPS, FTAPS = 4, 3
DFF = 2816
A_CH = 3 * GH * DK
A_TILES = A_CH // P
Z0, AB0, Q0 = 0, GH * DK, GH * DK + 2 * GH
K0 = Q0 + QH * HD
V0 = K0 + KVH * HD
ROW = V0 + KVH * HD
IN_W = A_CH + ROW
GROUPS = [(0, HALF), (HALF, HALF), (2 * HALF, ROW - 2 * HALF)]
NEG = -1e30

T_ID, T_TRI, T_STRICT = 0, P, 2 * P
LEVELS = [1, 2, 4, 8, 16, 32, 64]
T_LEVEL = 3 * P
T_LEVEL0T = T_LEVEL + len(LEVELS) * P
T_CUR, T_PREV = T_LEVEL0T + P, T_LEVEL0T + 2 * P
T_ONES = T_LEVEL0T + 3 * P
T_ROPE = T_ONES + P
T_W = T_ROPE + T * 2 * (ROT // 2)


def tables():
    i, j = np.arange(P)[:, None], np.arange(P)[None, :]
    t = np.zeros((P, T_W), np.float32)
    t[:, T_ID:T_ID + P] = i == j
    t[:, T_TRI:T_TRI + P] = i <= j
    t[:, T_STRICT:T_STRICT + P] = j < i
    for n, s in enumerate(LEVELS):
        m = (i // (2 * s) == j // (2 * s)) & ((i // s) % 2 == 1) & ((j // s) % 2 == 0)
        t[:, T_LEVEL + n * P:T_LEVEL + (n + 1) * P] = -1.0 * m
        if n == 0:
            t[:, T_LEVEL0T:T_LEVEL0T + P] = -1.0 * m.T
    t[:, T_CUR:T_CUR + P] = np.where(j // CHUNK <= i // CHUNK, 0.0, NEG)
    t[:, T_PREV:T_PREV + P] = np.where((i // CHUNK == 0) & (j // CHUNK == 1), 0.0, NEG)
    t[:, T_ONES:T_ONES + P] = 1.0
    pos = np.arange(S, dtype=np.float32)
    inv = (np.float32(ROPE_THETA) ** (-np.arange(0, ROT, 2, dtype=np.float32) / np.float32(ROT))).astype(np.float32)
    ang = (pos[:, None] * inv[None, :]).astype(np.float32).reshape(T, P, ROT // 2)
    r = t[:, T_ROPE:].reshape(P, T, 2, ROT // 2)
    r[:, :, 0] = np.cos(ang).transpose(1, 0, 2)
    r[:, :, 1] = np.sin(ang).transpose(1, 0, 2)
    return t


def project_block(nc, io):
    with ExitStack() as ctx:
        sb = lambda name, shape, dt=F32: ctx.enter_context(nc.sbuf_tensor(name, shape, dt))
        sem = lambda name: ctx.enter_context(nc.semaphore(name))

        h_hi = sb("h_hi", [P, KD, S], F32R)
        h_lo = sb("h_lo", [P, KD, S], F32R)
        wbuf = sb("wbuf", [P, 2 * KD * ROW], F32R)
        raw = sb("raw", [P, 2, KD * GROUPS[2][1]])
        tile_hi = sb("tile_hi", [P, 2, KD, P], F32R)
        tile_lo = sb("tile_lo", [P, 2, KD, P], F32R)
        xin = sb("xin", [P, 2, D])
        h = sb("h", [P, D])
        junk = sb("junk", [P, D], BF16)
        row = sb("row", [P, ROW])
        gain = sb("gain", [P, D])
        ident = sb("ident", [P, P])
        rope = sb("rope", [P, T, 2, ROT // 2])
        rot = sb("rot", [P, 4, QH + KVH, ROT // 2])
        stat = sb("stat", [P, 2, 4])
        power = sb("power", [P, 1])
        convrows = sb("convrows", [GTAPS * A_TILES, P])
        taps = sb("taps", [P, GTAPS * A_TILES])
        conv = xin

        ps_t = ctx.enter_context(nc.psum_tensor("ps_t", [P, 2, HALF], F32))
        ps_g = ctx.enter_context(nc.psum_tensor("ps_g", [P, 6, HALF], F32))

        s_x = [sem("s_x0"), sem("s_x1")]
        s_const, s_gain, s_rope, s_conv_rows = sem("s_const"), sem("s_gain"), sem("s_rope"), sem("s_conv_rows")
        s_raw = [sem("s_raw0"), sem("s_raw1")]
        s_whi, s_wlo = sem("s_whi"), sem("s_wlo")
        s_power = sem("s_power")
        s_taps_ps, s_taps = sem("s_taps_ps"), sem("s_taps")
        s_sq, s_ms, s_rstd = sem("s_sq"), sem("s_ms"), sem("s_rstd")
        s_h, s_tr = sem("s_h"), sem("s_tr")
        s_hi, s_lo, s_big = sem("s_hi"), sem("s_lo"), sem("s_big")
        s_mm = sem("s_mm")
        s_z, s_mid, s_last = sem("s_z"), sem("s_mid"), sem("s_last")
        s_rot4, s_rot, s_row_out = sem("s_rot4"), sem("s_rot"), sem("s_row_out")
        s_pair, s_first, s_tap, s_conv = sem("s_pair"), sem("s_first"), sem("s_tap"), sem("s_conv")
        s_silu = sem("s_silu")
        s_qkv_out = [sem("s_qkv_out0"), sem("s_qkv_out1")]

        w_in = io["w_in"].rearrange("o (k p) n -> p (o k) n", p=P)
        rows_flat = io["rows"].rearrange("t p n -> (t p n)")
        x_tiles = io["x"].rearrange("o (t p) d -> (o t) p d", p=P)

        chunks = [(0, 0, 4), (0, 4, 4), (1, 0, 4), (1, 4, 4), (2, 0, 8)]
        ready = [2, 4, 5]
        base = [0, 2 * KD * HALF, 4 * KD * HALF]

        def group_w(g, part):
            n = GROUPS[g][1]
            a = base[g] + part * KD * n
            return wbuf[:, a:a + KD * n].rearrange("p (k n) -> p k n", k=KD)

        def raw_chunk(c):
            g, _, nk = chunks[c]
            n = GROUPS[g][1]
            return raw[:, c % 2, 0:nk * n].rearrange("p (k n) -> p k n", k=nk)

        def slab_w(slot, part):
            a = slot * 4 * P * KD + part * 2 * P * KD
            return wbuf[:, a:a + 2 * P * KD].rearrange("p (k n) -> p k n", k=KD)

        NCH = len(chunks)
        SLABS = A_TILES // 2

        def raw_slab(slot):
            return raw[:, slot, 0:2 * P * KD].rearrange("p (k n) -> p k n", k=KD)

        def raw_count(n):
            return 16 * (n // 2 + 1)

        block = ctx.enter_context(nc.Block("project"))

        def tiles(eng, step, first=True):
            if first:
                step(0, 0, 0)
            with eng.Fori(0, T // 2 - 1) as i:
                step(i * 2 + 1, 1, i)
                step(i * 2 + 2, 0, i)
            step(T - 1, 1, T // 2 - 1)

        def slabs(eng, step):
            with eng.Fori(0, SLABS // 2 - 1) as i:
                step(i * 2, 0, i, False)
                step(i * 2 + 1, 1, i, False)
            step(SLABS - 2, 0, SLABS // 2 - 1, False)
            step(SLABS - 1, 1, SLABS // 2 - 1, True)

        @block.sync
        def _(sp):
            for q in s_qkv_out:
                sp.sem_inc(q, 16)
            sp.dma_start(xin[:, 0], x_tiles[0]).then_inc(s_x[0], 16)
            sp.dma_start(gain[:], io["g_pre_mix"][0:1, :].broadcast_to([P, D])).then_inc(s_gain, 16)
            sp.dma_start(ident[:], io["tables"][:, T_ID:T_ID + P]).then_inc(s_const, 16)

            def load_chunk(c):
                g, k0, nk = chunks[c]
                c0, n = GROUPS[g]
                if c >= 2:
                    sp.wait_ge(s_whi, c - 1)
                    sp.wait_ge(s_wlo, c - 1)
                sp.dma_start(raw_chunk(c), w_in[:, k0:k0 + nk, A_CH + c0:A_CH + c0 + n]).then_inc(s_raw[c % 2], 16)

            load_chunk(0)
            load_chunk(1)
            sp.dma_start(xin[:, 1], x_tiles[1]).then_inc(s_x[1], 16)
            sp.dma_start(rope[:].rearrange("p t c r -> p (t c r)"), io["tables"][:, T_ROPE:T_W]).then_inc(s_rope, 16)
            for c in range(2, NCH):
                load_chunk(c)

            def reg(v):
                return v if isinstance(v, int) else sp.snap(v)

            def load_slab(s, slot):
                before, src = reg(s + NCH - 1), w_in[:, :, bass.ds(reg(s * (2 * P)), 2 * P)]
                sp.wait_ge(s_whi, before)
                sp.wait_ge(s_wlo, before)
                sp.dma_start(raw_slab(slot), src).then_inc(s_raw[slot], 16)

            load_slab(0, NCH % 2)

            def tile(t, par, i):
                this, after = reg(t), reg(t + 1)
                row_at = reg((t - 1) * (P * ROW))
                sp.wait_ge(s_h, this)
                sp.dma_start(xin[:, 1 - par], x_tiles[bass.ds(after, 1)].rearrange("o p d -> (o p) d")).then_inc(
                    s_x[1 - par], 16)
                store(row_at, after, this)

            def store(row_at, moved, rotated):
                sp.wait_ge(s_z, moved)
                sp.wait_ge(s_rot, rotated)
                dst = rows_flat[bass.ds(row_at, P * ROW)].rearrange("(p n) -> p n", n=ROW)
                sp.dma_start(dst, row[:]).then_inc(s_row_out, 16)

            with sp.Fori(0, T // 2 - 1) as i:
                tile(i * 2 + 1, 1, i)
                tile(i * 2 + 2, 0, i)
            sp.dma_start(convrows[:], io["gdn_conv_w"].rearrange("o k (c p) -> (o k c) p", p=P)).then_inc(s_conv_rows, 16)
            for t in range(T - 2, T):
                store(t * P * ROW, t + 2, t + 1)
            load_slab(1, (NCH + 1) % 2)

            def slab(s, par, i, last):
                if not isinstance(s, int):
                    load_slab(s + 2, (NCH + par) % 2)
                for c in range(2):
                    tile_c, done = reg(s * 2 + c), reg(s * 2 + c + 1)
                    sp.wait_ge(s_silu, done)
                    dst = io["qkv"][:, :, bass.ds(tile_c, 1), :].rearrange("t p o s -> p (t o) s")
                    sp.dma_start(dst, conv[:, c].rearrange("p (t s) -> p t s", t=T)).then_inc(s_qkv_out[c], 16)

            slabs(sp, slab)
            sp.wait_ge(s_row_out, 16 * T)
            for q in s_qkv_out:
                sp.wait_ge(q, 16 * (A_TILES // 2 + 1))

        @block.gpsimd
        def _(pool):
            pool.memset(power[:], -0.5).then_inc(s_power, 1)
            pool.wait_ge(s_power, 1)

            def rstd(t, par):
                pool.wait_ge(s_ms, t + 1)
                pool.tensor_tensor(stat[:, par, 2:3], stat[:, par, 1:2], power[:], ALU.pow).then_inc(s_rstd, 1)

            def tile(t, par, i):
                if not (isinstance(t, int) and t == T - 1):
                    rstd(t + 1, 1 - par)
                pool.wait_ge(s_hi, 2 * (t + 1))
                pool.wait_ge(s_lo, 2 * (t + 1))
                pool.tensor_copy(h_hi[:, :, bass.ds(t * P, P)], tile_hi[:, par].bitcast(F32)).then_inc(s_big, 1)
                pool.tensor_copy(h_lo[:, :, bass.ds(t * P, P)], tile_lo[:, par].bitcast(F32)).then_inc(s_big, 1)

            rstd(0, 0)
            tiles(pool, tile)

        @block.scalar
        def _(act):
            def front(t, par, load):
                act.wait_ge(s_x[par], 16 * load)
                act.activation(junk[:], xin[:, par], ACT.Square, accum_out=stat[:, par, 0:1]).then_inc(s_sq, 1)
                if not (isinstance(t, int) and t < 2):
                    act.wait_ge(s_mm, 3 * (t - 1))
                    act.wait_ge(s_big, 2 * (t - 1))
                for b in range(2):
                    act.wait_ge(s_tr, 2 * t + b + 1)
                    act.copy(tile_hi[:, par, 4 * b:4 * b + 4], ps_t[:, b].rearrange("p (k s) -> p k s", k=4)).then_inc(s_hi, 1)

            def tile(t, par, i):
                if not (isinstance(t, int) and t == T - 1):
                    front(t + 1, 1 - par, i + 1 if isinstance(t, int) else i + 2)
                act.wait_ge(s_mm, 3 * t + 1)
                act.wait_ge(s_row_out, 16 * t)
                act.activation(row[:, 0:HALF], ps_g[:, 3 * par], ACT.Silu).then_inc(s_z, 1)
                act.wait_ge(s_mm, 3 * t + 3)
                act.copy(row[:, 2 * HALF:ROW], ps_g[:, 3 * par + 2, 0:GROUPS[2][1]]).then_inc(s_last, 1)

            front(0, 0, 1)
            for c in range(NCH):
                g, k0, nk = chunks[c]
                act.wait_ge(s_raw[c % 2], raw_count(c))
                act.copy(group_w(g, 0)[:, k0:k0 + nk], raw_chunk(c)).then_inc(s_whi, 1)
            tiles(act, tile)

            def split(s, par, loads):
                slot = (NCH + par) % 2
                act.wait_ge(s_raw[slot], 16 * loads)
                act.copy(slab_w(par, 0), raw_slab(slot)).then_inc(s_whi, 1)

            def slab(s, par, i, last):
                if not last:
                    act.wait_ge(s_pair, 2 * s + 2)
                    split(s + 1, 1 - par, i + 4)
                for c in range(2):
                    act.wait_ge(s_pair, 2 * s + c + 3)
                    act.wait_ge(s_qkv_out[c], 16 * s + 16)
                    act.activation(conv[:, c], ps_g[:, 2 * c:2 * c + 2].rearrange("p b n -> p (b n)"), ACT.Identity,
                                   scale=taps[:, bass.ds(2 * s + (c + (GTAPS - 1) * A_TILES), 1)]).then_inc(s_first, 1)
                for c in range(2):
                    act.wait_ge(s_conv, 2 * s + c + 3)
                    act.activation(conv[:, c], conv[:, c], ACT.Silu).then_inc(s_silu, 1)

            act.wait_ge(s_mm, 3 * T - 2)
            split(0, 0, 3)
            act.wait_ge(s_taps, 1)
            slabs(act, slab)

        @block.vector
        def _(dve):
            dve.sem_inc(s_conv, 2)
            for q in (s_z, s_mid, s_last):
                dve.sem_inc(q, 1)
            dve.wait_ge(s_gain, 16)

            def front(t, par):
                st = stat[:, par]
                dve.wait_ge(s_sq, t + 1)
                dve.tensor_scalar(st[:, 1:2], st[:, 0:1], 1.0 / D, EPS, ALU.mult, ALU.add).then_inc(s_ms, 1)
                dve.wait_ge(s_rstd, t + 1)
                if not (isinstance(t, int) and t == 0):
                    dve.wait_ge(s_tr, 2 * t)
                dve.scalar_tensor_tensor(h[:], xin[:, par], st[:, 2:3], gain[:], ALU.mult, ALU.mult).then_inc(s_h, 1)
                for b in range(2):
                    dve.wait_ge(s_hi, 2 * t + b + 1)
                    k = slice(4 * b, 4 * b + 4)
                    dve.tensor_tensor(tile_lo[:, par, k], ps_t[:, b].rearrange("p (k s) -> p k s", k=4),
                                      tile_hi[:, par, k].bitcast(F32), ALU.subtract).then_inc(s_lo, 1)

            heads = row[:, Q0:V0].rearrange("p (h d) -> p h d", d=HD)
            x1, x2 = heads[:, :, 0:ROT // 2], heads[:, :, ROT // 2:ROT]

            def tile(t, par, i):
                if not (isinstance(t, int) and t == T - 1):
                    front(t + 1, 1 - par)
                dve.wait_ge(s_mm, 3 * t + 2)
                dve.wait_ge(s_row_out, 16 * t)
                dve.tensor_copy(row[:, HALF:2 * HALF], ps_g[:, 3 * par + 1]).then_inc(s_mid, 1)
                dve.wait_ge(s_mid, t + 2)
                dve.wait_ge(s_last, t + 2)
                cos = rope[:, bass.ds(t, 1), 0, :].broadcast_to([P, QH + KVH, ROT // 2])
                sin = rope[:, bass.ds(t, 1), 1, :].broadcast_to([P, QH + KVH, ROT // 2])
                for n, (a, b) in enumerate([(x1, cos), (x2, sin), (x2, cos), (x1, sin)]):
                    dve.tensor_tensor(rot[:, n], a, b, ALU.mult).then_inc(s_rot4, 1)
                dve.wait_ge(s_rot4, 4 * (t + 1))
                dve.tensor_tensor(x1, rot[:, 0], rot[:, 1], ALU.subtract)
                dve.tensor_tensor(x2, rot[:, 2], rot[:, 3], ALU.add).then_inc(s_rot, 1)

            front(0, 0)
            for c in range(NCH):
                g, k0, nk = chunks[c]
                dve.wait_ge(s_whi, c + 1)
                dve.tensor_tensor(group_w(g, 1)[:, k0:k0 + nk], raw_chunk(c),
                                  group_w(g, 0)[:, k0:k0 + nk].bitcast(F32), ALU.subtract).then_inc(s_wlo, 1)
            dve.wait_ge(s_rope, 16)
            tiles(dve, tile)

            def split(s, par):
                dve.wait_ge(s_whi, s + NCH + 1)
                dve.tensor_tensor(slab_w(par, 1), raw_slab((NCH + par) % 2), slab_w(par, 0).bitcast(F32),
                                  ALU.subtract).then_inc(s_wlo, 1)

            def slab(s, par, i, last):
                if not last:
                    split(s + 1, 1 - par)
                for c in range(2):
                    src = ps_g[:, 2 * c:2 * c + 2].rearrange("p b n -> p (b n)")
                    dve.wait_ge(s_first, 2 * s + c + 1)
                    for k in range(1, GTAPS):
                        op = dve.scalar_tensor_tensor(
                            conv[:, c, k:S], src[:, 0:S - k], taps[:, bass.ds(2 * s + (c + (GTAPS - 1 - k) * A_TILES), 1)],
                            conv[:, c, k:S], ALU.mult, ALU.add)
                        if k < GTAPS - 1:
                            op.then_inc(s_tap, 1)
                            dve.wait_ge(s_tap, (2 * s + c) * (GTAPS - 2) + k)
                        else:
                            op.then_inc(s_conv, 1)

            dve.wait_ge(s_taps_ps, 1)
            dve.tensor_copy(taps[:], ps_g[:, 5, 0:GTAPS * A_TILES]).then_inc(s_taps, 1)
            split(0, 0)
            slabs(dve, slab)

        @block.tensor
        def _(pe):
            pe.sem_inc(s_pair, 2)
            pe.wait_ge(s_const, 16)

            def front(t, par):
                pe.wait_ge(s_h, t + 1)
                for b in range(2):
                    if not (isinstance(t, int) and t == 0):
                        pe.wait_ge(s_lo, 2 * t - 1 + b)
                    for k in range(4):
                        last = pe.transpose(ps_t[:, b, k * P:(k + 1) * P], h[:, (4 * b + k) * P:(4 * b + k + 1) * P], ident[:])
                    last.then_inc(s_tr, 1)

            def tile(t, par, i):
                pe.wait_ge(s_lo, 2 * (t + 1))
                for g, (c0, n) in enumerate(GROUPS):
                    pe.wait_ge(s_wlo, ready[g])
                    if not (isinstance(t, int) and t == 0):
                        pe.wait_ge((s_z, s_mid, s_last)[g], t)
                    bank = ps_g[:, 3 * par + g, 0:n]
                    for k in range(KD):
                        pe.matmul(bank, tile_hi[:, par, k], group_w(g, 0)[:, k], start=(k == 0), stop=False)
                        pe.matmul(bank, tile_hi[:, par, k], group_w(g, 1)[:, k], start=False, stop=False)
                        last = pe.matmul(bank, tile_lo[:, par, k], group_w(g, 0)[:, k], start=False, stop=(k == KD - 1))
                    last.then_inc(s_mm, 1)
                    if g == 0 and not (isinstance(t, int) and t == T - 1):
                        front(t + 1, 1 - par)

            front(0, 0)
            tiles(pe, tile)

            def slab(s, par, i, last):
                pe.wait_ge(s_wlo, s + NCH + 1)
                for c in range(2):
                    pe.wait_ge(s_conv, 2 * s + c + 1)
                    for half in range(2):
                        bank = ps_g[:, 2 * c + half]
                        cols = slice(half * HALF, (half + 1) * HALF)
                        for k in range(KD):
                            w_hi = slab_w(par, 0)[:, k, c * P:(c + 1) * P]
                            w_lo = slab_w(par, 1)[:, k, c * P:(c + 1) * P]
                            pe.matmul(bank, w_hi, h_hi[:, k, cols], start=(k == 0), stop=False)
                            pe.matmul(bank, w_hi, h_lo[:, k, cols], start=False, stop=False)
                            op = pe.matmul(bank, w_lo, h_hi[:, k, cols], start=False, stop=(k == KD - 1))
                    op.then_inc(s_pair, 1)

            pe.wait_ge(s_big, 2 * T)
            for q in (s_z, s_mid, s_last):
                pe.wait_ge(q, T + 1)
            pe.wait_ge(s_conv_rows, 16)
            n = GTAPS * A_TILES
            pe.transpose(ps_g[:, 5, 0:n], convrows[:], ident[0:n, 0:n]).then_inc(s_taps_ps, 1)
            slabs(pe, slab)


class Tally:

    def __init__(self, nc, ctx, name, per=1, credit=0):
        self.sem, self.per, self.credit = ctx.enter_context(nc.semaphore(name)), per, credit

    def at(self, t, k):
        return t * self.per + (k + self.credit)


def after(eng, tally, t, k=None):
    value = tally.at(t, tally.per if k is None else k)
    if not isinstance(value, int) or value > tally.credit:
        eng.wait_ge(tally.sem, value)


def mix_block(nc, io, h_t):
    with ExitStack() as ctx:
        sb = lambda name, shape, dt=F32: ctx.enter_context(nc.sbuf_tensor("m_" + name, shape, dt))
        sem = lambda name: ctx.enter_context(nc.semaphore("m_" + name))
        tally = lambda name, per=1, credit=0: Tally(nc, ctx, "m_" + name, per, credit)
        H = GH
        NG = 7
        I_G, I_CUM, I_BETA, I_NEG, I_OUT, I_IN, I_LAST = range(NG)

        w_hi = sb("w_hi", [P, KD, D], F32R)
        w_lo = sb("w_lo", [P, KD, D], F32R)
        qkv = sb("qkv", [P, A_TILES, P])
        row = sb("row", [P, ROW])
        gates = sb("gates", [P, T, NG, H])
        gs = sb("gs", [P, 2, NG, H])
        ab = sb("ab", [P, T, 2, H])
        g_tmp = sb("g_tmp", [P, 6, T, H])
        a_log = sb("a_log", [P, H])
        dt_bias = sb("dt_bias", [P, H])
        a_exp = sb("a_exp", [P, H])
        power = sb("power", [P, 2 * H])
        squares = sb("squares", [P, 2 * H, P])
        g_tri = sb("g_tri", [P, H, P])
        norm2 = sb("norm2", [P, 2, 2, 2 * H])
        k_tok = sb("k_tok", [P, H, P])
        k_t = sb("k_t", [P, H, P])
        q_t = sb("q_t", [P, H, P])
        k_out = sb("k_out", [P, H, P])
        b_v = sb("b_v", [P, H, P])
        dec_t = sb("dec_t", [P, H, P])
        dec = sb("dec", [P, H, P])
        low = sb("low", [P, H, P])
        low_t = sb("low_t", [P, H, P])
        qk_t = sb("qk_t", [P, H, P])
        inv = sb("inv", [P, H, P])
        inv_t = sb("inv_t", [P, H, P])
        off = sb("off", [P, H, P])
        state = sb("state", [P, H, P])
        resid = sb("resid", [P, H, P])
        v_new = sb("v_new", [P, H, P])
        o = sb("o", [P, H, P])
        zw = sb("zw", [P, H, P])
        o_stat = sb("o_stat", [P, 5, H])
        norm_w = sb("norm_w", [P, P])
        junk = sb("junk", [P, D], BF16)
        junk_o = sb("junk_o", [P, H, P], BF16)
        q_b = sb("q_b", [P, QH // 2, P])
        k_dup = sb("k_dup", [P, KVH, 2, HD])
        k_b = sb("k_b", [P, KVH, 2, P])
        v_b = sb("v_b", [P, 2, KVH * HD])
        scores = sb("scores", [P, 4, 2, P])
        p_t = sb("p_t", [P, 4, 2, P])
        masks = sb("masks", [P, 3, 2, P])
        sinks = sb("sinks", [P, QH])
        c_stat = sb("c_stat", [P, 7, QH])
        mix = sb("mix", [P, D])
        mix_hi = sb("mix_hi", [P, KD, P], F32R)
        mix_lo = sb("mix_lo", [P, KD, P], F32R)
        x = sb("x", [P, D])
        y = sb("y", [P, D])
        g_post = sb("g_post", [P, D])
        g_ffn = sb("g_ffn", [P, D])
        d_stat = sb("d_stat", [P, 6])
        table = sb("table", [P, T_ROPE])
        tab = lambda at: table[:, at:at + P]
        ident, tri, strict, ones = tab(T_ID), tab(T_TRI), tab(T_STRICT), tab(T_ONES)
        over_heads = lambda m: m.unsqueeze(1).broadcast_to([P, H, P])
        over_cols = lambda s: s.unsqueeze(2).broadcast_to([P, H, P])
        flat = lambda m: m.rearrange("p a b -> p (a b)")

        ps = {n: ctx.enter_context(nc.psum_tensor("m_ps_" + n, [P, HALF], F32)) for n in ("a0", "a1", "a2", "b0", "b1", "c0")}
        ps_d = ctx.enter_context(nc.psum_tensor("m_ps_d", [P, 2, HALF], F32))
        bank = lambda n: ps[n][:].rearrange("p (h c) -> p h c", c=P)

        fills = {"a0": 9, "a1": 3, "a2": 8, "b0": 3, "b1": 2, "c0": 12, "d0": 3, "d1": 3}
        frees = {"a0": 8, "a1": 3, "a2": 7, "b0": 2, "c0": 10, "d0": 3, "d1": 3}
        full = {n: tally(n + "_full", k, k if n[0] == "d" else 0) for n, k in fills.items()}
        free = {n: tally(n + "_free", k, k if n[0] == "d" else 0) for n, k in frees.items()}

        s_load, s_tab, s_ab, s_w = sem("load"), sem("tab"), sem("ab"), sem("w")
        s_whi, s_wlo, s_zero, s_gate = sem("whi"), sem("wlo"), sem("zero"), sem("gate")
        s_gv, s_ga, s_ps_g = sem("gate_vector"), sem("gate_scalar"), sem("gate_sums")
        s_order = sem("order")
        qkv_in, row_in = tally("qkv_in", 16), tally("row_in", 16)
        x_in, x_out = tally("x_in", 16, 16), tally("x_out", 16, 16)
        gs_set, tri_set, squared = tally("gs_set"), tally("tri_set"), tally("squared")
        n2, rn, khat, qt_set, kout_set = (tally(n) for n in ("n2", "rn", "khat", "qt_set", "kout_set"))
        clipped, dec_exp, dec_masked = tally("clipped", 2), tally("dec_exp", 2), tally("dec_masked", 3)
        init = tally("init", 4)
        st_set, o1_set, o_set = tally("st_set"), tally("o1_set"), tally("o_set")
        o_sq, o_n, o_ms, o_rstd, zw_set, mixa = tally("o_sq"), tally("o_n", 2), tally("o_ms"), tally("o_rstd", 2), tally("zw_set"), tally("mixa")
        kdup_set, vb_set = tally("kdup_set"), tally("vb_set")
        cmax, cneg, csub = tally("cmax", 2), tally("cneg", 2), tally("csub", 2)
        cexp, csink, cden, crec, mixb = tally("cexp", 2), tally("csink", 2), tally("cden", 2), tally("crec", 2), tally("mixb", 2)
        dhi, dsq, dms, drstd = (tally(n, 2, 2) for n in ("dhi", "dsq", "dms", "drstd"))
        dx, dh = (tally(n, 1, 1) for n in ("dx", "dh"))

        LV = len(LEVELS) - 1

        def halves(m, n, which):
            s = LEVELS[n]
            return m.rearrange("p h (g two s) -> p h g two s", two=2, s=s)[:, :, :, which]

        def half_cols(m, h, n, which):
            s = LEVELS[n]
            return m[:, h].rearrange("p (g two s) -> p g two s", two=2, s=s)[:, :, which]

        def ps_half(n, which):
            s = LEVELS[n]
            return ps["a2"][:, 256 * which:256 * which + 256].rearrange("p (h g s) -> p h g s", h=H, s=s)

        w_rows = io["w_out"].rearrange("o (k p) n -> p (o k) n", p=P)
        qkv_flat = io["qkv"].rearrange("t p c s -> (t p c s)")
        rows_flat = io["rows"].rearrange("t p n -> (t p n)")
        x_flat = io["x"].rearrange("o s d -> (o s d)")
        res_flat = io["res"].rearrange("t p d -> (t p d)")

        def carry(eng):
            eng.sem_inc(s_order, 1)

        block = ctx.enter_context(nc.Block("mix"))

        def steps(eng, step):
            step(0, 0, True, False)
            with eng.Fori(0, T // 2 - 1) as i:
                step(i * 2 + 1, 1, True, True)
                step(i * 2 + 2, 0, True, True)
            step(T - 1, 1, False, True)

        @block.sync
        def _(sp):
            def reg(v):
                return v if isinstance(v, int) else sp.snap(v)

            def ready(*needs):
                values = [(s, s.at(t, k)) for s, t, k in needs]
                for s, v in [(s, reg(v)) for s, v in values if not isinstance(v, int) or v > s.credit]:
                    sp.wait_ge(s.sem, v)
                    carry(sp)

            def load_qkv(u):
                at = reg(u * (P * A_TILES * P))
                ready((full["a1"], u - 1, 1), (qt_set, u - 1, 1), (squared, u - 1, 1))
                sp.dma_start(flat(qkv[:]), qkv_flat[bass.ds(at, P * A_TILES * P)].rearrange("(p n) -> p n", p=P)).then_inc(
                    qkv_in.sem, 16)

            def load_row(t):
                at = reg(t * (P * ROW))
                ready((full["c0"], t - 1, 1), (zw_set, t - 1, 1), (kdup_set, t - 1, 1), (vb_set, t - 1, 1))
                sp.dma_start(row[:], rows_flat[bass.ds(at, P * ROW)].rearrange("(p n) -> p n", p=P)).then_inc(row_in.sem, 16)

            def load_x(v):
                at = reg(v * (P * D))
                ready((x_out, v - 1, 16), (dh, v - 1, 1))
                sp.dma_start(x[:], x_flat[bass.ds(at, P * D)].rearrange("(p n) -> p n", p=P)).then_inc(x_in.sem, 16)

            def store_x(v):
                at = reg(v * (P * D))
                ready((dx, v, 1))
                sp.dma_start(res_flat[bass.ds(at, P * D)].rearrange("(p n) -> p n", p=P), x[:]).then_inc(x_out.sem, 16)

            sp.sem_inc(x_in.sem, 16)
            sp.sem_inc(x_out.sem, 16)
            sp.dma_start(ab[:].rearrange("p t c h -> p t (c h)"), io["rows"][:, :, AB0:Q0].rearrange("t p n -> p t n")).then_inc(s_ab, 16)
            sp.dma_start(a_log[:], io["gdn_A_log"][0:1, :].broadcast_to([P, H])).then_inc(s_ab, 16)
            sp.dma_start(dt_bias[:], io["gdn_dt_bias"][0:1, :].broadcast_to([P, H])).then_inc(s_ab, 16)
            load_qkv(0)
            sp.dma_start(table[:], io["tables"][:, 0:T_ROPE]).then_inc(s_tab, 16)
            for m, (a, b) in enumerate([(T_CUR, T_PREV), (T_PREV, T_CUR)]):
                sp.dma_start(masks[:, m, 0], io["tables"][:, a:a + P]).then_inc(s_load, 16)
                sp.dma_start(masks[:, m, 1], io["tables"][:, b:b + P]).then_inc(s_load, 16)
            sp.dma_start(masks[:, 2, 0], io["tables"][:, T_CUR:T_CUR + P]).then_inc(s_load, 16)
            sp.dma_start(norm_w[:], io["gdn_norm_w"][0:1, :].broadcast_to([P, P])).then_inc(s_load, 16)
            sp.dma_start(sinks[:], io["attn_sinks"][0:1, :].broadcast_to([P, QH])).then_inc(s_load, 16)
            load_row(0)
            sp.dma_start(h_t[:], w_rows).then_inc(s_w, 16)
            sp.dma_start(g_post[:], io["g_post_mix"][0:1, :].broadcast_to([P, D])).then_inc(s_load, 16)
            sp.dma_start(g_ffn[:], io["g_pre_ffn"][0:1, :].broadcast_to([P, D])).then_inc(s_load, 16)

            def step(t, par, a, d):
                if a:
                    load_qkv(t + 1)
                if d:
                    load_row(t)
                    load_x(t - 1)
                    store_x(t - 1)

            steps(sp, step)
            load_x(T - 1)
            store_x(T - 1)
            sp.wait_ge(x_out.sem, 16 * (T + 1))

        LOADS = 16 * 9

        @block.gpsimd
        def _(pool):
            pool.memset(power[:], -0.5).then_inc(s_zero, 1)
            pool.memset(state[:], 0.0).then_inc(s_zero, 1)
            pool.memset(k_b[:], 0.0).then_inc(s_zero, 1)
            pool.memset(v_b[:], 0.0).then_inc(s_zero, 1)
            pool.memset(masks[:, 2, 1], NEG).then_inc(s_zero, 1)
            pool.wait_ge(s_zero, 5)
            pool.wait_ge(s_tab, 16)
            pool.wait_ge(s_gate, 1)

            def a_gates(u, par):
                after(pool, st_set, u - 2)
                after(pool, o1_set, u - 2)
                carry(pool)
                pool.tensor_copy(gs[:, par].rearrange("p n h -> p (n h)"),
                                 gates[:, bass.ds(u, 1)].rearrange("p t n h -> p (t n h)")).then_inc(gs_set.sem, 1)
                after(pool, gs_set, u)
                after(pool, full["a1"], u - 1, 2)
                pool.tensor_tensor(g_tri[:], over_heads(tri), over_cols(gs[:, par, I_G]), ALU.mult).then_inc(tri_set.sem, 1)

            def a_rnorm(u, par):
                after(pool, n2, u)
                pool.tensor_tensor(norm2[:, par, 1], norm2[:, par, 0], power[:], ALU.pow).then_inc(rn.sem, 1)

            def a_kout(u, par):
                after(pool, khat, u)
                after(pool, full["b0"], u - 1, 3)
                pool.tensor_tensor(k_out[:], k_tok[:], over_cols(gs[:, par, I_OUT]), ALU.mult).then_inc(kout_set.sem, 1)

            def a_masks(u, par):
                after(pool, dec_exp, u, 1)
                pool.tensor_tensor(dec_t[:], dec_t[:], over_heads(tri), ALU.mult).then_inc(dec_masked.sem, 1)
                after(pool, dec_exp, u, 2)
                pool.tensor_tensor(dec[:], dec[:], over_heads(strict), ALU.mult).then_inc(dec_masked.sem, 1)
                after(pool, dec_masked, u, 2)
                pool.tensor_tensor(dec[:], dec[:], over_cols(gs[:, par, I_BETA]), ALU.mult).then_inc(dec_masked.sem, 1)

            def c_row(t, par):
                after(pool, row_in, t)
                after(pool, full["c0"], t - 1, 2)
                carry(pool)
                pool.tensor_copy(k_dup[:], row[:, K0:V0].rearrange("p (k d) -> p k d", d=HD).unsqueeze(2).broadcast_to(
                    [P, KVH, 2, HD])).then_inc(kdup_set.sem, 1)
                after(pool, full["c0"], t - 1, 12)
                carry(pool)
                pool.tensor_copy(v_b[:, par], row[:, V0:ROW]).then_inc(vb_set.sem, 1)
                after(pool, mixa, t - 1)
                pool.tensor_tensor(zw[:], row[:, 0:H * P].rearrange("p (h c) -> p h c", c=P), over_heads(norm_w[:]),
                                   ALU.mult).then_inc(zw_set.sem, 1)

            def b_scale(t, par):
                rq = norm2[:, par, 1, 0:H]
                after(pool, rn, t)
                pool.tensor_tensor(o_stat[:, 1], rq, rq, ALU.mult).then_inc(o_n.sem, 1)
                after(pool, o_sq, t)
                after(pool, o_n, t, 1)
                pool.tensor_tensor(o_stat[:, 2], o_stat[:, 1], o_stat[:, 0], ALU.mult).then_inc(o_n.sem, 1)

            def b_rstd(t, par):
                after(pool, o_ms, t)
                pool.tensor_tensor(o_stat[:, 4], o_stat[:, 3], power[:, 0:H], ALU.pow).then_inc(o_rstd.sem, 1)
                after(pool, o_rstd, t, 1)
                after(pool, mixa, t - 1)
                pool.tensor_tensor(o_stat[:, 4], o_stat[:, 4], norm2[:, par, 1, 0:H], ALU.mult).then_inc(o_rstd.sem, 1)

            def d_rstd(v, n):
                after(pool, dms, v, n)
                pool.tensor_tensor(d_stat[:, 3 * n - 1:3 * n], d_stat[:, 3 * n - 2:3 * n - 1], power[:, 0:1], ALU.pow).then_inc(drstd.sem, 1)

            a_gates(0, 0)
            a_rnorm(0, 0)
            a_kout(0, 0)
            a_masks(0, 0)
            pool.wait_ge(s_load, LOADS)

            def step(t, par, a, d):
                if a:
                    a_gates(t + 1, 1 - par)
                c_row(t, par)
                if a:
                    a_rnorm(t + 1, 1 - par)
                    a_kout(t + 1, 1 - par)
                b_scale(t, par)
                if a:
                    a_masks(t + 1, 1 - par)
                b_rstd(t, par)
                if d:
                    d_rstd(t - 1, 1)
                    d_rstd(t - 1, 2)

            steps(pool, step)
            d_rstd(T - 1, 1)
            d_rstd(T - 1, 2)

        @block.scalar
        def _(act):
            act.wait_ge(s_ab, 48)
            act.activation(a_exp[:], a_log[:], ACT.Exp).then_inc(s_ga, 1)
            act.activation(g_tmp[:, 3], ab[:, :, 1], ACT.Exp, scale=-1.0).then_inc(s_ga, 1)
            act.wait_ge(s_gv, 2)
            act.activation(g_tmp[:, 2], g_tmp[:, 1], ACT.Exp, scale=-1.0).then_inc(s_ga, 1)
            act.wait_ge(s_gv, 3)
            act.activation(g_tmp[:, 2], g_tmp[:, 2], ACT.Ln).then_inc(s_ga, 1)
            act.wait_ge(s_ps_g, 1)
            sums = ps["a0"][:, 0:2 * T * H].rearrange("p (c t h) -> p c t h", c=2, h=H)
            act.activation(gates[:, :, I_IN], sums[:, 0], ACT.Exp).then_inc(s_ga, 1)
            act.activation(gates[:, :, I_LAST], sums[:, 1], ACT.Exp).then_inc(s_ga, 1)
            act.wait_ge(s_gv, 9)
            act.activation(gates[:, :, I_OUT], g_tmp[:, 4], ACT.Exp).then_inc(s_ga, 1)

            def a_square(u):
                after(act, qkv_in, u)
                after(act, full["a2"], u - 1, 1)
                act.activation(squares[:], qkv[:, 0:2 * H], ACT.Square).then_inc(squared.sem, 1)

            def a_q(u):
                after(act, full["b1"], u - 1, 1)
                act.copy(q_t[:], qkv[:, 0:H]).then_inc(qt_set.sem, 1)

            def a_kt(u):
                after(act, full["a0"], u, 2)
                after(act, full["b0"], u - 1, 1)
                act.copy(k_t[:], bank("a0")).then_inc(free["a0"].sem, 1)

            def a_exp_(u):
                after(act, clipped, u, 1)
                act.activation(dec_t[:], dec_t[:], ACT.Exp).then_inc(dec_exp.sem, 1)
                after(act, clipped, u, 2)
                act.activation(dec[:], dec[:], ACT.Exp, scale=-1.0).then_inc(dec_exp.sem, 1)

            def a_lowt(u):
                after(act, full["a1"], u, 3)
                act.copy(low_t[:], bank("a1")).then_inc(free["a1"].sem, 1)

            def b_v_new(t):
                after(act, full["b0"], t, 2)
                after(act, full["b1"], t - 1, 2)
                act.copy(v_new[:], bank("b0")).then_inc(free["b0"].sem, 1)

            def b_square(t):
                after(act, o_set, t)
                after(act, o_ms, t - 1)
                for h in range(H):
                    op = act.activation(junk_o[:, h], o[:, h], ACT.Square, accum_out=o_stat[:, 0, h:h + 1])
                op.then_inc(o_sq.sem, 1)

            def c_qb(t):
                after(act, full["c0"], t, 1)
                act.copy(q_b[:], bank("c0")).then_inc(free["c0"].sem, 1)

            def c_kb(t, par):
                after(act, full["c0"], t, 2)
                act.copy(k_b[:, :, par], bank("c0")[:, 0:KVH]).then_inc(free["c0"].sem, 1)

            def c_exp(t, r):
                after(act, cneg, t, r + 1)
                after(act, mixb, t - 1, r + 1)
                for h in range(4):
                    op = act.activation(scores[:, h].rearrange("p a b -> p (a b)"), scores[:, h].rearrange("p a b -> p (a b)"), ACT.Exp,
                                        bias=c_stat[:, 2, 4 * r + h:4 * r + h + 1], accum_out=c_stat[:, 3, 4 * r + h:4 * r + h + 1])
                op.then_inc(cexp.sem, 1)
                after(act, csub, t, r + 1)
                act.activation(c_stat[:, 4, 4 * r:4 * r + 4], c_stat[:, 4, 4 * r:4 * r + 4], ACT.Exp).then_inc(csink.sem, 1)

            def c_pt(t, n):
                use = (5, 6, 10, 11)[n]
                after(act, full["c0"], t, use)
                act.copy(p_t[:, 2 * (n % 2):2 * (n % 2) + 2].rearrange("p h k c -> p (h k) c"), bank("c0")).then_inc(free["c0"].sem, 1)

            def d_hi(v):
                for b in range(2):
                    after(act, full[f"d{b}"], v, 1)
                    after(act, full["d1"], v - 1, 2)
                    act.copy(mix_hi[:, 4 * b:4 * b + 4], ps_d[:, b].rearrange("p (k c) -> p k c", c=P)).then_inc(dhi.sem, 1)

            def d_square(v, n):
                if n == 1:
                    after(act, full["d0"], v, 2)
                    after(act, full["d1"], v, 2)
                    src = flat(ps_d[:])
                else:
                    after(act, dx, v)
                    src = x[:]
                act.activation(junk[:], src, ACT.Square, accum_out=d_stat[:, 3 * n - 3:3 * n - 2]).then_inc(dsq.sem, 1)

            def d_out(v):
                act.wait_ge(s_wlo, 1)
                for b in range(2):
                    after(act, full[f"d{b}"], v, 3)
                    act.copy(h_t[:, 4 * b:4 * b + 4, bass.ds(v * P, P)],
                             ps_d[:, b].rearrange("p (k c) -> p k c", c=P)).then_inc(free[f"d{b}"].sem, 1)

            a_square(0)
            a_q(0)
            a_kt(0)
            a_exp_(0)
            a_lowt(0)
            act.wait_ge(s_w, 16)
            act.copy(w_hi[:], h_t[:]).then_inc(s_whi, 1)

            def step(t, par, a, d):
                if a:
                    a_square(t + 1)
                b_v_new(t)
                if d:
                    d_hi(t - 1)
                c_qb(t)
                c_kb(t, par)
                if a:
                    a_q(t + 1)
                    a_kt(t + 1)
                b_square(t)
                if a:
                    a_exp_(t + 1)
                c_exp(t, 0)
                if a:
                    a_lowt(t + 1)
                c_pt(t, 0)
                c_pt(t, 1)
                if d:
                    d_square(t - 1, 1)
                    d_square(t - 1, 2)
                c_exp(t, 1)
                c_pt(t, 2)
                c_pt(t, 3)
                if d:
                    d_out(t - 1)

            steps(act, step)
            d_hi(T - 1)
            d_square(T - 1, 1)
            d_square(T - 1, 2)
            d_out(T - 1)

        @block.vector
        def _(dve):
            n_gv = [0]

            def gv(op):
                op.then_inc(s_gv, 1)
                n_gv[0] += 1
                dve.wait_ge(s_gv, n_gv[0])

            by_tile = lambda m: m.unsqueeze(1).broadcast_to([P, T, H])
            dve.wait_ge(s_ab, 48)
            gv(dve.tensor_tensor(g_tmp[:, 0], ab[:, :, 0], by_tile(dt_bias[:]), ALU.add))
            gv(dve.scalar_tensor_tensor(g_tmp[:, 1], g_tmp[:, 0], -1.0, g_tmp[:, 0], ALU.mult, ALU.max))
            dve.wait_ge(s_ga, 3)
            gv(dve.tensor_scalar(g_tmp[:, 2], g_tmp[:, 2], 1.0, None, ALU.add))
            gv(dve.tensor_scalar(g_tmp[:, 3], g_tmp[:, 3], 1.0, None, ALU.add))
            gv(dve.reciprocal(gates[:, :, I_BETA], g_tmp[:, 3]))
            dve.wait_ge(s_ga, 4)
            gv(dve.scalar_tensor_tensor(g_tmp[:, 5], g_tmp[:, 0], 0.0, g_tmp[:, 2], ALU.max, ALU.add))
            gv(dve.scalar_tensor_tensor(gates[:, :, I_G], g_tmp[:, 5], -1.0, by_tile(a_exp[:]), ALU.mult, ALU.mult))
            dve.wait_ge(s_ga, 6)
            sums = ps["a0"][:, 0:2 * T * H].rearrange("p (c t h) -> p c t h", c=2, h=H)
            gv(dve.tensor_copy(gates[:, :, I_CUM], sums[:, 0]))
            gv(dve.tensor_tensor(g_tmp[:, 4], sums[:, 1], gates[:, :, I_CUM], ALU.subtract))
            dve.wait_ge(s_ga, 7)
            dve.scalar_tensor_tensor(gates[:, :, I_NEG], gates[:, :, I_BETA], -1.0, gates[:, :, I_IN], ALU.mult, ALU.mult).then_inc(s_gate, 1)

            def a_bv(u, par):
                after(dve, full["a1"], u, 1)
                after(dve, gs_set, u)
                after(dve, free["b0"], u - 1, 1)
                dve.tensor_tensor(b_v[:], bank("a1"), over_cols(gs[:, par, I_BETA]), ALU.mult).then_inc(free["a1"].sem, 1)

            def a_n2(u, par):
                after(dve, full["a2"], u, 1)
                after(dve, o_rstd, u - 2)
                dve.tensor_scalar(norm2[:, par, 0], ps["a2"][:, 0:2 * H], EPS, None, ALU.add).then_inc(n2.sem, 1)

            def a_khat(u, par):
                after(dve, rn, u)
                after(dve, kout_set, u - 1)
                dve.tensor_tensor(k_tok[:], bank("a0"), over_cols(norm2[:, par, 1, H:2 * H]), ALU.mult).then_inc(khat.sem, 1)

            def a_diff(u, par):
                after(dve, full["a1"], u, 2)
                dve.tensor_tensor(dec[:], bank("a1"), over_cols(gs[:, par, I_CUM]), ALU.subtract).then_inc(free["a1"].sem, 1)
                after(dve, free["a1"], u, 2)
                dve.tensor_scalar(dec_t[:], dec[:], 0.0, None, ALU.min).then_inc(clipped.sem, 1)
                after(dve, clipped, u, 1)
                dve.tensor_scalar(dec[:], dec[:], 0.0, None, ALU.max).then_inc(clipped.sem, 1)

            def a_low(u):
                after(dve, dec_masked, u, 3)
                after(dve, full["a0"], u, 3)
                dve.tensor_tensor(low[:], bank("a0"), dec[:], ALU.mult).then_inc(free["a0"].sem, 1)

            def a_qk(u):
                after(dve, full["a2"], u, 2)
                after(dve, full["b1"], u - 1, 2)
                dve.tensor_tensor(qk_t[:], bank("a2"), dec_t[:], ALU.mult).then_inc(free["a2"].sem, 1)

            def a_init(u):
                after(dve, free["a0"], u, 2)
                dve.tensor_tensor(off[:], low[:], over_heads(tab(T_LEVEL)), ALU.mult).then_inc(init.sem, 1)
                after(dve, init, u, 1)
                dve.tensor_tensor(inv[:], off[:], over_heads(ident), ALU.add).then_inc(init.sem, 1)
                after(dve, init, u, 2)
                after(dve, free["a1"], u, 3)
                after(dve, full["b0"], u - 1, 2)
                dve.tensor_tensor(off[:], low_t[:], over_heads(tab(T_LEVEL0T)), ALU.mult).then_inc(init.sem, 1)
                after(dve, init, u, 3)
                dve.tensor_tensor(inv_t[:], off[:], over_heads(ident), ALU.add).then_inc(init.sem, 1)

            def a_off(u, n):
                after(dve, full["a0"], u, 3 + n)
                if n == 1:
                    after(dve, init, u, 4)
                dve.tensor_tensor(off[:], bank("a0"), over_heads(tab(T_LEVEL + n * P)), ALU.mult).then_inc(free["a0"].sem, 1)

            def a_inv(u, n):
                after(dve, full["a2"], u, 2 + n)
                if n < LV:
                    dve.tensor_tensor(halves(inv[:], n, 0), ps_half(n, 0), halves(inv[:], n, 0), ALU.add)
                dve.tensor_tensor(halves(inv_t[:], n, 1), ps_half(n, 1), halves(inv_t[:], n, 1), ALU.add).then_inc(free["a2"].sem, 1)

            def b_resid(t, par):
                after(dve, full["b0"], t, 1)
                for h in range(H):
                    op = dve.scalar_tensor_tensor(resid[:, h], bank("b0")[:, h], gs[:, par, I_NEG, h:h + 1], b_v[:, h], ALU.mult, ALU.add)
                op.then_inc(free["b0"].sem, 1)

            def b_state(t, par):
                after(dve, full["b0"], t, 3)
                after(dve, full["b1"], t, 1)
                for h in range(H):
                    op = dve.scalar_tensor_tensor(state[:, h], state[:, h], gs[:, par, I_LAST, h:h + 1], bank("b0")[:, h], ALU.mult, ALU.add)
                op.then_inc(st_set.sem, 1)

            def b_o1(t, par):
                after(dve, full["b1"], t, 1)
                dve.tensor_tensor(o[:], bank("b1"), over_cols(gs[:, par, I_IN]), ALU.mult).then_inc(o1_set.sem, 1)

            def b_o(t):
                after(dve, full["b1"], t, 2)
                after(dve, o1_set, t)
                dve.tensor_tensor(o[:], bank("b1"), o[:], ALU.add).then_inc(o_set.sem, 1)

            def b_ms(t):
                after(dve, o_n, t, 2)
                dve.tensor_scalar(o_stat[:, 3], o_stat[:, 2], 1.0 / P, EPS * DK, ALU.mult, ALU.add).then_inc(o_ms.sem, 1)

            def b_mix(t):
                after(dve, o_rstd, t, 2)
                after(dve, zw_set, t)
                after(dve, full["d1"], t - 1, 1)
                for h in range(H):
                    op = dve.scalar_tensor_tensor(mix[:, h * P:(h + 1) * P], o[:, h], o_stat[:, 4, h:h + 1], zw[:, h], ALU.mult, ALU.mult)
                op.then_inc(mixa.sem, 1)

            def c_scores(t, par, n):
                after(dve, full["c0"], t, (3, 4, 8, 9)[n])
                carry(dve)
                mask = masks[:, 2 if isinstance(t, int) and t == 0 else par].rearrange("p a b -> p (a b)")
                for h in range(2):
                    slot = n % 2 + 2 * h
                    op = dve.tensor_tensor_reduce(scores[:, slot].rearrange("p a b -> p (a b)"),
                                                  ps["c0"][:, 256 * h:256 * h + 256], mask, HD ** -0.5, -3e38, ALU.add, ALU.max,
                                                  c_stat[:, 0, 4 * (n // 2) + slot:4 * (n // 2) + slot + 1])
                op.then_inc(free["c0"].sem, 1)

            def c_max(t, r):
                q = slice(4 * r, 4 * r + 4)
                after(dve, free["c0"], t, (4, 8)[r])
                dve.tensor_tensor(c_stat[:, 1, q], c_stat[:, 0, q], sinks[:, q], ALU.max).then_inc(cmax.sem, 1)
                after(dve, cmax, t, r + 1)
                dve.tensor_scalar(c_stat[:, 2, q], c_stat[:, 1, q], -1.0, None, ALU.mult).then_inc(cneg.sem, 1)
                dve.tensor_tensor(c_stat[:, 4, q], sinks[:, q], c_stat[:, 1, q], ALU.subtract).then_inc(csub.sem, 1)

            def c_out(t, r):
                q = slice(4 * r, 4 * r + 4)
                after(dve, cexp, t, r + 1)
                after(dve, csink, t, r + 1)
                dve.tensor_tensor(c_stat[:, 5, q], c_stat[:, 3, q], c_stat[:, 4, q], ALU.add).then_inc(cden.sem, 1)
                after(dve, cden, t, r + 1)
                dve.reciprocal(c_stat[:, 6, q], c_stat[:, 5, q]).then_inc(crec.sem, 1)
                after(dve, crec, t, r + 1)
                after(dve, full["c0"], t, (7, 12)[r])
                after(dve, full["d1"], t - 1, 1)
                cols = slice(H * P + r * 4 * HD, H * P + (r + 1) * 4 * HD)
                dve.tensor_tensor(mix[:, cols].rearrange("p (h d) -> p h d", d=HD), ps["c0"][:, 0:4 * HD].rearrange("p (h d) -> p h d", d=HD),
                                  c_stat[:, 6, q].unsqueeze(2).broadcast_to([P, 4, HD]), ALU.mult).then_inc(mixb.sem, 1)

            def d_lo(v):
                for b in range(2):
                    after(dve, dhi, v, b + 1)
                    after(dve, full["d1"], v - 1, 2)
                    dve.tensor_tensor(mix_lo[:, 4 * b:4 * b + 4], ps_d[:, b].rearrange("p (k c) -> p k c", c=P),
                                      mix_hi[:, 4 * b:4 * b + 4].bitcast(F32), ALU.subtract).then_inc(free[f"d{b}"].sem, 1)

            def d_ms(v, n):
                after(dve, dsq, v, n)
                dve.tensor_scalar(d_stat[:, 3 * n - 2:3 * n - 1], d_stat[:, 3 * n - 3:3 * n - 2], 1.0 / D, EPS, ALU.mult,
                                  ALU.add).then_inc(dms.sem, 1)

            def d_res(v):
                after(dve, drstd, v, 1)
                after(dve, full["d1"], v - 1, 3)
                for b in range(2):
                    cols = slice(b * HALF, (b + 1) * HALF)
                    dve.scalar_tensor_tensor(y[:, cols], ps_d[:, b], d_stat[:, 2:3], g_post[:, cols], ALU.mult, ALU.mult).then_inc(
                        free[f"d{b}"].sem, 1)
                after(dve, free["d1"], v, 2)
                after(dve, x_in, v)
                dve.tensor_tensor(x[:], x[:], y[:], ALU.add).then_inc(dx.sem, 1)

            def d_norm(v):
                after(dve, drstd, v, 2)
                dve.scalar_tensor_tensor(y[:], x[:], d_stat[:, 5:6], g_ffn[:], ALU.mult, ALU.mult).then_inc(dh.sem, 1)

            for s in [full[n] for n in ("d0", "d1")] + [free[n] for n in ("d0", "d1")] + [dhi, dsq, dms, drstd, dx, dh]:
                dve.sem_inc(s.sem, s.credit)
            dve.wait_ge(s_tab, 16)
            a_bv(0, 0)
            a_n2(0, 0)
            a_khat(0, 0)
            a_diff(0, 0)
            a_low(0)
            a_qk(0)
            a_init(0)
            for n in range(1, LV + 1):
                a_off(0, n)
                a_inv(0, n)
            dve.wait_ge(s_load, LOADS)
            dve.wait_ge(s_zero, 5)
            dve.wait_ge(s_whi, 1)
            dve.tensor_tensor(w_lo[:], h_t[:], w_hi[:].bitcast(F32), ALU.subtract).then_inc(s_wlo, 1)

            def step(t, par, a, d):
                b_resid(t, par)
                if a:
                    a_bv(t + 1, 1 - par)
                if d:
                    d_lo(t - 1)
                if a:
                    a_n2(t + 1, 1 - par)
                    a_khat(t + 1, 1 - par)
                b_o1(t, par)
                b_state(t, par)
                if a:
                    a_diff(t + 1, 1 - par)
                b_o(t)
                c_scores(t, par, 0)
                if a:
                    a_low(t + 1)
                    a_qk(t + 1)
                b_ms(t)
                c_scores(t, par, 1)
                c_max(t, 0)
                b_mix(t)
                if a:
                    a_init(t + 1)
                    a_off(t + 1, 1)
                    a_inv(t + 1, 1)
                    a_off(t + 1, 2)
                    a_inv(t + 1, 2)
                c_out(t, 0)
                if d:
                    d_ms(t - 1, 1)
                if a:
                    a_off(t + 1, 3)
                if d:
                    d_res(t - 1)
                if a:
                    a_inv(t + 1, 3)
                c_scores(t, par, 2)
                if a:
                    a_off(t + 1, 4)
                if d:
                    d_ms(t - 1, 2)
                c_scores(t, par, 3)
                c_max(t, 1)
                if a:
                    a_inv(t + 1, 4)
                if d:
                    d_norm(t - 1)
                if a:
                    a_off(t + 1, 5)
                    a_inv(t + 1, 5)
                c_out(t, 1)
                if a:
                    a_off(t + 1, 6)
                    a_inv(t + 1, 6)

            steps(dve, step)
            d_lo(T - 1)
            d_ms(T - 1, 1)
            d_res(T - 1)
            d_ms(T - 1, 2)
            d_norm(T - 1)

        @block.tensor
        def _(pe):
            def fill(name, t, k):
                after(pe, free[name], t if k > 1 else t - 1, k - 1 if k > 1 else None)

            def a_tr(u):
                after(pe, qkv_in, u)
                fill("a0", u, 1)
                for h in range(H):
                    op = pe.transpose(bank("a0")[:, h], qkv[:, H + h], ident)
                op.then_inc(full["a0"].sem, 1)
                fill("a1", u, 1)
                for h in range(H):
                    op = pe.transpose(bank("a1")[:, h], qkv[:, 2 * H + h], ident)
                op.then_inc(full["a1"].sem, 1)

            def a_norms(u):
                after(pe, squared, u)
                fill("a2", u, 1)
                for c in range(2 * H):
                    op = pe.matmul(ps["a2"][:, c:c + 1], squares[:, c], ones[:, 0:1], start=True, stop=True)
                op.then_inc(full["a2"].sem, 1)

            def a_sums(u):
                after(pe, tri_set, u)
                fill("a1", u, 2)
                pe.matmul(ps["a1"][:], ones, flat(g_tri[:]), start=True, stop=True).then_inc(full["a1"].sem, 1)

            def a_trk(u):
                after(pe, khat, u)
                for h in range(H):
                    op = pe.transpose(bank("a0")[:, h], k_tok[:, h], ident)
                op.then_inc(full["a0"].sem, 1)

            def a_kk(u):
                after(pe, free["a0"], u, 1)
                for h in range(H):
                    op = pe.matmul(bank("a0")[:, h], k_t[:, h], k_t[:, h], start=True, stop=True)
                op.then_inc(full["a0"].sem, 1)

            def a_kq(u):
                after(pe, n2, u)
                after(pe, qt_set, u)
                for h in range(H):
                    op = pe.matmul(bank("a2")[:, h], k_t[:, h], q_t[:, h], start=True, stop=True)
                op.then_inc(full["a2"].sem, 1)

            def a_trl(u):
                after(pe, free["a0"], u, 2)
                fill("a1", u, 3)
                for h in range(H):
                    op = pe.transpose(bank("a1")[:, h], low[:, h], ident)
                op.then_inc(full["a1"].sem, 1)

            def a_off(u, n):
                if n == 1:
                    after(pe, init, u, 2)
                    after(pe, free["a1"], u, 3)
                else:
                    after(pe, free["a2"], u, n)
                for h in range(H):
                    op = pe.matmul(bank("a0")[:, h], low_t[:, h], inv[:, h], start=True, stop=True)
                op.then_inc(full["a0"].sem, 1)

            def a_inv(u, n):
                after(pe, free["a0"], u, 2 + n)
                after(pe, init, u, 4)
                after(pe, free["a2"], u, n)
                for h in range(H):
                    if n < LV:
                        pe.matmul(ps_half(n, 0)[:, h], inv_t[:, h], half_cols(off[:], h, n, 0), start=True, stop=True)
                    op = pe.matmul(ps_half(n, 1)[:, h], off[:, h], half_cols(inv_t[:], h, n, 1), start=True, stop=True)
                op.then_inc(full["a2"].sem, 1)

            def b_ks(t):
                after(pe, st_set, t - 1)
                for h in range(H):
                    op = pe.matmul(bank("b0")[:, h], k_t[:, h], state[:, h], start=True, stop=True)
                op.then_inc(full["b0"].sem, 1)

            def b_vnew(t):
                after(pe, free["b0"], t, 1)
                for h in range(H):
                    op = pe.matmul(bank("b0")[:, h], inv_t[:, h], resid[:, h], start=True, stop=True)
                op.then_inc(full["b0"].sem, 1)

            def b_o1(t):
                after(pe, o_set, t - 1)
                for h in range(H):
                    op = pe.matmul(bank("b1")[:, h], q_t[:, h], state[:, h], start=True, stop=True)
                op.then_inc(full["b1"].sem, 1)

            def b_ds(t):
                after(pe, free["b0"], t, 2)
                after(pe, kout_set, t)
                for h in range(H):
                    op = pe.matmul(bank("b0")[:, h], k_out[:, h], v_new[:, h], start=True, stop=True)
                op.then_inc(full["b0"].sem, 1)

            def b_o2(t):
                after(pe, o1_set, t)
                for h in range(H):
                    op = pe.matmul(bank("b1")[:, h], qk_t[:, h], v_new[:, h], start=True, stop=True)
                op.then_inc(full["b1"].sem, 1)

            def c_trq(t):
                after(pe, row_in, t)
                after(pe, mixb, t - 1, 2)
                for b in range(4):
                    op = pe.transpose(bank("c0")[:, b], row[:, Q0 + b * P:Q0 + (b + 1) * P], ident)
                op.then_inc(full["c0"].sem, 1)

            def c_trk(t):
                after(pe, kdup_set, t)
                after(pe, free["c0"], t, 1)
                for kv in range(KVH):
                    op = pe.transpose(bank("c0")[:, kv], k_dup[:, kv].rearrange("p a d -> p (a d)"), ident)
                op.then_inc(full["c0"].sem, 1)

            def c_scores(t, n):
                if n == 2:
                    after(pe, mixb, t, 1)
                else:
                    after(pe, free["c0"], t, (2, 3, None, 7)[n])
                for h in range(2):
                    part = slice(n % 2 * HD, (n % 2 + 1) * HD)
                    op = pe.matmul(ps["c0"][:, 256 * h:256 * h + 256], q_b[part, n // 2 * 2 + h], k_b[part, n // 2].rearrange("p a b -> p (a b)"),
                                   start=True, stop=True)
                op.then_inc(full["c0"].sem, 1)

            def c_trp(t, n):
                after(pe, cexp, t, n // 2 + 1)
                after(pe, free["c0"], t, (4, 5, 8, 9)[n])
                for j in range(4):
                    op = pe.transpose(bank("c0")[:, j], scores[:, 2 * (n % 2) + j // 2, j % 2], ident)
                op.then_inc(full["c0"].sem, 1)

            def c_pv(t, r):
                after(pe, free["c0"], t, (6, 10)[r])
                after(pe, vb_set, t)
                for h in range(4):
                    for kt in range(2):
                        op = pe.matmul(ps["c0"][:, h * HD:(h + 1) * HD], p_t[:, h, kt], v_b[:, kt, r * HD:(r + 1) * HD],
                                       start=(kt == 0), stop=(kt == 1))
                op.then_inc(full["c0"].sem, 1)

            def d_tr(v):
                after(pe, mixa, v)
                after(pe, mixb, v, 2)
                for b in range(2):
                    fill(f"d{b}", v, 1)
                    for j in range(4):
                        k = 4 * b + j
                        op = pe.transpose(ps_d[:, b, j * P:(j + 1) * P], mix[:, k * P:(k + 1) * P], ident)
                    op.then_inc(full[f"d{b}"].sem, 1)

            def d_mm(v, half, ks):
                if half == 0 and ks[0] == 0:
                    pe.wait_ge(s_wlo, 1)
                    after(pe, free["d0"], v, 1)
                    after(pe, free["d1"], v, 1)
                cols = slice(half * HALF, (half + 1) * HALF)
                for k in ks:
                    pe.matmul(ps_d[:, half], mix_hi[:, k], w_hi[:, k, cols], start=(k == 0), stop=False)
                    pe.matmul(ps_d[:, half], mix_hi[:, k], w_lo[:, k, cols], start=False, stop=False)
                    op = pe.matmul(ps_d[:, half], mix_lo[:, k], w_hi[:, k, cols], start=False, stop=(k == KD - 1))
                if ks[-1] == KD - 1:
                    op.then_inc(full[f"d{half}"].sem, 1)

            def d_tr2(v):
                after(pe, dh, v)
                for b in range(2):
                    for j in range(4):
                        k = 4 * b + j
                        op = pe.transpose(ps_d[:, b, j * P:(j + 1) * P], y[:, k * P:(k + 1) * P], ident)
                    op.then_inc(full[f"d{b}"].sem, 1)

            pe.wait_ge(s_tab, 16)
            pe.wait_ge(s_gv, 7)
            for c, m in enumerate((tri, ones)):
                op = pe.matmul(ps["a0"][:, c * T * H:(c + 1) * T * H].rearrange("p (t h) -> p t h", h=H), m, gates[:, :, I_G],
                               start=True, stop=True)
            op.then_inc(s_ps_g, 1)
            pe.wait_ge(s_gate, 1)
            pe.wait_ge(s_zero, 5)
            a_tr(0)
            a_norms(0)
            a_sums(0)
            a_trk(0)
            a_kk(0)
            a_kq(0)
            a_trl(0)
            for n in range(1, LV + 1):
                a_off(0, n)
                a_inv(0, n)

            def step(t, par, a, d):
                A = (lambda f, *w: f(t + 1, *w)) if a else (lambda f, *w: None)
                D_ = (lambda f, *w: f(t - 1, *w)) if d else (lambda f, *w: None)
                after(pe, free["a2"], t)
                b_ks(t)
                A(a_tr)
                b_vnew(t)
                D_(d_tr)
                A(a_norms)
                c_trq(t)
                b_o1(t)
                b_ds(t)
                A(a_sums)
                D_(d_mm, 0, [0, 1])
                c_trk(t)
                b_o2(t)
                A(a_trk)
                D_(d_mm, 0, [2, 3, 4])
                c_scores(t, 0)
                A(a_kk)
                A(a_kq)
                D_(d_mm, 0, [5, 6, 7])
                c_scores(t, 1)
                A(a_trl)
                D_(d_mm, 1, [0, 1, 2])
                A(a_off, 1)
                D_(d_mm, 1, [3])
                A(a_inv, 1)
                c_trp(t, 0)
                D_(d_mm, 1, [4])
                A(a_off, 2)
                c_trp(t, 1)
                D_(d_mm, 1, [5])
                A(a_inv, 2)
                c_pv(t, 0)
                D_(d_mm, 1, [6, 7])
                A(a_off, 3)
                c_scores(t, 2)
                A(a_inv, 3)
                c_scores(t, 3)
                A(a_off, 4)
                A(a_inv, 4)
                c_trp(t, 2)
                A(a_off, 5)
                c_trp(t, 3)
                A(a_inv, 5)
                c_pv(t, 1)
                A(a_off, 6)
                D_(d_tr2)
                A(a_inv, 6)

            steps(pe, step)
            d_tr(T - 1)
            d_mm(T - 1, 0, list(range(KD)))
            d_mm(T - 1, 1, list(range(KD)))
            d_tr2(T - 1)


FT = DFF // P
FG = FT // 2


def ffn_block(nc, io, h_t):
    with ExitStack() as ctx:
        sb = lambda name, shape, dt=F32: ctx.enter_context(nc.sbuf_tensor(name, shape, dt))
        sem = lambda name: ctx.enter_context(nc.semaphore(name))

        NT = FTAPS * 2 * FT
        h_hi = sb("f_h_hi", [P, KD, S], F32R)
        h_lo = sb("f_h_lo", [P, KD, S], F32R)
        acc = h_t[:].rearrange("p k s -> p (k s)").rearrange("p (t d) -> p t d", t=T)
        slab = 2 * P * KD
        raw = sb("f_raw", [P, 2, slab])
        w_hi = sb("f_w_hi", [P, 3, slab], F32R)
        w_lo = sb("f_w_lo", [P, 3, slab], F32R)
        conv = sb("f_conv", [P, 4, S])
        y_hi = sb("f_y_hi", [P, 2, S], F32R)
        y_lo = sb("f_y_lo", [P, 2, S], F32R)
        junk = sb("f_junk", [P, D], BF16)
        gain = sb("f_gain", [P, D])
        ident = sb("f_ident", [P, P])
        rows_a = sb("f_rows_a", [P, P])
        rows_b = sb("f_rows_b", [NT + 2 * FT - P, P])
        taps = sb("f_taps", [P, NT + 2 * FT])
        stat = sb("f_stat", [P, 3, T])
        power = sb("f_power", [P, 1])

        ps_up = ctx.enter_context(nc.psum_tensor("f_ps_up", [P, 2, S], F32))
        ps_dn = ctx.enter_context(nc.psum_tensor("f_ps_dn", [P, 4, HALF], F32))

        s_ident, s_rows, s_gain = sem("f_ident_in"), sem("f_rows_in"), sem("f_gain_in")
        s_raw = [sem("f_raw0"), sem("f_raw1")]
        s_taps_ps, s_taps = sem("f_taps_ps"), sem("f_taps_ready")
        s_hhi, s_hlo, s_zero = sem("f_hhi"), sem("f_hlo"), sem("f_zero")
        s_whi, s_wlo = sem("f_whi"), sem("f_wlo")
        s_pair = sem("f_pair")
        s_first, s_tap, s_conv = sem("f_first"), sem("f_tap"), sem("f_convolved")
        s_gelu, s_prod = sem("f_gelu"), sem("f_prod")
        s_yhi, s_ylo = sem("f_yhi"), sem("f_ylo")
        s_dn, s_acc = sem("f_dn"), sem("f_acc")
        s_freed, s_power = sem("f_freed"), sem("f_power_set")
        s_sq, s_ms, s_rstd, s_norm, s_res = sem("f_sq"), sem("f_ms"), sem("f_rstd"), sem("f_norm"), sem("f_res")
        s_xr = [sem(f"f_xr{n}") for n in range(4)]
        s_out = [sem(f"f_out{n}") for n in range(4)]

        w_up = io["w_up"].rearrange("o (k p) n -> p (o k) n", p=P)
        w_down = io["w_down"].rearrange("o f d -> (o f d)")
        GATE, VALUE, DOWN = 0, 1, 2

        def n_gate(g):
            return 3 * g

        def n_value(g):
            return 3 * g + 1

        def n_down(g):
            return 3 * g + 2

        LAST_DOWN = n_down(FG) - 2

        def steps(eng, step):
            with eng.Fori(1, FG - 1) as g:
                step(g, False)
            step(FG - 1, True)

        def up_w(part, kind):
            return (w_hi, w_lo)[part][:, kind].rearrange("p (k n) -> p k n", k=KD)

        def dn_w(part):
            return (w_hi, w_lo)[part][:, DOWN].rearrange("p (k n) -> p k n", k=2)

        block = ctx.enter_context(nc.Block("ffn"))

        @block.sync
        def _(sp):
            def reg(v):
                return v if isinstance(v, int) else sp.snap(v)

            def up_src(kind, g):
                return w_up[:, :, bass.ds(reg(g * (2 * P) + kind * DFF), 2 * P)]

            def down_src(g):
                return w_down[bass.ds(reg(g * (2 * P * D)), 2 * P * D)].rearrange("(k p d) -> p k d", k=2, p=P)

            def load(slot, src, k):
                sp.dma_start(raw[:, slot].rearrange("p (k n) -> p k n", k=k), src).then_inc(s_raw[slot], 16)

            def free(n):
                sp.wait_ge(s_whi, n)
                sp.wait_ge(s_wlo, n)
                sp.sem_inc(s_freed, 1)

            load(0, up_src(GATE, 0), KD)
            load(1, up_src(VALUE, 0), KD)
            sp.dma_start(ident[:], io["tables"][:, T_ID:T_ID + P]).then_inc(s_ident, 16)
            rows = io["ffn_conv_w"].rearrange("o k (c p) -> (o k c) p", p=P)
            sp.dma_start(rows_a[:], rows[0:P]).then_inc(s_rows, 16)
            sp.dma_start(rows_b[0:NT - P], rows[P:NT]).then_inc(s_rows, 16)
            sp.dma_start(rows_b[NT - P:], io["ffn_conv_b"].rearrange("o (c p) -> (o c) p", p=P)).then_inc(s_rows, 16)
            free(1)
            load(0, up_src(GATE, 1), KD)
            free(2)
            load(1, up_src(VALUE, 1), KD)
            sp.dma_start(gain[:], io["g_post_ffn"][0:1, :].broadcast_to([P, D])).then_inc(s_gain, 16)
            free(3)
            load(0, down_src(0), 2)

            def step(g, last):
                if not last:
                    value_free, gate_free, down_free = reg(n_value(g)), reg(n_down(g)), reg(n_gate(g + 1))
                    gate_from, value_from, down_from = up_src(GATE, g + 1), up_src(VALUE, g + 1), down_src(g)
                    free(value_free)
                    load(1, value_from, KD)
                    free(gate_free)
                    load(0, gate_from, KD)
                    free(down_free)
                    load(0, down_from, 2)
                else:
                    free(n_down(g))
                    load(0, down_src(g), 2)

            steps(sp, step)
            sp.wait_ge(s_ylo, 2 * FG)
            sp.wait_ge(s_yhi, 2 * FG)
            for t in range(4):
                sp.dma_start(conv[:, t], io["res"][t]).then_inc(s_xr[t], 16)
            for t in range(T):
                sp.wait_ge(s_res, t + 1)
                sp.dma_start(io["out"][0, t * P:(t + 1) * P, :], conv[:, t % 4]).then_inc(s_out[t % 4], 16)
                if t + 4 < T:
                    sp.wait_ge(s_out[t % 4], 16)
                    sp.dma_start(conv[:, t % 4], io["res"][t + 4]).then_inc(s_xr[t % 4], 16)
            for q in s_out:
                sp.wait_ge(q, 16 * (T // 4))

        @block.scalar
        def _(act):
            def split(n, kind, slot, loads):
                act.wait_ge(s_raw[slot], 16 * loads)
                act.copy(w_hi[:, kind], raw[:, slot]).then_inc(s_whi, 1)

            def first(n, q, ct):
                act.wait_ge(s_pair, n + 1)
                act.activation(conv[:, q], ps_up[:, q % 2], ACT.Identity, bias=taps[:, bass.ds(ct + NT, 1)],
                               scale=taps[:, bass.ds(ct + (FTAPS - 1) * 2 * FT, 1)]).then_inc(s_first, 1)

            def step(g, last, lead=False):
                if not lead:
                    act.wait_ge(s_dn, g * 16 - 15)
                    split(n_down(g), DOWN, 0, g * 2 + 1)
                    act.wait_ge(s_prod, 2 * g)
                for c in range(2):
                    first(4 * g + c, c, g * 2 + c)
                for c in range(2):
                    act.wait_ge(s_conv, 4 * g + c + 3)
                    act.activation(conv[:, c], conv[:, c], ACT.Gelu_apprx_tanh).then_inc(s_gelu, 1)
                if not last:
                    act.wait_ge(s_pair, 4 * g + 2)
                    split(n_gate(g + 1), GATE, 0, 2 * g + 2)
                if not lead:
                    act.wait_ge(s_ylo, 2 * g)
                for c in range(2):
                    first(4 * g + 2 + c, 2 + c, g * 2 + (c + FT))
                if not last:
                    act.wait_ge(s_pair, 4 * g + 4)
                    split(n_value(g + 1), VALUE, 1, g + 2)
                for c in range(2):
                    act.wait_ge(s_prod, 2 * g + c + 1)
                    if not lead:
                        act.wait_ge(s_dn, 16 * g + 1)
                    act.copy(y_hi[:, c], conv[:, 2 + c]).then_inc(s_yhi, 1)

            for n, (kind, slot) in enumerate([(GATE, 0), (VALUE, 1)]):
                split(n + 1, kind, slot, 1)
                for k in range(4 * n, 4 * n + 4):
                    act.copy(h_hi[:, k], h_t[:, k]).then_inc(s_hhi, 1)
            act.wait_ge(s_taps, 1)
            step(0, False, lead=True)
            steps(act, step)
            act.wait_ge(s_dn, 16 * (FG - 1) + 1)
            split(LAST_DOWN, DOWN, 0, 2 * FG)
            for t in range(T):
                act.wait_ge(s_acc, 16 * (FG - 1) + 2 * t + 2 + 4)
                act.activation(junk[:], acc[:, t], ACT.Square, accum_out=stat[:, 0, t:t + 1]).then_inc(s_sq, 1)

        @block.vector
        def _(dve):
            dve.sem_inc(s_conv, 2)
            dve.sem_inc(s_acc, 4)

            def split(n, kind, slot):
                dve.wait_ge(s_whi, n)
                dve.tensor_tensor(w_lo[:, kind], raw[:, slot], w_hi[:, kind].bitcast(F32), ALU.subtract).then_inc(s_wlo, 1)

            def convolve(n, q, ct):
                dve.wait_ge(s_first, n + 1)
                for k in range(1, FTAPS):
                    op = dve.scalar_tensor_tensor(conv[:, q, k:S], ps_up[:, q % 2, 0:S - k],
                                                  taps[:, bass.ds(ct + (FTAPS - 1 - k) * 2 * FT, 1)], conv[:, q, k:S],
                                                  ALU.mult, ALU.add)
                    if k == 1:
                        op.then_inc(s_tap, 1)
                        dve.wait_ge(s_tap, n + 1)
                    else:
                        op.then_inc(s_conv, 1)

            def accumulate(m, t, half):
                dve.wait_ge(s_dn, m + 2)
                cols = acc[:, t, half * HALF:(half + 1) * HALF]
                dve.tensor_tensor(cols, ps_dn[:, (2 * t + half) % 4], cols, ALU.add).then_inc(s_acc, 1)

            def step(g, last, lead=False):
                if not lead:
                    split(n_down(g), DOWN, 0)
                for c in range(2):
                    convolve(4 * g + c, c, g * 2 + c)
                if not last:
                    split(n_gate(g + 1), GATE, 0)
                for c in range(2):
                    convolve(4 * g + 2 + c, 2 + c, g * 2 + (c + FT))
                for c in range(2):
                    dve.wait_ge(s_gelu, 2 * g + c + 1)
                    dve.wait_ge(s_conv, 4 * g + c + 5)
                    dve.tensor_tensor(conv[:, 2 + c], conv[:, c], conv[:, 2 + c], ALU.mult).then_inc(s_prod, 1)
                if not last:
                    split(n_value(g + 1), VALUE, 1)
                if not lead:
                    for j in range(2 * T):
                        accumulate(g * 16 + (j - 16), j // 2, j % 2)
                for c in range(2):
                    dve.wait_ge(s_yhi, 2 * g + c + 1)
                    dve.tensor_tensor(y_lo[:, c], conv[:, 2 + c], y_hi[:, c].bitcast(F32), ALU.subtract).then_inc(s_ylo, 1)

            def finish(t):
                dve.wait_ge(s_rstd, t + 1)
                dve.scalar_tensor_tensor(acc[:, t], acc[:, t], stat[:, 2, t:t + 1], gain[:], ALU.mult, ALU.mult).then_inc(s_norm, 1)
                dve.wait_ge(s_norm, t + 1)
                dve.wait_ge(s_xr[t % 4], 16 * (t // 4 + 1))
                dve.tensor_tensor(conv[:, t % 4], conv[:, t % 4], acc[:, t], ALU.add).then_inc(s_res, 1)

            for n, (kind, slot) in enumerate([(GATE, 0), (VALUE, 1)]):
                split(n + 1, kind, slot)
                for k in range(4 * n, 4 * n + 4):
                    dve.wait_ge(s_hhi, k + 1)
                    dve.tensor_tensor(h_lo[:, k], h_t[:, k], h_hi[:, k].bitcast(F32), ALU.subtract).then_inc(s_hlo, 1)
            dve.wait_ge(s_taps_ps, 1)
            dve.tensor_copy(taps[:], ps_dn[:, 0, 0:NT + 2 * FT]).then_inc(s_taps, 1)
            dve.wait_ge(s_taps, 1)
            step(0, False, lead=True)
            dve.wait_ge(s_zero, 1)
            steps(dve, step)
            split(LAST_DOWN, DOWN, 0)
            dve.wait_ge(s_gain, 16)
            for t in range(T + 1):
                if t < T:
                    for half in range(2):
                        accumulate(16 * (FG - 1) + 2 * t + half, t, half)
                    dve.wait_ge(s_sq, t + 1)
                    dve.tensor_scalar(stat[:, 1, t:t + 1], stat[:, 0, t:t + 1], 1.0 / D, EPS, ALU.mult, ALU.add).then_inc(s_ms, 1)
                if t >= 1:
                    finish(t - 1)

        @block.gpsimd
        def _(pool):
            pool.memset(power[:], -0.5).then_inc(s_power, 1)
            pool.wait_ge(s_hlo, KD)
            pool.wait_ge(s_hhi, KD)
            pool.memset(acc, 0.0).then_inc(s_zero, 1)
            pool.wait_ge(s_power, 1)
            for t in range(T):
                pool.wait_ge(s_ms, t + 1)
                pool.tensor_tensor(stat[:, 2, t:t + 1], stat[:, 1, t:t + 1], power[:], ALU.pow).then_inc(s_rstd, 1)

        @block.tensor
        def _(pe):
            def up(n, kind, c):
                pe.wait_ge(s_conv, n + 1)
                for half in range(2):
                    bank = ps_up[:, c, half * HALF:(half + 1) * HALF]
                    cols = slice(half * HALF, (half + 1) * HALF)
                    for k in range(KD):
                        hi = up_w(0, kind)[:, k, c * P:(c + 1) * P]
                        lo = up_w(1, kind)[:, k, c * P:(c + 1) * P]
                        pe.matmul(bank, hi, h_hi[:, k, cols], start=(k == 0), stop=False)
                        pe.matmul(bank, hi, h_lo[:, k, cols], start=False, stop=False)
                        op = pe.matmul(bank, lo, h_hi[:, k, cols], start=False, stop=(k == KD - 1))
                op.then_inc(s_pair, 1)

            def down(g):
                pe.wait_ge(s_wlo, LAST_DOWN if isinstance(g, int) and g == FG else n_down(g))
                pe.wait_ge(s_ylo, 2 * g)
                for j in range(2 * T):
                    t, half = j // 2, j % 2
                    pe.wait_ge(s_acc, g * 16 + (j - 15))
                    for k in range(2):
                        y = slice(t * P, (t + 1) * P)
                        cols = slice(half * HALF, (half + 1) * HALF)
                        bank = ps_dn[:, j % 4]
                        pe.matmul(bank, y_hi[:, k, y], dn_w(0)[:, k, cols], start=(k == 0), stop=False)
                        pe.matmul(bank, y_hi[:, k, y], dn_w(1)[:, k, cols], start=False, stop=False)
                        op = pe.matmul(bank, y_lo[:, k, y], dn_w(0)[:, k, cols], start=False, stop=(k == 1))
                    op.then_inc(s_dn, 1)

            def ups(g):
                for kind, n in ((GATE, n_gate(g)), (VALUE, n_value(g))):
                    pe.wait_ge(s_wlo, n)
                    for c in range(2):
                        up(4 * g + 2 * kind + c, kind, c)

            def step(g, last):
                ups(g)
                down(g)

            pe.sem_inc(s_dn, 1)
            pe.wait_ge(s_ident, 16)
            pe.wait_ge(s_rows, 48)
            nb = NT + 2 * FT - P
            pe.transpose(ps_dn[:, 0, 0:P], rows_a[:], ident[:])
            pe.transpose(ps_dn[:, 0, P:P + nb], rows_b[:], ident[0:nb, 0:nb]).then_inc(s_taps_ps, 1)
            pe.wait_ge(s_hlo, KD)
            for kind in (GATE, VALUE):
                pe.wait_ge(s_wlo, kind + 1)
                for c in range(2):
                    up(2 * kind + c, kind, c)
            pe.wait_ge(s_taps, 1)
            steps(pe, step)
            down(FG)


_INS = ["x", "g_pre_mix", "w_in", "gdn_conv_w", "gdn_A_log", "gdn_dt_bias", "gdn_norm_w", "attn_sinks", "w_out",
        "g_post_mix", "g_pre_ffn", "w_up", "ffn_conv_w", "ffn_conv_b", "w_down", "g_post_ffn"]


def kernel(**inputs):
    import concourse.bacc as bacc
    from concourse.bass_utils import run_bass_kernel_spmd

    nc = bacc.Bacc("TRN2", target_bir_lowering=False, num_devices=1)
    arrays, io = {}, {}
    for name in _INS:
        a = np.ascontiguousarray(inputs[name])
        arrays[f"in_{name}"] = a
        io[name] = nc.dram_tensor(f"in_{name}", a.shape, mybir.dt.from_np(a.dtype), kind="ExternalInput").ap()
    arrays["in_tables"] = tables()
    io["tables"] = nc.dram_tensor("in_tables", (P, T_W), F32, kind="ExternalInput").ap()
    SCR = "Internal"
    io["rows"] = nc.dram_tensor("rows", (T, P, ROW), F32, kind=SCR).ap()
    io["qkv"] = nc.dram_tensor("qkv", (T, P, A_TILES, P), F32, kind=SCR).ap()
    io["out"] = nc.dram_tensor("out", (1, S, D), F32, kind="ExternalOutput").ap()
    io["res"] = nc.dram_tensor("res", (T, P, D), F32, kind=SCR).ap()
    project_block(nc, io)
    with nc.sbuf_tensor("h_t", [P, KD, S], F32) as h_t:
        mix_block(nc, io, h_t)
        ffn_block(nc, io, h_t)
    r = run_bass_kernel_spmd(nc, [arrays], core_ids=[0])
    return r.results[0]["out"]
```

```python
from contextlib import ExitStack

import numpy as np

import concourse.bass as bass
from concourse import mybir

P = 128
F32 = mybir.dt.float32
F32R = mybir.dt.float32r
BF16 = mybir.dt.bfloat16
ALU = mybir.AluOpType
ACT = mybir.ActivationFunctionType
AX_X = mybir.AxisListType.X

EPS = 1e-6
D = 1024
S = 1024
T = S // P
KD = D // P
HALF = 512
GH, DK = 4, 128
QH, KVH, HD = 8, 2, 64
GROUP = QH // KVH
CHUNK = 64
ROT = HD // 4
ROPE_THETA = 500000.0
GTAPS, FTAPS = 4, 3
DFF = 2816
A_CH = 3 * GH * DK
A_TILES = A_CH // P
Z0, AB0, Q0 = 0, GH * DK, GH * DK + 2 * GH
K0 = Q0 + QH * HD
V0 = K0 + KVH * HD
ROW = V0 + KVH * HD
IN_W = A_CH + ROW
GROUPS = [(0, HALF), (HALF, HALF), (2 * HALF, ROW - 2 * HALF)]
NEG = -1e30

T_ID, T_TRI, T_STRICT = 0, P, 2 * P
LEVELS = [1, 2, 4, 8, 16, 32, 64]
T_LEVEL = 3 * P
T_LEVEL0T = T_LEVEL + len(LEVELS) * P
T_CUR, T_PREV = T_LEVEL0T + P, T_LEVEL0T + 2 * P
T_ONES = T_LEVEL0T + 3 * P
T_ROPE = T_ONES + P
T_W = T_ROPE + T * 2 * (ROT // 2)


def tables():
    i, j = np.arange(P)[:, None], np.arange(P)[None, :]
    t = np.zeros((P, T_W), np.float32)
    t[:, T_ID:T_ID + P] = i == j
    t[:, T_TRI:T_TRI + P] = i <= j
    t[:, T_STRICT:T_STRICT + P] = j < i
    for n, s in enumerate(LEVELS):
        m = (i // (2 * s) == j // (2 * s)) & ((i // s) % 2 == 1) & ((j // s) % 2 == 0)
        t[:, T_LEVEL + n * P:T_LEVEL + (n + 1) * P] = -1.0 * m
        if n == 0:
            t[:, T_LEVEL0T:T_LEVEL0T + P] = -1.0 * m.T
    t[:, T_CUR:T_CUR + P] = np.where(j // CHUNK <= i // CHUNK, 0.0, NEG)
    t[:, T_PREV:T_PREV + P] = np.where((i // CHUNK == 0) & (j // CHUNK == 1), 0.0, NEG)
    t[:, T_ONES:T_ONES + P] = 1.0
    pos = np.arange(S, dtype=np.float32)
    inv = (np.float32(ROPE_THETA) ** (-np.arange(0, ROT, 2, dtype=np.float32) / np.float32(ROT))).astype(np.float32)
    ang = (pos[:, None] * inv[None, :]).astype(np.float32).reshape(T, P, ROT // 2)
    r = t[:, T_ROPE:].reshape(P, T, 2, ROT // 2)
    r[:, :, 0] = np.cos(ang).transpose(1, 0, 2)
    r[:, :, 1] = np.sin(ang).transpose(1, 0, 2)
    return t


def project_block(nc, io):
    SLOTS = 4
    with ExitStack() as ctx:
        sb = lambda name, shape, dt=F32: ctx.enter_context(nc.sbuf_tensor(name, shape, dt))
        sem = lambda name: ctx.enter_context(nc.semaphore(name))

        h_hi = sb("h_hi", [P, KD, S], F32R)
        h_lo = sb("h_lo", [P, KD, S], F32R)
        wbuf = sb("wbuf", [P, 2 * KD * ROW], F32R)
        raw = sb("raw", [P, SLOTS, KD // 2 * GROUPS[2][1]])
        tile_hi = sb("tile_hi", [P, 2, KD, P], F32R)
        tile_lo = sb("tile_lo", [P, 2, KD, P], F32R)
        xin = sb("xin", [P, 2, D])
        h = sb("h", [P, D])
        junk = sb("junk", [P, D], BF16)
        row = sb("row", [P, ROW])
        gain = sb("gain", [P, D])
        ident = sb("ident", [P, P])
        rope = sb("rope", [P, T, 2, ROT // 2])
        rot = sb("rot", [P, 4, QH + KVH, ROT // 2])
        stat = sb("stat", [P, 2, 4])
        power = sb("power", [P, 1])
        convrows = sb("convrows", [GTAPS * A_TILES, P])
        taps = sb("taps", [P, GTAPS * A_TILES])
        conv = xin

        ps_t = ctx.enter_context(nc.psum_tensor("ps_t", [P, 2, HALF], F32))
        ps_g = ctx.enter_context(nc.psum_tensor("ps_g", [P, 6, HALF], F32))

        s_x = [sem("s_x0"), sem("s_x1")]
        s_const, s_gain, s_rope, s_conv_rows = sem("s_const"), sem("s_gain"), sem("s_rope"), sem("s_conv_rows")
        s_raw = [sem(f"s_raw{n}") for n in range(SLOTS)]
        s_slab = [sem("s_slab0"), sem("s_slab1")]
        s_whi, s_wlo = sem("s_whi"), sem("s_wlo")
        s_power = sem("s_power")
        s_taps_ps, s_taps = sem("s_taps_ps"), sem("s_taps")
        s_sq, s_ms, s_rstd = sem("s_sq"), sem("s_ms"), sem("s_rstd")
        s_h, s_tr = sem("s_h"), sem("s_tr")
        s_hi, s_lo, s_big = sem("s_hi"), sem("s_lo"), sem("s_big")
        s_mm = sem("s_mm")
        s_z, s_mid, s_last = sem("s_z"), sem("s_mid"), sem("s_last")
        s_rot4, s_rot, s_row_out = sem("s_rot4"), sem("s_rot"), sem("s_row_out")
        s_pair, s_first, s_tap, s_conv = sem("s_pair"), sem("s_first"), sem("s_tap"), sem("s_conv")
        s_silu = sem("s_silu")
        s_qkv_out = [sem("s_qkv_out0"), sem("s_qkv_out1")]

        w_in = io["w_in"].rearrange("o (k p) n -> p (o k) n", p=P)
        rows_flat = io["rows"].rearrange("t p n -> (t p n)")
        x_tiles = io["x"].rearrange("o (t p) d -> (o t) p d", p=P)

        chunks = [(g, k, 2) for g in range(2) for k in range(0, KD, 2)] + [(2, 0, KD // 2), (2, KD // 2, KD // 2)]
        ready = [4, 8, 10]
        base = [0, 2 * KD * HALF, 4 * KD * HALF]

        def group_w(g, part):
            n = GROUPS[g][1]
            a = base[g] + part * KD * n
            return wbuf[:, a:a + KD * n].rearrange("p (k n) -> p k n", k=KD)

        def raw_chunk(c):
            g, _, nk = chunks[c]
            n = GROUPS[g][1]
            return raw[:, c % SLOTS, 0:nk * n].rearrange("p (k n) -> p k n", k=nk)

        def slab_w(slot, part):
            a = slot * 4 * P * KD + part * 2 * P * KD
            return wbuf[:, a:a + 2 * P * KD].rearrange("p (k n) -> p k n", k=KD)

        NCH = len(chunks)
        SLABS = A_TILES // 2

        def raw_slab(slot):
            both = raw[:, 2 * slot:2 * slot + 2].rearrange("p a n -> p (a n)")
            return both[:, 0:2 * P * KD].rearrange("p (k n) -> p k n", k=KD)

        def raw_count(n):
            return 16 * (n // SLOTS + 1)

        block = ctx.enter_context(nc.Block("project"))

        def tiles(eng, step, first=True):
            if first:
                step(0, 0, 0)
            with eng.Fori(0, T // 2 - 1) as i:
                step(i * 2 + 1, 1, i)
                step(i * 2 + 2, 0, i)
            step(T - 1, 1, T // 2 - 1)

        def slabs(eng, step):
            with eng.Fori(0, SLABS // 2 - 1) as i:
                step(i * 2, 0, i, False)
                step(i * 2 + 1, 1, i, False)
            step(SLABS - 2, 0, SLABS // 2 - 1, False)
            step(SLABS - 1, 1, SLABS // 2 - 1, True)

        @block.sync
        def _(sp):
            for q in s_qkv_out:
                sp.sem_inc(q, 16)
            sp.dma_start(xin[:, 0], x_tiles[0]).then_inc(s_x[0], 16)
            sp.dma_start(gain[:], io["g_pre_mix"][0:1, :].broadcast_to([P, D])).then_inc(s_gain, 16)
            sp.dma_start(ident[:], io["tables"][:, T_ID:T_ID + P]).then_inc(s_const, 16)

            def load_chunk(c):
                g, k0, nk = chunks[c]
                c0, n = GROUPS[g]
                if c >= SLOTS:
                    sp.wait_ge(s_whi, c - SLOTS + 1)
                    sp.wait_ge(s_wlo, c - SLOTS + 1)
                sp.dma_start(raw_chunk(c), w_in[:, k0:k0 + nk, A_CH + c0:A_CH + c0 + n]).then_inc(s_raw[c % SLOTS], 16)

            for c in range(SLOTS):
                load_chunk(c)
            sp.dma_start(xin[:, 1], x_tiles[1]).then_inc(s_x[1], 16)
            sp.dma_start(rope[:].rearrange("p t c r -> p (t c r)"), io["tables"][:, T_ROPE:T_W]).then_inc(s_rope, 16)
            for c in range(SLOTS, NCH):
                load_chunk(c)

            def reg(v):
                return v if isinstance(v, int) else sp.snap(v)

            def load_slab(s, slot):
                before = NCH if isinstance(s, int) and s < 2 else reg(s + NCH - 1)
                src = w_in[:, :, bass.ds(reg(s * (2 * P)), 2 * P)]
                sp.wait_ge(s_whi, before)
                sp.wait_ge(s_wlo, before)
                sp.dma_start(raw_slab(slot), src).then_inc(s_slab[slot], 16)

            load_slab(0, 0)
            load_slab(1, 1)

            def tile(t, par, i):
                this, after = reg(t), reg(t + 1)
                row_at = reg((t - 1) * (P * ROW))
                sp.wait_ge(s_h, this)
                sp.dma_start(xin[:, 1 - par], x_tiles[bass.ds(after, 1)].rearrange("o p d -> (o p) d")).then_inc(
                    s_x[1 - par], 16)
                store(row_at, after, this)

            def store(row_at, moved, rotated):
                sp.wait_ge(s_z, moved)
                sp.wait_ge(s_rot, rotated)
                dst = rows_flat[bass.ds(row_at, P * ROW)].rearrange("(p n) -> p n", n=ROW)
                sp.dma_start(dst, row[:]).then_inc(s_row_out, 16)

            with sp.Fori(0, T // 2 - 1) as i:
                tile(i * 2 + 1, 1, i)
                tile(i * 2 + 2, 0, i)
            sp.dma_start(convrows[:], io["gdn_conv_w"].rearrange("o k (c p) -> (o k c) p", p=P)).then_inc(s_conv_rows, 16)
            for t in range(T - 2, T):
                store(t * P * ROW, t + 2, t + 1)

            def slab(s, par, i, last):
                if not isinstance(s, int):
                    load_slab(s + 2, par)
                for c in range(2):
                    tile_c, done = reg(s * 2 + c), reg(s * 2 + c + 1)
                    sp.wait_ge(s_silu, done)
                    dst = io["qkv"][:, :, bass.ds(tile_c, 1), :].rearrange("t p o s -> p (t o) s")
                    sp.dma_start(dst, conv[:, c].rearrange("p (t s) -> p t s", t=T)).then_inc(s_qkv_out[c], 16)

            slabs(sp, slab)
            sp.wait_ge(s_row_out, 16 * T)
            for q in s_qkv_out:
                sp.wait_ge(q, 16 * (A_TILES // 2 + 1))

        @block.gpsimd
        def _(pool):
            pool.memset(power[:], -0.5).then_inc(s_power, 1)
            pool.wait_ge(s_power, 1)

            def rstd(t, par):
                pool.wait_ge(s_ms, t + 1)
                pool.tensor_tensor(stat[:, par, 2:3], stat[:, par, 1:2], power[:], ALU.pow).then_inc(s_rstd, 1)

            def tile(t, par, i):
                if not (isinstance(t, int) and t == T - 1):
                    rstd(t + 1, 1 - par)
                pool.wait_ge(s_hi, 2 * (t + 1))
                pool.wait_ge(s_lo, 2 * (t + 1))
                pool.tensor_copy(h_hi[:, :, bass.ds(t * P, P)], tile_hi[:, par].bitcast(F32)).then_inc(s_big, 1)
                pool.tensor_copy(h_lo[:, :, bass.ds(t * P, P)], tile_lo[:, par].bitcast(F32)).then_inc(s_big, 1)

            rstd(0, 0)
            tiles(pool, tile)

        @block.scalar
        def _(act):
            def front(t, par, load):
                square(t, par, load)
                keep_hi(t, par)

            def square(t, par, load):
                act.wait_ge(s_x[par], 16 * load)
                act.activation(junk[:], xin[:, par], ACT.Square, accum_out=stat[:, par, 0:1]).then_inc(s_sq, 1)

            def keep_hi(t, par):
                if not (isinstance(t, int) and t < 2):
                    act.wait_ge(s_mm, 3 * (t - 1))
                    act.wait_ge(s_big, 2 * (t - 1))
                for b in range(2):
                    act.wait_ge(s_tr, 2 * t + b + 1)
                    act.copy(tile_hi[:, par, 4 * b:4 * b + 4], ps_t[:, b].rearrange("p (k s) -> p k s", k=4)).then_inc(s_hi, 1)

            def split(s, par, loads):
                act.wait_ge(s_slab[par], 16 * loads)
                act.copy(slab_w(par, 0), raw_slab(par)).then_inc(s_whi, 1)

            def tile(t, par, i):
                if not (isinstance(t, int) and t in (0, T - 1)):
                    front(t + 1, 1 - par, i + 2)
                act.wait_ge(s_mm, 3 * t + 1)
                act.wait_ge(s_row_out, 16 * t)
                act.activation(row[:, 0:HALF], ps_g[:, 3 * par], ACT.Silu).then_inc(s_z, 1)
                if isinstance(t, int) and t == T - 1:
                    split(0, 0, 1)
                act.wait_ge(s_mm, 3 * t + 3)
                act.copy(row[:, 2 * HALF:ROW], ps_g[:, 3 * par + 2, 0:GROUPS[2][1]]).then_inc(s_last, 1)

            front(0, 0, 1)
            for c in range(NCH):
                g, k0, nk = chunks[c]
                act.wait_ge(s_raw[c % SLOTS], raw_count(c))
                act.copy(group_w(g, 0)[:, k0:k0 + nk], raw_chunk(c)).then_inc(s_whi, 1)
                if c == ready[0] - 1:
                    square(1, 1, 1)
                if c == ready[1] - 1:
                    keep_hi(1, 1)
            tiles(act, tile)

            def slab(s, par, i, last):
                if not last:
                    act.wait_ge(s_pair, 2 * s + 2)
                    split(s + 1, 1 - par, i + 1 + par)
                for c in range(2):
                    act.wait_ge(s_pair, 2 * s + c + 3)
                    act.wait_ge(s_qkv_out[c], 16 * s + 16)
                    act.activation(conv[:, c], ps_g[:, 2 * c:2 * c + 2].rearrange("p b n -> p (b n)"), ACT.Identity,
                                   scale=taps[:, bass.ds(2 * s + (c + (GTAPS - 1) * A_TILES), 1)]).then_inc(s_first, 1)
                for c in range(2):
                    act.wait_ge(s_conv, 2 * s + c + 3)
                    act.activation(conv[:, c], conv[:, c], ACT.Silu).then_inc(s_silu, 1)

            act.wait_ge(s_taps, 1)
            slabs(act, slab)

        @block.vector
        def _(dve):
            dve.sem_inc(s_conv, 2)
            for q in (s_z, s_mid, s_last):
                dve.sem_inc(q, 1)
            dve.wait_ge(s_gain, 16)

            def front(t, par):
                norm(t, par)
                keep_lo(t, par)

            def norm(t, par):
                st = stat[:, par]
                dve.wait_ge(s_sq, t + 1)
                dve.tensor_scalar(st[:, 1:2], st[:, 0:1], 1.0 / D, EPS, ALU.mult, ALU.add).then_inc(s_ms, 1)
                dve.wait_ge(s_rstd, t + 1)
                if not (isinstance(t, int) and t == 0):
                    dve.wait_ge(s_tr, 2 * t)
                dve.scalar_tensor_tensor(h[:], xin[:, par], st[:, 2:3], gain[:], ALU.mult, ALU.mult).then_inc(s_h, 1)

            def keep_lo(t, par):
                for b in range(2):
                    dve.wait_ge(s_hi, 2 * t + b + 1)
                    k = slice(4 * b, 4 * b + 4)
                    dve.tensor_tensor(tile_lo[:, par, k], ps_t[:, b].rearrange("p (k s) -> p k s", k=4),
                                      tile_hi[:, par, k].bitcast(F32), ALU.subtract).then_inc(s_lo, 1)

            heads = row[:, Q0:V0].rearrange("p (h d) -> p h d", d=HD)
            x1, x2 = heads[:, :, 0:ROT // 2], heads[:, :, ROT // 2:ROT]

            def split(s, par):
                dve.wait_ge(s_whi, s + NCH + 1)
                dve.tensor_tensor(slab_w(par, 1), raw_slab(par), slab_w(par, 0).bitcast(F32), ALU.subtract).then_inc(s_wlo, 1)

            def tile(t, par, i):
                if not (isinstance(t, int) and t in (0, T - 1)):
                    front(t + 1, 1 - par)
                dve.wait_ge(s_mm, 3 * t + 2)
                dve.wait_ge(s_row_out, 16 * t)
                dve.tensor_copy(row[:, HALF:2 * HALF], ps_g[:, 3 * par + 1]).then_inc(s_mid, 1)
                if isinstance(t, int) and t == T - 1:
                    split(0, 0)
                dve.wait_ge(s_mid, t + 2)
                dve.wait_ge(s_last, t + 2)
                cos = rope[:, bass.ds(t, 1), 0, :].broadcast_to([P, QH + KVH, ROT // 2])
                sin = rope[:, bass.ds(t, 1), 1, :].broadcast_to([P, QH + KVH, ROT // 2])
                for n, (a, b) in enumerate([(x1, cos), (x2, sin), (x2, cos), (x1, sin)]):
                    dve.tensor_tensor(rot[:, n], a, b, ALU.mult).then_inc(s_rot4, 1)
                dve.wait_ge(s_rot4, 4 * (t + 1))
                dve.tensor_tensor(x1, rot[:, 0], rot[:, 1], ALU.subtract)
                dve.tensor_tensor(x2, rot[:, 2], rot[:, 3], ALU.add).then_inc(s_rot, 1)

            front(0, 0)
            for c in range(NCH):
                g, k0, nk = chunks[c]
                dve.wait_ge(s_whi, c + 1)
                dve.tensor_tensor(group_w(g, 1)[:, k0:k0 + nk], raw_chunk(c),
                                  group_w(g, 0)[:, k0:k0 + nk].bitcast(F32), ALU.subtract).then_inc(s_wlo, 1)
                if c == ready[0] - 1:
                    norm(1, 1)
                if c == ready[1] - 1:
                    keep_lo(1, 1)
            dve.wait_ge(s_rope, 16)
            tiles(dve, tile)

            def slab(s, par, i, last):
                if not last:
                    split(s + 1, 1 - par)
                for c in range(2):
                    src = ps_g[:, 2 * c:2 * c + 2].rearrange("p b n -> p (b n)")
                    dve.wait_ge(s_first, 2 * s + c + 1)
                    for k in range(1, GTAPS):
                        op = dve.scalar_tensor_tensor(
                            conv[:, c, k:S], src[:, 0:S - k], taps[:, bass.ds(2 * s + (c + (GTAPS - 1 - k) * A_TILES), 1)],
                            conv[:, c, k:S], ALU.mult, ALU.add)
                        if k < GTAPS - 1:
                            op.then_inc(s_tap, 1)
                            dve.wait_ge(s_tap, (2 * s + c) * (GTAPS - 2) + k)
                        else:
                            op.then_inc(s_conv, 1)

            dve.wait_ge(s_taps_ps, 1)
            dve.tensor_copy(taps[:], ps_t[:, 0, 0:GTAPS * A_TILES]).then_inc(s_taps, 1)
            slabs(dve, slab)

        @block.tensor
        def _(pe):
            pe.sem_inc(s_pair, 2)
            pe.wait_ge(s_const, 16)

            def front(t, par):
                pe.wait_ge(s_h, t + 1)
                for b in range(2):
                    if not (isinstance(t, int) and t == 0):
                        pe.wait_ge(s_lo, 2 * t - 1 + b)
                    for k in range(4):
                        last = pe.transpose(ps_t[:, b, k * P:(k + 1) * P], h[:, (4 * b + k) * P:(4 * b + k + 1) * P], ident[:])
                    last.then_inc(s_tr, 1)

            def tile(t, par, i):
                pe.wait_ge(s_lo, 2 * (t + 1))
                for g, (c0, n) in enumerate(GROUPS):
                    pe.wait_ge(s_wlo, ready[g])
                    if not (isinstance(t, int) and t == 0):
                        pe.wait_ge((s_z, s_mid, s_last)[g], t)
                    bank = ps_g[:, 3 * par + g, 0:n]
                    for k in range(KD):
                        pe.matmul(bank, tile_hi[:, par, k], group_w(g, 0)[:, k], start=(k == 0), stop=False)
                        pe.matmul(bank, tile_hi[:, par, k], group_w(g, 1)[:, k], start=False, stop=False)
                        last = pe.matmul(bank, tile_lo[:, par, k], group_w(g, 0)[:, k], start=False, stop=(k == KD - 1))
                    last.then_inc(s_mm, 1)
                    if g == 0 and not (isinstance(t, int) and t == T - 1):
                        front(t + 1, 1 - par)

            front(0, 0)
            tiles(pe, tile)

            def slab(s, par, i, last):
                pe.wait_ge(s_wlo, s + NCH + 1)
                for c in range(2):
                    pe.wait_ge(s_conv, 2 * s + c + 1)
                    for half in range(2):
                        bank = ps_g[:, 2 * c + half]
                        cols = slice(half * HALF, (half + 1) * HALF)
                        for k in range(KD):
                            w_hi = slab_w(par, 0)[:, k, c * P:(c + 1) * P]
                            w_lo = slab_w(par, 1)[:, k, c * P:(c + 1) * P]
                            pe.matmul(bank, w_hi, h_hi[:, k, cols], start=(k == 0), stop=False)
                            pe.matmul(bank, w_hi, h_lo[:, k, cols], start=False, stop=False)
                            op = pe.matmul(bank, w_lo, h_hi[:, k, cols], start=False, stop=(k == KD - 1))
                    op.then_inc(s_pair, 1)

            pe.wait_ge(s_big, 2 * T)
            pe.wait_ge(s_conv_rows, 16)
            n = GTAPS * A_TILES
            pe.transpose(ps_t[:, 0, 0:n], convrows[:], ident[0:n, 0:n]).then_inc(s_taps_ps, 1)
            pe.wait_ge(s_z, T + 1)
            pe.wait_ge(s_mid, T)
            pe.wait_ge(s_last, T)
            slabs(pe, slab)


class Tally:

    def __init__(self, nc, ctx, name, per=1, credit=0):
        self.sem, self.per, self.credit = ctx.enter_context(nc.semaphore(name)), per, credit

    def at(self, t, k):
        return t * self.per + (k + self.credit)


def after(eng, tally, t, k=None):
    value = tally.at(t, tally.per if k is None else k)
    if not isinstance(value, int) or value > tally.credit:
        eng.wait_ge(tally.sem, value)


def mix_block(nc, io, h_t, split, stage, s_stage):
    with ExitStack() as ctx:
        sb = lambda name, shape, dt=F32: ctx.enter_context(nc.sbuf_tensor("m_" + name, shape, dt))
        sem = lambda name: ctx.enter_context(nc.semaphore("m_" + name))
        tally = lambda name, per=1, credit=0: Tally(nc, ctx, "m_" + name, per, credit)
        H = GH
        NG = 7
        I_G, I_CUM, I_BETA, I_NEG, I_OUT, I_IN, I_LAST = range(NG)

        w_hi, w_lo = split[:, 0], split[:, 1]
        left, right = stage[:, 0], stage[:, 1]
        qkv = left[:, 0:A_TILES * P].rearrange("p (c s) -> p c s", s=P)
        zw = left[:, A_TILES * P:(A_TILES + H) * P].rearrange("p (h c) -> p h c", c=P)
        row = right[:, 0:ROW]
        o = right[:, ROW:ROW + H * P].rearrange("p (h c) -> p h c", c=P)
        gates = sb("gates", [P, T, NG, H])
        gs = sb("gs", [P, 2, NG, H])
        ab = sb("ab", [P, T, 2, H])
        g_tmp = right[:, ROW + H * P:ROW + H * P + 6 * T * H].rearrange("p (n t h) -> p n t h", n=6, h=H)
        a_log = sb("a_log", [P, H])
        dt_bias = sb("dt_bias", [P, H])
        a_exp = sb("a_exp", [P, H])
        power = sb("power", [P, 2 * H])
        squares = sb("squares", [P, 2 * H, P])
        g_tri = sb("g_tri", [P, H, P])
        norm2 = sb("norm2", [P, 2, 2, 2 * H])
        k_tok = sb("k_tok", [P, H, P])
        k_t = sb("k_t", [P, H, P])
        q_t = sb("q_t", [P, H, P])
        k_out = sb("k_out", [P, H, P])
        b_v = sb("b_v", [P, H, P])
        dec_t = sb("dec_t", [P, H, P])
        dec = sb("dec", [P, H, P])
        low = sb("low", [P, H, P])
        low_t = sb("low_t", [P, H, P])
        qk_t = sb("qk_t", [P, H, P])
        inv = sb("inv", [P, H, P])
        inv_t = sb("inv_t", [P, H, P])
        off = sb("off", [P, H, P])
        beta_low = squares[:, 0:H]
        state = sb("state", [P, H, P])
        resid = sb("resid", [P, H, P])
        v_new = sb("v_new", [P, H, P])
        o_stat = sb("o_stat", [P, 5, H])
        norm_w = sb("norm_w", [P, P])
        junk = sb("junk", [P, D], BF16)
        junk_o = sb("junk_o", [P, H, P], BF16)
        q_b = sb("q_b", [P, QH // 2, P])
        k_dup = sb("k_dup", [P, KVH, 2, HD])
        k_b = sb("k_b", [P, KVH, 2, P])
        v_b = sb("v_b", [P, 2, KVH * HD])
        scores = sb("scores", [P, 4, 2, P])
        p_t = sb("p_t", [P, 4, 2, P])
        masks = sb("masks", [P, 3, 2, P])
        sinks = sb("sinks", [P, QH])
        c_stat = sb("c_stat", [P, 7, QH])
        mix = sb("mix", [P, D])
        mix_hi = sb("mix_hi", [P, KD, P], F32R)
        mix_lo = sb("mix_lo", [P, KD, P], F32R)
        x = sb("x", [P, D])
        y = sb("y", [P, D])
        g_post = sb("g_post", [P, D])
        g_ffn = sb("g_ffn", [P, D])
        d_stat = sb("d_stat", [P, 6])
        table = sb("table", [P, T_ROPE])
        tab = lambda at: table[:, at:at + P]
        ident, tri, strict, ones = tab(T_ID), tab(T_TRI), tab(T_STRICT), tab(T_ONES)
        over_heads = lambda m: m.unsqueeze(1).broadcast_to([P, H, P])
        over_cols = lambda s: s.unsqueeze(2).broadcast_to([P, H, P])
        flat = lambda m: m.rearrange("p a b -> p (a b)")

        ps = {n: ctx.enter_context(nc.psum_tensor("m_ps_" + n, [P, HALF], F32)) for n in ("a0", "a1", "a2", "b0", "b1", "c0")}
        ps_d = ctx.enter_context(nc.psum_tensor("m_ps_d", [P, 2, HALF], F32))
        bank = lambda n: ps[n][:].rearrange("p (h c) -> p h c", c=P)

        fills = {"a0": 9, "a1": 4, "a2": 7, "b0": 3, "b1": 2, "c0": 12, "d0": 2, "d1": 2}
        frees = {"a0": 8, "a1": 3, "a2": 7, "b0": 2, "c0": 10, "d0": 2, "d1": 2}
        full = {n: tally(n + "_full", k, k if n[0] == "d" else 0) for n, k in fills.items()}
        free = {n: tally(n + "_free", k, k if n[0] == "d" else 0) for n, k in frees.items()}

        s_load, s_tab, s_ab, s_w = sem("load"), sem("tab"), sem("ab"), sem("w")
        s_whi, s_wlo, s_zero, s_gate = sem("whi"), sem("wlo"), sem("zero"), sem("gate")
        s_gv, s_ga, s_ps_g = sem("gate_vector"), sem("gate_scalar"), sem("gate_sums")
        s_order, s_hhi = sem("order"), sem("hhi")
        qkv_in, row_in = tally("qkv_in", 16), tally("row_in", 16)
        x_in, x_out = tally("x_in", 16, 16), tally("x_out", 16, 16)
        gs_set, tri_set, squared = tally("gs_set"), tally("tri_set"), tally("squared")
        n2, rn, khat, qt_set, kout_set = (tally(n) for n in ("n2", "rn", "khat", "qt_set", "kout_set"))
        clipped, dec_exp, dec_masked = tally("clipped", 2), tally("dec_exp", 2), tally("dec_masked", 2)
        beta_set, init, init_t = tally("beta_set"), tally("init", 2), tally("init_t", 2)
        st_set, o1_set, o_set = tally("st_set"), tally("o1_set"), tally("o_set")
        o_sq, o_n, o_ms, o_rstd, zw_set, mixa = tally("o_sq"), tally("o_n", 2), tally("o_ms"), tally("o_rstd", 2), tally("zw_set"), tally("mixa")
        kdup_set, vb_set = tally("kdup_set"), tally("vb_set")
        cmax, cneg, csub = tally("cmax", 2), tally("cneg", 2), tally("csub", 2)
        cexp, csink, cden, crec, mixb = tally("cexp", 2), tally("csink", 2), tally("cden", 2), tally("crec", 2), tally("mixb", 2)
        dhi, dsq, dms, drstd = (tally(n, 2, 2) for n in ("dhi", "dsq", "dms", "drstd"))
        dx, dh = (tally(n, 1, 1) for n in ("dx", "dh"))
        e_full, e_free = (tally(n, 2, 2) for n in ("e_full", "e_free"))

        LV = len(LEVELS) - 1

        def halves(m, n, which):
            s = LEVELS[n]
            return m.rearrange("p h (g two s) -> p h g two s", two=2, s=s)[:, :, :, which]

        def half_cols(m, h, n, which):
            s = LEVELS[n]
            return m[:, h].rearrange("p (g two s) -> p g two s", two=2, s=s)[:, :, which]

        def ps_half(n, which):
            s = LEVELS[n]
            return ps["a2"][:, 256 * which:256 * which + 256].rearrange("p (h g s) -> p h g s", h=H, s=s)

        w_rows = io["w_out"].rearrange("o (k p) n -> p (o k) n", p=P)
        qkv_flat = io["qkv"].rearrange("t p c s -> (t p c s)")
        rows_flat = io["rows"].rearrange("t p n -> (t p n)")
        x_flat = io["x"].rearrange("o s d -> (o s d)")
        res_flat = io["res"].rearrange("t p d -> (t p d)")

        def carry(eng):
            eng.sem_inc(s_order, 1)

        block = ctx.enter_context(nc.Block("mix"))

        def steps(eng, step):
            step(0, 0, True, True, False, False)
            step(1, 1, True, True, True, False)
            with eng.Fori(1, T // 2 - 1) as i:
                step(i * 2, 0, True, True, True, True)
                step(i * 2 + 1, 1, True, True, True, True)
            step(T - 2, 0, False, True, True, True)
            step(T - 1, 1, False, False, True, True)

        @block.sync
        def _(sp):
            def reg(v):
                return v if isinstance(v, int) else sp.snap(v)

            def ready(*needs):
                values = [(s, s.at(t, k)) for s, t, k in needs]
                for s, v in [(s, reg(v)) for s, v in values if not isinstance(v, int) or v > s.credit]:
                    sp.wait_ge(s.sem, v)
                    carry(sp)

            def load_qkv(u):
                at = reg(u * (P * A_TILES * P))
                ready((full["a1"], u - 1, 2), (qt_set, u - 1, 1), (squared, u - 1, 1))
                sp.dma_start(flat(qkv), qkv_flat[bass.ds(at, P * A_TILES * P)].rearrange("(p n) -> p n", p=P)).then_inc(
                    qkv_in.sem, 16)

            def load_row(t):
                at = reg(t * (P * ROW))
                ready((full["c0"], t - 1, 1), (zw_set, t - 1, 1), (kdup_set, t - 1, 1), (vb_set, t - 1, 1))
                sp.dma_start(row, rows_flat[bass.ds(at, P * ROW)].rearrange("(p n) -> p n", p=P)).then_inc(row_in.sem, 16)

            def load_x(v):
                at = reg(v * (P * D))
                ready((x_out, v - 1, 16), (dh, v - 1, 1))
                sp.dma_start(x[:], x_flat[bass.ds(at, P * D)].rearrange("(p n) -> p n", p=P)).then_inc(x_in.sem, 16)

            def store_x(v):
                at = reg(v * (P * D))
                ready((dx, v, 1))
                sp.dma_start(res_flat[bass.ds(at, P * D)].rearrange("(p n) -> p n", p=P), x[:]).then_inc(x_out.sem, 16)

            sp.sem_inc(x_in.sem, 16)
            sp.sem_inc(x_out.sem, 16)
            sp.dma_start(ab[:].rearrange("p t c h -> p t (c h)"), io["rows"][:, :, AB0:Q0].rearrange("t p n -> p t n")).then_inc(s_ab, 16)
            sp.dma_start(a_log[:], io["gdn_A_log"][0:1, :].broadcast_to([P, H])).then_inc(s_ab, 16)
            sp.dma_start(dt_bias[:], io["gdn_dt_bias"][0:1, :].broadcast_to([P, H])).then_inc(s_ab, 16)
            load_qkv(0)
            sp.dma_start(table[:], io["tables"][:, 0:T_ROPE]).then_inc(s_tab, 16)
            for m, (a, b) in enumerate([(T_CUR, T_PREV), (T_PREV, T_CUR)]):
                sp.dma_start(masks[:, m, 0], io["tables"][:, a:a + P]).then_inc(s_load, 16)
                sp.dma_start(masks[:, m, 1], io["tables"][:, b:b + P]).then_inc(s_load, 16)
            sp.dma_start(masks[:, 2, 0], io["tables"][:, T_CUR:T_CUR + P]).then_inc(s_load, 16)
            sp.dma_start(norm_w[:], io["gdn_norm_w"][0:1, :].broadcast_to([P, P])).then_inc(s_load, 16)
            sp.dma_start(sinks[:], io["attn_sinks"][0:1, :].broadcast_to([P, QH])).then_inc(s_load, 16)
            load_row(0)
            sp.dma_start(h_t[:], w_rows).then_inc(s_w, 16)
            sp.dma_start(g_post[:], io["g_post_mix"][0:1, :].broadcast_to([P, D])).then_inc(s_load, 16)
            sp.dma_start(g_ffn[:], io["g_pre_ffn"][0:1, :].broadcast_to([P, D])).then_inc(s_load, 16)

            load_qkv(1)

            def step(t, par, n, a, d, e):
                if d:
                    load_row(t)
                if n:
                    load_qkv(t + 2)
                if e:
                    store_x(t - 2)
                if d:
                    load_x(t - 1)

            steps(sp, step)
            store_x(T - 2)
            load_x(T - 1)
            last = T - 1
            ready((full["a1"], last, 2), (qt_set, last, 1), (squared, last, 1), (full["c0"], last, 1), (kdup_set, last, 1),
                  (vb_set, last, 1), (zw_set, last, 1), (o_sq, last, 1), (mixa, last, 1))
            for kind in range(2):
                src = io["w_up"].rearrange("o (k p) n -> p (o k) n", p=P)[:, :, kind * DFF:kind * DFF + 2 * P]
                sp.dma_start(stage[:, kind].rearrange("p (k n) -> p k n", k=KD), src).then_inc(s_stage[kind], 16)
            store_x(T - 1)
            sp.wait_ge(x_out.sem, 16 * (T + 1))

        LOADS = 16 * 9

        @block.gpsimd
        def _(pool):
            pool.memset(power[:], -0.5).then_inc(s_zero, 1)
            pool.memset(state[:], 0.0).then_inc(s_zero, 1)
            pool.memset(k_b[:], 0.0).then_inc(s_zero, 1)
            pool.memset(v_b[:], 0.0).then_inc(s_zero, 1)
            pool.memset(masks[:, 2, 1], NEG).then_inc(s_zero, 1)
            pool.wait_ge(s_zero, 5)
            pool.wait_ge(s_tab, 16)
            pool.wait_ge(s_gate, 1)

            def a_gates(u, par):
                after(pool, st_set, u - 2)
                after(pool, o1_set, u - 2)
                carry(pool)
                pool.tensor_copy(gs[:, par].rearrange("p n h -> p (n h)"),
                                 gates[:, bass.ds(u, 1)].rearrange("p t n h -> p (t n h)")).then_inc(gs_set.sem, 1)
                after(pool, gs_set, u)
                after(pool, full["a1"], u - 1, 3)
                pool.tensor_tensor(g_tri[:], over_heads(tri), over_cols(gs[:, par, I_G]), ALU.mult).then_inc(tri_set.sem, 1)

            def a_rnorm(u, par):
                after(pool, n2, u)
                pool.tensor_tensor(norm2[:, par, 1], norm2[:, par, 0], power[:], ALU.pow).then_inc(rn.sem, 1)

            def a_kout(u, par):
                after(pool, khat, u)
                after(pool, full["b0"], u - 1, 3)
                pool.tensor_tensor(k_out[:], k_tok[:], over_cols(gs[:, par, I_OUT]), ALU.mult).then_inc(kout_set.sem, 1)

            def a_beta(u, par):
                after(pool, gs_set, u)
                after(pool, n2, u)
                pool.tensor_tensor(beta_low, over_heads(strict), over_cols(gs[:, par, I_BETA]), ALU.mult).then_inc(beta_set.sem, 1)

            def a_masks(u):
                after(pool, dec_exp, u, 1)
                after(pool, beta_set, u)
                pool.tensor_tensor(dec[:], dec[:], beta_low, ALU.mult).then_inc(dec_masked.sem, 1)
                after(pool, dec_exp, u, 2)
                pool.tensor_tensor(dec_t[:], dec_t[:], over_heads(tri), ALU.mult).then_inc(dec_masked.sem, 1)

            def a_init_t(u):
                after(pool, free["a1"], u, 3)
                after(pool, full["b0"], u - 1, 2)
                pool.tensor_tensor(inv_t[:], low_t[:], over_heads(tab(T_LEVEL0T)), ALU.mult).then_inc(init_t.sem, 1)
                after(pool, init_t, u, 1)
                pool.tensor_tensor(inv_t[:], inv_t[:], over_heads(ident), ALU.add).then_inc(init_t.sem, 1)

            def c_kdup(t):
                after(pool, row_in, t)
                after(pool, full["c0"], t - 1, 2)
                carry(pool)
                pool.tensor_copy(k_dup[:], row[:, K0:V0].rearrange("p (k d) -> p k d", d=HD).unsqueeze(2).broadcast_to(
                    [P, KVH, 2, HD])).then_inc(kdup_set.sem, 1)

            def c_vb(t, par):
                after(pool, full["c0"], t - 1, 12)
                carry(pool)
                pool.tensor_copy(v_b[:, par], row[:, V0:ROW]).then_inc(vb_set.sem, 1)

            def b_zw(t):
                after(pool, mixa, t - 1)
                pool.tensor_tensor(zw, row[:, 0:H * P].rearrange("p (h c) -> p h c", c=P), over_heads(norm_w[:]),
                                   ALU.mult).then_inc(zw_set.sem, 1)

            def b_scale(t, par):
                rq = norm2[:, par, 1, 0:H]
                after(pool, rn, t)
                pool.tensor_tensor(o_stat[:, 1], rq, rq, ALU.mult).then_inc(o_n.sem, 1)
                after(pool, o_sq, t)
                after(pool, o_n, t, 1)
                pool.tensor_tensor(o_stat[:, 2], o_stat[:, 1], o_stat[:, 0], ALU.mult).then_inc(o_n.sem, 1)

            def b_rstd(t, par):
                after(pool, o_ms, t)
                pool.tensor_tensor(o_stat[:, 4], o_stat[:, 3], power[:, 0:H], ALU.pow).then_inc(o_rstd.sem, 1)
                after(pool, o_rstd, t, 1)
                after(pool, mixa, t - 1)
                pool.tensor_tensor(o_stat[:, 4], o_stat[:, 4], norm2[:, par, 1, 0:H], ALU.mult).then_inc(o_rstd.sem, 1)

            def d_rstd(v, n):
                after(pool, dms, v, n)
                pool.tensor_tensor(d_stat[:, 3 * n - 1:3 * n], d_stat[:, 3 * n - 2:3 * n - 1], power[:, 0:1], ALU.pow).then_inc(drstd.sem, 1)

            def d_res(v):
                after(pool, free["d1"], v, 2)
                after(pool, x_in, v)
                pool.tensor_tensor(x[:], x[:], y[:], ALU.add).then_inc(dx.sem, 1)

            a_gates(0, 0)
            a_rnorm(0, 0)
            a_beta(0, 0)
            a_kout(0, 0)
            a_masks(0)
            a_init_t(0)
            a_rnorm(1, 1)
            a_gates(1, 1)
            pool.wait_ge(s_load, LOADS)

            def step(t, par, n, a, d, e):
                if a:
                    a_beta(t + 1, 1 - par)
                if e:
                    d_rstd(t - 2, 1)
                c_kdup(t)
                b_zw(t)
                if a:
                    a_kout(t + 1, 1 - par)
                    a_masks(t + 1)
                b_scale(t, par)
                b_rstd(t, par)
                if a:
                    a_init_t(t + 1)
                if e:
                    d_res(t - 2)
                    d_rstd(t - 2, 2)
                c_vb(t, par)
                if n:
                    a_rnorm(t + 2, par)
                    a_gates(t + 2, par)

            steps(pool, step)
            for v in (T - 2, T - 1):
                d_rstd(v, 1)
                d_res(v)
                d_rstd(v, 2)

        @block.scalar
        def _(act):
            act.wait_ge(s_ab, 48)
            act.activation(a_exp[:], a_log[:], ACT.Exp).then_inc(s_ga, 1)
            act.activation(g_tmp[:, 3], ab[:, :, 1], ACT.Exp, scale=-1.0).then_inc(s_ga, 1)
            act.wait_ge(s_gv, 2)
            act.activation(g_tmp[:, 2], g_tmp[:, 1], ACT.Exp, scale=-1.0).then_inc(s_ga, 1)
            act.wait_ge(s_gv, 3)
            act.activation(g_tmp[:, 2], g_tmp[:, 2], ACT.Ln).then_inc(s_ga, 1)
            act.wait_ge(s_ps_g, 1)
            sums = ps["a0"][:, 0:2 * T * H].rearrange("p (c t h) -> p c t h", c=2, h=H)
            act.activation(gates[:, :, I_IN], sums[:, 0], ACT.Exp).then_inc(s_ga, 1)
            act.activation(gates[:, :, I_LAST], sums[:, 1], ACT.Exp).then_inc(s_ga, 1)
            act.wait_ge(s_gv, 9)
            act.activation(gates[:, :, I_OUT], g_tmp[:, 4], ACT.Exp).then_inc(s_ga, 1)

            def a_square(u):
                after(act, qkv_in, u)
                after(act, dec_masked, u - 1, 1)
                act.activation(squares[:], qkv[:, 0:2 * H], ACT.Square).then_inc(squared.sem, 1)

            def a_q(u):
                after(act, full["b1"], u - 1, 1)
                act.copy(q_t[:], qkv[:, 0:H]).then_inc(qt_set.sem, 1)

            def a_kt(u):
                after(act, full["a0"], u, 2)
                after(act, full["b0"], u - 1, 1)
                act.copy(k_t[:], bank("a0")).then_inc(free["a0"].sem, 1)

            def a_exp_(u):
                after(act, clipped, u, 2)
                act.activation(dec[:], dec[:], ACT.Exp, scale=-1.0).then_inc(dec_exp.sem, 1)
                act.activation(dec_t[:], dec_t[:], ACT.Exp).then_inc(dec_exp.sem, 1)

            def a_lowt(u):
                after(act, full["a1"], u, 4)
                act.copy(low_t[:], bank("a1")).then_inc(free["a1"].sem, 1)

            def b_v_new(t):
                after(act, full["b0"], t, 2)
                after(act, full["b1"], t - 1, 2)
                act.copy(v_new[:], bank("b0")).then_inc(free["b0"].sem, 1)

            def b_square(t):
                after(act, o_set, t)
                after(act, o_ms, t - 1)
                for h in range(H):
                    op = act.activation(junk_o[:, h], o[:, h], ACT.Square, accum_out=o_stat[:, 0, h:h + 1])
                op.then_inc(o_sq.sem, 1)

            def c_qb(t):
                after(act, full["c0"], t, 1)
                act.copy(q_b[:], bank("c0")).then_inc(free["c0"].sem, 1)

            def c_kb(t, par):
                after(act, full["c0"], t, 2)
                act.copy(k_b[:, :, par], bank("c0")[:, 0:KVH]).then_inc(free["c0"].sem, 1)

            def c_exp(t, r):
                after(act, cneg, t, r + 1)
                after(act, mixb, t - 1, r + 1)
                for h in range(4):
                    op = act.activation(scores[:, h].rearrange("p a b -> p (a b)"), scores[:, h].rearrange("p a b -> p (a b)"), ACT.Exp,
                                        bias=c_stat[:, 2, 4 * r + h:4 * r + h + 1], accum_out=c_stat[:, 3, 4 * r + h:4 * r + h + 1])
                op.then_inc(cexp.sem, 1)
                after(act, csub, t, r + 1)
                act.activation(c_stat[:, 4, 4 * r:4 * r + 4], c_stat[:, 4, 4 * r:4 * r + 4], ACT.Exp).then_inc(csink.sem, 1)

            def c_pt(t, n):
                use = (5, 6, 10, 11)[n]
                after(act, full["c0"], t, use)
                act.copy(p_t[:, 2 * (n % 2):2 * (n % 2) + 2].rearrange("p h k c -> p (h k) c"), bank("c0")).then_inc(free["c0"].sem, 1)

            def d_hi(v):
                for b in range(2):
                    after(act, full[f"d{b}"], v, 1)
                    after(act, full["d1"], v - 1, 2)
                    act.copy(mix_hi[:, 4 * b:4 * b + 4], ps_d[:, b].rearrange("p (k c) -> p k c", c=P)).then_inc(dhi.sem, 1)

            def d_square(v, n):
                if n == 1:
                    after(act, full["d0"], v, 2)
                    after(act, full["d1"], v, 2)
                    src = flat(ps_d[:])
                else:
                    after(act, dx, v)
                    src = x[:]
                act.activation(junk[:], src, ACT.Square, accum_out=d_stat[:, 3 * n - 3:3 * n - 2]).then_inc(dsq.sem, 1)

            def d_out(v):
                act.wait_ge(s_wlo, KD)
                for b in range(2):
                    after(act, e_full, v, b + 1)
                    act.copy(h_t[:, 4 * b:4 * b + 4, bass.ds(v * P, P)], bank(f"b{b}")).then_inc(e_free.sem, 1)

            a_square(0)
            a_q(0)
            a_kt(0)
            a_exp_(0)
            a_lowt(0)
            act.wait_ge(s_w, 16)
            for k in range(KD):
                act.copy(w_hi[:, k], h_t[:, k]).then_inc(s_whi, 1)
            a_square(1)

            def step(t, par, n, a, d, e):
                if e:
                    d_square(t - 2, 1)
                b_v_new(t)
                if a:
                    a_q(t + 1)
                c_qb(t)
                if d:
                    d_hi(t - 1)
                if a:
                    a_kt(t + 1)
                c_kb(t, par)
                if a:
                    a_exp_(t + 1)
                b_square(t)
                if a:
                    a_lowt(t + 1)
                c_exp(t, 0)
                if e:
                    d_square(t - 2, 2)
                c_pt(t, 0)
                if n:
                    a_square(t + 2)
                c_pt(t, 1)
                c_exp(t, 1)
                if e:
                    d_out(t - 2)
                c_pt(t, 2)
                c_pt(t, 3)

            steps(act, step)
            d_square(T - 2, 1)
            d_square(T - 2, 2)
            d_out(T - 2)
            d_hi(T - 1)
            d_square(T - 1, 1)
            for k in range(KD):
                if k == KD // 2:
                    d_square(T - 1, 2)
                act.copy(w_hi[:, k, 0:S - P], h_t[:, k, 0:S - P]).then_inc(s_hhi, 1)
            for b in range(2):
                after(act, e_full, T - 1, b + 1)
                act.copy(w_hi[:, 4 * b:4 * b + 4, S - P:S], bank(f"b{b}")).then_inc(s_hhi, 1)

        @block.vector
        def _(dve):
            n_gv = [0]

            def gv(op):
                op.then_inc(s_gv, 1)
                n_gv[0] += 1
                dve.wait_ge(s_gv, n_gv[0])

            by_tile = lambda m: m.unsqueeze(1).broadcast_to([P, T, H])
            dve.wait_ge(s_ab, 48)
            gv(dve.tensor_tensor(g_tmp[:, 0], ab[:, :, 0], by_tile(dt_bias[:]), ALU.add))
            gv(dve.scalar_tensor_tensor(g_tmp[:, 1], g_tmp[:, 0], -1.0, g_tmp[:, 0], ALU.mult, ALU.max))
            dve.wait_ge(s_ga, 3)
            gv(dve.tensor_scalar(g_tmp[:, 2], g_tmp[:, 2], 1.0, None, ALU.add))
            gv(dve.tensor_scalar(g_tmp[:, 3], g_tmp[:, 3], 1.0, None, ALU.add))
            gv(dve.reciprocal(gates[:, :, I_BETA], g_tmp[:, 3]))
            dve.wait_ge(s_ga, 4)
            gv(dve.scalar_tensor_tensor(g_tmp[:, 5], g_tmp[:, 0], 0.0, g_tmp[:, 2], ALU.max, ALU.add))
            gv(dve.scalar_tensor_tensor(gates[:, :, I_G], g_tmp[:, 5], -1.0, by_tile(a_exp[:]), ALU.mult, ALU.mult))
            dve.wait_ge(s_ga, 6)
            sums = ps["a0"][:, 0:2 * T * H].rearrange("p (c t h) -> p c t h", c=2, h=H)
            gv(dve.tensor_copy(gates[:, :, I_CUM], sums[:, 0]))
            gv(dve.tensor_tensor(g_tmp[:, 4], sums[:, 1], gates[:, :, I_CUM], ALU.subtract))
            dve.wait_ge(s_ga, 7)
            dve.scalar_tensor_tensor(gates[:, :, I_NEG], gates[:, :, I_BETA], -1.0, gates[:, :, I_IN], ALU.mult, ALU.mult).then_inc(s_gate, 1)

            def a_bv(u, par):
                after(dve, full["a1"], u, 2)
                after(dve, gs_set, u)
                after(dve, free["b0"], u - 1, 1)
                dve.tensor_tensor(b_v[:], bank("a1"), over_cols(gs[:, par, I_BETA]), ALU.mult).then_inc(free["a1"].sem, 1)

            def a_n2(u, par):
                after(dve, full["a1"], u, 1)
                after(dve, o_rstd, u - 2)
                dve.tensor_scalar(norm2[:, par, 0], ps["a1"][:, 0:2 * H], EPS, None, ALU.add).then_inc(n2.sem, 1)

            def a_khat(u, par):
                after(dve, rn, u)
                after(dve, kout_set, u - 1)
                dve.tensor_tensor(k_tok[:], bank("a0"), over_cols(norm2[:, par, 1, H:2 * H]), ALU.mult).then_inc(khat.sem, 1)

            def a_diff(u, par):
                after(dve, full["a1"], u, 3)
                dve.tensor_tensor(dec[:], bank("a1"), over_cols(gs[:, par, I_CUM]), ALU.subtract).then_inc(free["a1"].sem, 1)
                after(dve, free["a1"], u, 2)
                dve.tensor_scalar(dec_t[:], dec[:], 0.0, None, ALU.min).then_inc(clipped.sem, 1)
                after(dve, clipped, u, 1)
                dve.tensor_scalar(dec[:], dec[:], 0.0, None, ALU.max).then_inc(clipped.sem, 1)

            def a_low(u):
                after(dve, dec_masked, u, 1)
                after(dve, full["a0"], u, 3)
                dve.tensor_tensor(low[:], bank("a0"), dec[:], ALU.mult).then_inc(free["a0"].sem, 1)

            def a_qk(u):
                after(dve, dec_masked, u, 2)
                after(dve, full["a2"], u, 1)
                after(dve, full["b1"], u - 1, 2)
                dve.tensor_tensor(qk_t[:], bank("a2"), dec_t[:], ALU.mult).then_inc(free["a2"].sem, 1)

            def a_init(u):
                after(dve, free["a0"], u, 2)
                dve.tensor_tensor(off[:], low[:], over_heads(tab(T_LEVEL)), ALU.mult).then_inc(init.sem, 1)
                after(dve, init, u, 1)
                dve.tensor_tensor(inv[:], off[:], over_heads(ident), ALU.add).then_inc(init.sem, 1)

            def a_off(u, n):
                after(dve, full["a0"], u, 3 + n)
                if n == 1:
                    after(dve, init, u, 2)
                dve.tensor_tensor(off[:], bank("a0"), over_heads(tab(T_LEVEL + n * P)), ALU.mult).then_inc(free["a0"].sem, 1)

            def a_inv(u, n):
                after(dve, full["a2"], u, 1 + n)
                if n < LV:
                    dve.tensor_tensor(halves(inv[:], n, 0), ps_half(n, 0), halves(inv[:], n, 0), ALU.add)
                dve.tensor_tensor(halves(inv_t[:], n, 1), ps_half(n, 1), halves(inv_t[:], n, 1), ALU.add).then_inc(free["a2"].sem, 1)

            def b_resid(t, par):
                after(dve, full["b0"], t, 1)
                for h in range(H):
                    op = dve.scalar_tensor_tensor(resid[:, h], bank("b0")[:, h], gs[:, par, I_NEG, h:h + 1], b_v[:, h], ALU.mult, ALU.add)
                op.then_inc(free["b0"].sem, 1)

            def b_state(t, par):
                after(dve, full["b0"], t, 3)
                after(dve, full["b1"], t, 1)
                for h in range(H):
                    op = dve.scalar_tensor_tensor(state[:, h], state[:, h], gs[:, par, I_LAST, h:h + 1], bank("b0")[:, h], ALU.mult, ALU.add)
                op.then_inc(st_set.sem, 1)

            def b_o1(t, par):
                after(dve, full["b1"], t, 1)
                dve.tensor_tensor(o, bank("b1"), over_cols(gs[:, par, I_IN]), ALU.mult).then_inc(o1_set.sem, 1)

            def b_o(t):
                after(dve, full["b1"], t, 2)
                after(dve, o1_set, t)
                dve.tensor_tensor(o, bank("b1"), o, ALU.add).then_inc(o_set.sem, 1)

            def b_ms(t):
                after(dve, o_n, t, 2)
                dve.tensor_scalar(o_stat[:, 3], o_stat[:, 2], 1.0 / P, EPS * DK, ALU.mult, ALU.add).then_inc(o_ms.sem, 1)

            def b_mix(t):
                after(dve, o_rstd, t, 2)
                after(dve, zw_set, t)
                after(dve, full["d1"], t - 1, 1)
                for h in range(H):
                    op = dve.scalar_tensor_tensor(mix[:, h * P:(h + 1) * P], o[:, h], o_stat[:, 4, h:h + 1], zw[:, h], ALU.mult, ALU.mult)
                op.then_inc(mixa.sem, 1)

            def c_scores(t, par, n):
                after(dve, full["c0"], t, (3, 4, 8, 9)[n])
                carry(dve)
                mask = masks[:, 2 if isinstance(t, int) and t == 0 else par].rearrange("p a b -> p (a b)")
                for h in range(2):
                    slot = n % 2 + 2 * h
                    op = dve.tensor_tensor_reduce(scores[:, slot].rearrange("p a b -> p (a b)"),
                                                  ps["c0"][:, 256 * h:256 * h + 256], mask, HD ** -0.5, -3e38, ALU.add, ALU.max,
                                                  c_stat[:, 0, 4 * (n // 2) + slot:4 * (n // 2) + slot + 1])
                op.then_inc(free["c0"].sem, 1)

            def c_max(t, r):
                q = slice(4 * r, 4 * r + 4)
                after(dve, free["c0"], t, (4, 8)[r])
                dve.tensor_tensor(c_stat[:, 1, q], c_stat[:, 0, q], sinks[:, q], ALU.max).then_inc(cmax.sem, 1)
                after(dve, cmax, t, r + 1)
                dve.tensor_scalar(c_stat[:, 2, q], c_stat[:, 1, q], -1.0, None, ALU.mult).then_inc(cneg.sem, 1)
                dve.tensor_tensor(c_stat[:, 4, q], sinks[:, q], c_stat[:, 1, q], ALU.subtract).then_inc(csub.sem, 1)

            def c_out(t, r):
                q = slice(4 * r, 4 * r + 4)
                after(dve, cexp, t, r + 1)
                after(dve, csink, t, r + 1)
                dve.tensor_tensor(c_stat[:, 5, q], c_stat[:, 3, q], c_stat[:, 4, q], ALU.add).then_inc(cden.sem, 1)
                after(dve, cden, t, r + 1)
                dve.reciprocal(c_stat[:, 6, q], c_stat[:, 5, q]).then_inc(crec.sem, 1)
                after(dve, crec, t, r + 1)
                after(dve, full["c0"], t, (7, 12)[r])
                after(dve, full["d1"], t - 1, 1)
                cols = slice(H * P + r * 4 * HD, H * P + (r + 1) * 4 * HD)
                dve.tensor_tensor(mix[:, cols].rearrange("p (h d) -> p h d", d=HD), ps["c0"][:, 0:4 * HD].rearrange("p (h d) -> p h d", d=HD),
                                  c_stat[:, 6, q].unsqueeze(2).broadcast_to([P, 4, HD]), ALU.mult).then_inc(mixb.sem, 1)

            def d_lo(v):
                for b in range(2):
                    after(dve, dhi, v, b + 1)
                    after(dve, full["d1"], v - 1, 2)
                    dve.tensor_tensor(mix_lo[:, 4 * b:4 * b + 4], ps_d[:, b].rearrange("p (k c) -> p k c", c=P),
                                      mix_hi[:, 4 * b:4 * b + 4].bitcast(F32), ALU.subtract).then_inc(free[f"d{b}"].sem, 1)

            def d_ms(v, n):
                after(dve, dsq, v, n)
                dve.tensor_scalar(d_stat[:, 3 * n - 2:3 * n - 1], d_stat[:, 3 * n - 3:3 * n - 2], 1.0 / D, EPS, ALU.mult,
                                  ALU.add).then_inc(dms.sem, 1)

            def d_res(v):
                after(dve, drstd, v, 1)
                after(dve, e_full, v - 1)
                for b in range(2):
                    cols = slice(b * HALF, (b + 1) * HALF)
                    dve.scalar_tensor_tensor(y[:, cols], ps_d[:, b], d_stat[:, 2:3], g_post[:, cols], ALU.mult, ALU.mult).then_inc(
                        free[f"d{b}"].sem, 1)

            def d_norm(v):
                after(dve, drstd, v, 2)
                after(dve, free["d1"], v, 2)
                dve.scalar_tensor_tensor(y[:], x[:], d_stat[:, 5:6], g_ffn[:], ALU.mult, ALU.mult).then_inc(dh.sem, 1)

            for s in [full[n] for n in ("d0", "d1")] + [free[n] for n in ("d0", "d1")] + [dhi, dsq, dms, drstd, dx, dh, e_full, e_free]:
                dve.sem_inc(s.sem, s.credit)
            dve.wait_ge(s_tab, 16)
            a_n2(0, 0)
            a_bv(0, 0)
            a_khat(0, 0)
            a_diff(0, 0)
            a_low(0)
            a_qk(0)
            a_init(0)

            def w_split(k):
                dve.wait_ge(s_whi, k + 1)
                dve.tensor_tensor(w_lo[:, k], h_t[:, k], w_hi[:, k].bitcast(F32), ALU.subtract).then_inc(s_wlo, 1)

            for n in range(1, LV + 1):
                a_off(0, n)
                w_split(n - 1)
                a_inv(0, n)
            for k in range(LV, KD):
                w_split(k)
            a_n2(1, 1)
            dve.wait_ge(s_load, LOADS)
            dve.wait_ge(s_zero, 5)

            def step(t, par, n, a, d, e):
                b_resid(t, par)
                if a:
                    a_bv(t + 1, 1 - par)
                if e:
                    d_ms(t - 2, 1)
                if a:
                    a_khat(t + 1, 1 - par)
                if e:
                    d_res(t - 2)
                b_o1(t, par)
                if a:
                    a_diff(t + 1, 1 - par)
                b_state(t, par)
                if d:
                    d_lo(t - 1)
                b_o(t)
                c_scores(t, par, 0)
                if a:
                    a_low(t + 1)
                    a_qk(t + 1)
                b_ms(t)
                if a:
                    a_init(t + 1)
                c_scores(t, par, 1)
                c_max(t, 0)
                if a:
                    a_off(t + 1, 1)
                b_mix(t)
                if a:
                    a_inv(t + 1, 1)
                    a_off(t + 1, 2)
                    a_inv(t + 1, 2)
                if e:
                    d_ms(t - 2, 2)
                if a:
                    a_off(t + 1, 3)
                c_out(t, 0)
                if a:
                    a_inv(t + 1, 3)
                if e:
                    d_norm(t - 2)
                c_scores(t, par, 2)
                if n:
                    a_n2(t + 2, par)
                if a:
                    a_off(t + 1, 4)
                c_scores(t, par, 3)
                c_max(t, 1)
                if a:
                    a_inv(t + 1, 4)
                    a_off(t + 1, 5)
                    a_inv(t + 1, 5)
                    a_off(t + 1, 6)
                    a_inv(t + 1, 6)
                c_out(t, 1)

            steps(dve, step)
            def h_lo(k):
                dve.wait_ge(s_hhi, k + 1)
                dve.tensor_tensor(w_lo[:, k, 0:S - P], h_t[:, k, 0:S - P], w_hi[:, k, 0:S - P].bitcast(F32), ALU.subtract)

            d_ms(T - 2, 1)
            d_res(T - 2)
            d_ms(T - 2, 2)
            d_norm(T - 2)
            d_lo(T - 1)
            d_ms(T - 1, 1)
            d_res(T - 1)
            for k in range(KD // 2):
                h_lo(k)
            d_ms(T - 1, 2)
            d_norm(T - 1)
            for k in range(KD // 2, KD):
                h_lo(k)
            for b in range(2):
                dve.wait_ge(s_hhi, KD + b + 1)
                dve.tensor_tensor(w_lo[:, 4 * b:4 * b + 4, S - P:S], bank(f"b{b}"), w_hi[:, 4 * b:4 * b + 4, S - P:S].bitcast(F32),
                                  ALU.subtract)

        @block.tensor
        def _(pe):
            def fill(name, t, k):
                after(pe, free[name], t if k > 1 else t - 1, k - 1 if k > 1 else None)

            def a_tr(u):
                after(pe, qkv_in, u)
                fill("a0", u, 1)
                for h in range(H):
                    op = pe.transpose(bank("a0")[:, h], qkv[:, H + h], ident)
                op.then_inc(full["a0"].sem, 1)
                after(pe, n2, u)
                for h in range(H):
                    op = pe.transpose(bank("a1")[:, h], qkv[:, 2 * H + h], ident)
                op.then_inc(full["a1"].sem, 1)

            def a_norms(u):
                after(pe, squared, u)
                after(pe, qkv_in, u)
                fill("a1", u, 1)
                for c in range(2 * H):
                    op = pe.matmul(ps["a1"][:, c:c + 1], squares[:, c], ones[:, 0:1], start=True, stop=True)
                op.then_inc(full["a1"].sem, 1)

            def a_sums(u):
                after(pe, tri_set, u)
                fill("a1", u, 2)
                pe.matmul(ps["a1"][:], ones, flat(g_tri[:]), start=True, stop=True).then_inc(full["a1"].sem, 1)

            def a_trk(u):
                after(pe, khat, u)
                for h in range(H):
                    op = pe.transpose(bank("a0")[:, h], k_tok[:, h], ident)
                op.then_inc(full["a0"].sem, 1)

            def a_kk(u):
                after(pe, free["a0"], u, 1)
                for h in range(H):
                    op = pe.matmul(bank("a0")[:, h], k_t[:, h], k_t[:, h], start=True, stop=True)
                op.then_inc(full["a0"].sem, 1)

            def a_kq(u):
                fill("a2", u, 1)
                after(pe, qt_set, u)
                for h in range(H):
                    op = pe.matmul(bank("a2")[:, h], k_t[:, h], q_t[:, h], start=True, stop=True)
                op.then_inc(full["a2"].sem, 1)

            def a_trl(u):
                after(pe, free["a0"], u, 2)
                fill("a1", u, 3)
                for h in range(H):
                    op = pe.transpose(bank("a1")[:, h], low[:, h], ident)
                op.then_inc(full["a1"].sem, 1)

            def a_off(u, n):
                if n == 1:
                    after(pe, init, u, 2)
                    after(pe, free["a1"], u, 3)
                else:
                    after(pe, free["a2"], u, n)
                for h in range(H):
                    op = pe.matmul(bank("a0")[:, h], low_t[:, h], inv[:, h], start=True, stop=True)
                op.then_inc(full["a0"].sem, 1)

            def a_inv(u, n):
                after(pe, free["a0"], u, 2 + n)
                if n == 1:
                    after(pe, init_t, u, 2)
                after(pe, free["a2"], u, n)
                for h in range(H):
                    if n < LV:
                        pe.matmul(ps_half(n, 0)[:, h], inv_t[:, h], half_cols(off[:], h, n, 0), start=True, stop=True)
                    op = pe.matmul(ps_half(n, 1)[:, h], off[:, h], half_cols(inv_t[:], h, n, 1), start=True, stop=True)
                op.then_inc(full["a2"].sem, 1)

            def b_ks(t):
                after(pe, st_set, t - 1)
                after(pe, e_free, t - 3)
                for h in range(H):
                    op = pe.matmul(bank("b0")[:, h], k_t[:, h], state[:, h], start=True, stop=True)
                op.then_inc(full["b0"].sem, 1)

            def b_vnew(t):
                after(pe, free["b0"], t, 1)
                for h in range(H):
                    op = pe.matmul(bank("b0")[:, h], inv_t[:, h], resid[:, h], start=True, stop=True)
                op.then_inc(full["b0"].sem, 1)

            def b_o1(t):
                after(pe, o_set, t - 1)
                for h in range(H):
                    op = pe.matmul(bank("b1")[:, h], q_t[:, h], state[:, h], start=True, stop=True)
                op.then_inc(full["b1"].sem, 1)

            def b_ds(t):
                after(pe, free["b0"], t, 2)
                after(pe, kout_set, t)
                for h in range(H):
                    op = pe.matmul(bank("b0")[:, h], k_out[:, h], v_new[:, h], start=True, stop=True)
                op.then_inc(full["b0"].sem, 1)

            def b_o2(t):
                after(pe, o1_set, t)
                for h in range(H):
                    op = pe.matmul(bank("b1")[:, h], qk_t[:, h], v_new[:, h], start=True, stop=True)
                op.then_inc(full["b1"].sem, 1)

            def c_trq(t):
                after(pe, row_in, t)
                after(pe, mixb, t - 1, 2)
                for b in range(4):
                    op = pe.transpose(bank("c0")[:, b], row[:, Q0 + b * P:Q0 + (b + 1) * P], ident)
                op.then_inc(full["c0"].sem, 1)

            def c_trk(t):
                after(pe, kdup_set, t)
                after(pe, free["c0"], t, 1)
                for kv in range(KVH):
                    op = pe.transpose(bank("c0")[:, kv], k_dup[:, kv].rearrange("p a d -> p (a d)"), ident)
                op.then_inc(full["c0"].sem, 1)

            def c_scores(t, n):
                if n == 2:
                    after(pe, mixb, t, 1)
                else:
                    after(pe, free["c0"], t, (2, 3, None, 7)[n])
                for h in range(2):
                    part = slice(n % 2 * HD, (n % 2 + 1) * HD)
                    op = pe.matmul(ps["c0"][:, 256 * h:256 * h + 256], q_b[part, n // 2 * 2 + h], k_b[part, n // 2].rearrange("p a b -> p (a b)"),
                                   start=True, stop=True)
                op.then_inc(full["c0"].sem, 1)

            def c_trp(t, n):
                after(pe, cexp, t, n // 2 + 1)
                after(pe, free["c0"], t, (4, 5, 8, 9)[n])
                for j in range(4):
                    op = pe.transpose(bank("c0")[:, j], scores[:, 2 * (n % 2) + j // 2, j % 2], ident)
                op.then_inc(full["c0"].sem, 1)

            def c_pv(t, r):
                after(pe, free["c0"], t, (6, 10)[r])
                after(pe, vb_set, t)
                for h in range(4):
                    for kt in range(2):
                        op = pe.matmul(ps["c0"][:, h * HD:(h + 1) * HD], p_t[:, h, kt], v_b[:, kt, r * HD:(r + 1) * HD],
                                       start=(kt == 0), stop=(kt == 1))
                op.then_inc(full["c0"].sem, 1)

            def d_tr(v):
                after(pe, mixa, v)
                after(pe, mixb, v, 2)
                for b in range(2):
                    fill(f"d{b}", v, 1)
                    for j in range(4):
                        k = 4 * b + j
                        op = pe.transpose(ps_d[:, b, j * P:(j + 1) * P], mix[:, k * P:(k + 1) * P], ident)
                    op.then_inc(full[f"d{b}"].sem, 1)

            def d_mm(v, half, ks):
                if half == 0 and ks[0] == 0:
                    pe.wait_ge(s_wlo, KD)
                    after(pe, free["d0"], v, 1)
                    after(pe, free["d1"], v, 1)
                cols = slice(half * HALF, (half + 1) * HALF)
                for k in ks:
                    pe.matmul(ps_d[:, half], mix_hi[:, k], w_hi[:, k, cols], start=(k == 0), stop=False)
                    pe.matmul(ps_d[:, half], mix_hi[:, k], w_lo[:, k, cols], start=False, stop=False)
                    op = pe.matmul(ps_d[:, half], mix_lo[:, k], w_hi[:, k, cols], start=False, stop=(k == KD - 1))
                if ks[-1] == KD - 1:
                    op.then_inc(full[f"d{half}"].sem, 1)

            def d_tr2(v, t):
                after(pe, st_set, t)
                after(pe, o_set, t)
                after(pe, dh, v)
                after(pe, e_free, v - 1)
                for b in range(2):
                    for j in range(4):
                        k = 4 * b + j
                        op = pe.transpose(bank(f"b{b}")[:, j], y[:, k * P:(k + 1) * P], ident)
                    op.then_inc(e_full.sem, 1)

            pe.wait_ge(s_tab, 16)
            pe.wait_ge(s_gv, 7)
            for c, m in enumerate((tri, ones)):
                op = pe.matmul(ps["a0"][:, c * T * H:(c + 1) * T * H].rearrange("p (t h) -> p t h", h=H), m, gates[:, :, I_G],
                               start=True, stop=True)
            op.then_inc(s_ps_g, 1)
            pe.wait_ge(s_gate, 1)
            pe.wait_ge(s_zero, 5)
            a_norms(0)
            a_tr(0)
            a_sums(0)
            a_trk(0)
            a_kk(0)
            a_kq(0)
            a_trl(0)
            for n in range(1, LV + 1):
                a_off(0, n)
                a_inv(0, n)
            a_norms(1)

            def step(t, par, n, a, d, e):
                A = (lambda f, *w: f(t + 1, *w)) if a else (lambda f, *w: None)
                D_ = (lambda f, *w: f(t - 1, *w)) if d else (lambda f, *w: None)
                after(pe, free["a2"], t)
                b_ks(t)
                A(a_tr)
                b_vnew(t)
                A(a_sums)
                D_(d_tr)
                c_trq(t)
                b_o1(t)
                A(a_trk)
                b_ds(t)
                c_trk(t)
                b_o2(t)
                A(a_kk)
                c_scores(t, 0)
                A(a_kq)
                D_(d_mm, 0, [0, 1])
                c_scores(t, 1)
                D_(d_mm, 0, [2, 3])
                A(a_trl)
                D_(d_mm, 0, [4, 5, 6])
                A(a_off, 1)
                D_(d_mm, 0, [7])
                A(a_inv, 1)
                D_(d_mm, 1, [0])
                A(a_off, 2)
                c_trp(t, 0)
                A(a_inv, 2)
                c_trp(t, 1)
                D_(d_mm, 1, [1])
                A(a_off, 3)
                c_pv(t, 0)
                A(a_inv, 3)
                c_scores(t, 2)
                if n:
                    a_norms(t + 2)
                A(a_off, 4)
                D_(d_mm, 1, [2])
                c_scores(t, 3)
                A(a_inv, 4)
                D_(d_mm, 1, [3])
                A(a_off, 5)
                if e:
                    d_tr2(t - 2, t)
                A(a_inv, 5)
                c_trp(t, 2)
                D_(d_mm, 1, [4])
                A(a_off, 6)
                c_trp(t, 3)
                D_(d_mm, 1, [5, 6])
                A(a_inv, 6)
                D_(d_mm, 1, [7])
                c_pv(t, 1)

            steps(pe, step)
            d_tr2(T - 2, T - 1)
            d_tr(T - 1)
            d_mm(T - 1, 0, list(range(KD)))
            d_mm(T - 1, 1, list(range(KD)))
            d_tr2(T - 1, T - 1)


FT = DFF // P
FG = FT // 2


def ffn_block(nc, io, acc, h, raw, s_raw):
    with ExitStack() as ctx:
        sb = lambda name, shape, dt=F32: ctx.enter_context(nc.sbuf_tensor(name, shape, dt))
        sem = lambda name: ctx.enter_context(nc.semaphore(name))

        NT = FTAPS * 2 * FT
        h_hi, h_lo = h[:, 0], h[:, 1]
        acc = acc[:].rearrange("p k s -> p (k s)").rearrange("p (t d) -> p t d", t=T)
        slab = 2 * P * KD
        w_hi = sb("f_w_hi", [P, 3, slab], F32R)
        w_lo = sb("f_w_lo", [P, 3, slab], F32R)
        conv = sb("f_conv", [P, 4, S])
        y_hi = sb("f_y_hi", [P, 2, S], F32R)
        y_lo = sb("f_y_lo", [P, 2, S], F32R)
        junk = sb("f_junk", [P, D], BF16)
        gain = sb("f_gain", [P, D])
        ident = sb("f_ident", [P, P])
        rows_a = sb("f_rows_a", [P, P])
        rows_b = sb("f_rows_b", [NT + 2 * FT - P, P])
        taps = sb("f_taps", [P, NT + 2 * FT])
        stat = sb("f_stat", [P, 3, T])
        power = sb("f_power", [P, 1])

        ps_up = ctx.enter_context(nc.psum_tensor("f_ps_up", [P, 2, S], F32))
        ps_dn = ctx.enter_context(nc.psum_tensor("f_ps_dn", [P, 4, HALF], F32))

        s_ident, s_rows, s_gain = sem("f_ident_in"), sem("f_rows_in"), sem("f_gain_in")
        s_taps_ps, s_taps = sem("f_taps_ps"), sem("f_taps_ready")
        s_zero = sem("f_zero")
        s_whi, s_wlo = sem("f_whi"), sem("f_wlo")
        s_pair = sem("f_pair")
        s_first, s_tap, s_conv = sem("f_first"), sem("f_tap"), sem("f_convolved")
        s_gelu, s_prod = sem("f_gelu"), sem("f_prod")
        s_yhi, s_ylo = sem("f_yhi"), sem("f_ylo")
        s_dn, s_acc = sem("f_dn"), sem("f_acc")
        s_freed, s_power = sem("f_freed"), sem("f_power_set")
        s_sq, s_ms, s_rstd, s_norm, s_res = sem("f_sq"), sem("f_ms"), sem("f_rstd"), sem("f_norm"), sem("f_res")
        s_xr = [sem(f"f_xr{n}") for n in range(4)]
        s_out = [sem(f"f_out{n}") for n in range(4)]

        w_up = io["w_up"].rearrange("o (k p) n -> p (o k) n", p=P)
        w_down = io["w_down"].rearrange("o f d -> (o f d)")
        GATE, VALUE, DOWN = 0, 1, 2

        def n_gate(g):
            return 3 * g

        def n_value(g):
            return 3 * g + 1

        def n_down(g):
            return 3 * g + 2

        LAST_DOWN = n_down(FG) - 2

        def steps(eng, step):
            with eng.Fori(1, FG - 1) as g:
                step(g, False)
            step(FG - 1, True)

        def up_w(part, kind):
            return (w_hi, w_lo)[part][:, kind].rearrange("p (k n) -> p k n", k=KD)

        def dn_w(part, kind):
            return (w_hi, w_lo)[part][:, kind].rearrange("p (k n) -> p k n", k=2)

        def y_of(part, last):
            if last:
                return (w_hi, w_lo)[part][:, VALUE].rearrange("p (c s) -> p c s", c=2)
            return (y_hi, y_lo)[part][:]

        block = ctx.enter_context(nc.Block("ffn"))

        def residual(eng, t):
            eng.wait_ge(s_norm, t + 1)
            eng.wait_ge(s_xr[t % 4], 16 * (t // 4 + 1))
            if t == T - 1:
                eng.wait_ge(s_res, t)
            eng.tensor_tensor(conv[:, t % 4], conv[:, t % 4], acc[:, t], ALU.add).then_inc(s_res, 1)

        @block.sync
        def _(sp):
            def reg(v):
                return v if isinstance(v, int) else sp.snap(v)

            def up_src(kind, g):
                return w_up[:, :, bass.ds(reg(g * (2 * P) + kind * DFF), 2 * P)]

            def down_src(g):
                return w_down[bass.ds(reg(g * (2 * P * D)), 2 * P * D)].rearrange("(k p d) -> p k d", k=2, p=P)

            def load(slot, src, k):
                sp.dma_start(raw[:, slot].rearrange("p (k n) -> p k n", k=k), src).then_inc(s_raw[slot], 16)

            def free(n):
                sp.wait_ge(s_whi, n)
                sp.wait_ge(s_wlo, n)
                sp.sem_inc(s_freed, 1)

            sp.dma_start(ident[:], io["tables"][:, T_ID:T_ID + P]).then_inc(s_ident, 16)
            rows = io["ffn_conv_w"].rearrange("o k (c p) -> (o k c) p", p=P)
            sp.dma_start(rows_a[:], rows[0:P]).then_inc(s_rows, 16)
            sp.dma_start(rows_b[0:NT - P], rows[P:NT]).then_inc(s_rows, 16)
            sp.dma_start(rows_b[NT - P:], io["ffn_conv_b"].rearrange("o (c p) -> (o c) p", p=P)).then_inc(s_rows, 16)
            free(1)
            load(0, up_src(GATE, 1), KD)
            free(2)
            load(1, up_src(VALUE, 1), KD)
            sp.dma_start(gain[:], io["g_post_ffn"][0:1, :].broadcast_to([P, D])).then_inc(s_gain, 16)
            free(3)
            load(0, down_src(0), 2)

            def step(g, last):
                if not last:
                    value_free, gate_free, down_free = reg(n_value(g)), reg(n_down(g)), reg(n_gate(g + 1))
                    gate_from, value_from, down_from = up_src(GATE, g + 1), up_src(VALUE, g + 1), down_src(g)
                    free(value_free)
                    load(1, value_from, KD)
                    free(gate_free)
                    load(0, gate_from, KD)
                    free(down_free)
                    load(0, down_from, 2)
                else:
                    free(n_down(g))
                    load(0, down_src(g), 2)

            steps(sp, step)
            sp.wait_ge(s_ylo, 2 * FG)
            sp.wait_ge(s_yhi, 2 * FG)
            for t in range(4):
                sp.dma_start(conv[:, t], io["res"][t]).then_inc(s_xr[t], 16)
            for t in range(T):
                sp.wait_ge(s_res, t + 1)
                sp.dma_start(io["out"][0, t * P:(t + 1) * P, :], conv[:, t % 4]).then_inc(s_out[t % 4], 16)
                if t + 4 < T:
                    sp.wait_ge(s_out[t % 4], 16)
                    sp.dma_start(conv[:, t % 4], io["res"][t + 4]).then_inc(s_xr[t % 4], 16)
            for q in s_out:
                sp.wait_ge(q, 16 * (T // 4))

        @block.scalar
        def _(act):
            def split(n, kind, slot, loads):
                act.wait_ge(s_raw[slot], 16 * loads)
                act.copy(w_hi[:, kind], raw[:, slot]).then_inc(s_whi, 1)

            def first(n, q, ct):
                act.wait_ge(s_pair, n + 1)
                act.activation(conv[:, q], ps_up[:, q % 2], ACT.Identity, bias=taps[:, bass.ds(ct + NT, 1)],
                               scale=taps[:, bass.ds(ct + (FTAPS - 1) * 2 * FT, 1)]).then_inc(s_first, 1)

            def step(g, last, lead=False):
                if not lead:
                    act.wait_ge(s_dn, g * 16 - 15)
                    split(n_down(g), DOWN, 0, g * 2 + 1)
                    act.wait_ge(s_prod, 2 * g)
                for c in range(2):
                    first(4 * g + c, c, g * 2 + c)
                for c in range(2):
                    act.wait_ge(s_conv, 4 * g + c + 3)
                    act.activation(conv[:, c], conv[:, c], ACT.Gelu_apprx_tanh).then_inc(s_gelu, 1)
                if not last:
                    act.wait_ge(s_pair, 4 * g + 2)
                    split(n_gate(g + 1), GATE, 0, 2 * g + 2)
                else:
                    act.wait_ge(s_pair, 4 * g + 2)
                    split(LAST_DOWN, GATE, 0, 2 * FG)
                if not lead:
                    act.wait_ge(s_ylo, 2 * g)
                for c in range(2):
                    first(4 * g + 2 + c, 2 + c, g * 2 + (c + FT))
                if not last:
                    act.wait_ge(s_pair, 4 * g + 4)
                    split(n_value(g + 1), VALUE, 1, g + 2)
                for c in range(2):
                    act.wait_ge(s_prod, 2 * g + c + 1)
                    if last:
                        act.wait_ge(s_pair, 4 * g + 4)
                    elif not lead:
                        act.wait_ge(s_dn, 16 * g + 1)
                    act.copy(y_of(0, last)[:, c], conv[:, 2 + c]).then_inc(s_yhi, 1)

            for n, (kind, slot) in enumerate([(GATE, 0), (VALUE, 1)]):
                split(n + 1, kind, slot, 1)
            act.wait_ge(s_taps, 1)
            step(0, False, lead=True)
            steps(act, step)
            for t in range(T):
                act.wait_ge(s_acc, 16 * (FG - 1) + 2 * t + 2 + 4)
                act.activation(junk[:], acc[:, t], ACT.Square, accum_out=stat[:, 0, t:t + 1]).then_inc(s_sq, 1)

        @block.vector
        def _(dve):
            dve.sem_inc(s_conv, 2)
            dve.sem_inc(s_acc, 4)

            def split(n, kind, slot):
                dve.wait_ge(s_whi, n)
                dve.tensor_tensor(w_lo[:, kind], raw[:, slot], w_hi[:, kind].bitcast(F32), ALU.subtract).then_inc(s_wlo, 1)

            def convolve(n, q, ct):
                dve.wait_ge(s_first, n + 1)
                for k in range(1, FTAPS):
                    op = dve.scalar_tensor_tensor(conv[:, q, k:S], ps_up[:, q % 2, 0:S - k],
                                                  taps[:, bass.ds(ct + (FTAPS - 1 - k) * 2 * FT, 1)], conv[:, q, k:S],
                                                  ALU.mult, ALU.add)
                    if k == 1:
                        op.then_inc(s_tap, 1)
                        dve.wait_ge(s_tap, n + 1)
                    else:
                        op.then_inc(s_conv, 1)

            def accumulate(m, t, half):
                dve.wait_ge(s_dn, m + 2)
                cols = acc[:, t, half * HALF:(half + 1) * HALF]
                dve.tensor_tensor(cols, ps_dn[:, (2 * t + half) % 4], cols, ALU.add).then_inc(s_acc, 1)

            def step(g, last, lead=False):
                if not lead:
                    split(n_down(g), DOWN, 0)
                for c in range(2):
                    convolve(4 * g + c, c, g * 2 + c)
                split(LAST_DOWN if last else n_gate(g + 1), GATE, 0)
                for c in range(2):
                    convolve(4 * g + 2 + c, 2 + c, g * 2 + (c + FT))
                def low_part(c):
                    dve.wait_ge(s_yhi, 2 * g + c + 1)
                    dve.tensor_tensor(y_of(1, last)[:, c], conv[:, 2 + c], y_of(0, last)[:, c].bitcast(F32), ALU.subtract).then_inc(
                        s_ylo, 1)

                for j in range(2 * T):
                    if not lead:
                        accumulate(g * 16 + (j - 16), j // 2, j % 2)
                    if j in (3, 6):
                        c = (j - 3) // 3
                        dve.wait_ge(s_gelu, 2 * g + c + 1)
                        dve.wait_ge(s_conv, 4 * g + c + 5)
                        dve.tensor_tensor(conv[:, 2 + c], conv[:, c], conv[:, 2 + c], ALU.mult).then_inc(s_prod, 1)
                    if j == 9 and not last:
                        split(n_value(g + 1), VALUE, 1)
                    if j in (9, 12) and last:
                        low_part((j - 9) // 3)
                if not last:
                    for c in range(2):
                        low_part(c)

            def finish(t):
                dve.wait_ge(s_rstd, t + 1)
                dve.scalar_tensor_tensor(acc[:, t], acc[:, t], stat[:, 2, t:t + 1], gain[:], ALU.mult, ALU.mult).then_inc(s_norm, 1)
                if t == T - 1:
                    residual(dve, t)

            for n, (kind, slot) in enumerate([(GATE, 0), (VALUE, 1)]):
                split(n + 1, kind, slot)
            dve.wait_ge(s_taps_ps, 1)
            dve.tensor_copy(taps[:], ps_dn[:, 0, 0:NT + 2 * FT]).then_inc(s_taps, 1)
            dve.wait_ge(s_taps, 1)
            step(0, False, lead=True)
            dve.wait_ge(s_zero, 1)
            steps(dve, step)
            dve.wait_ge(s_gain, 16)
            for t in range(T + 1):
                if t < T:
                    for half in range(2):
                        accumulate(16 * (FG - 1) + 2 * t + half, t, half)
                    dve.wait_ge(s_sq, t + 1)
                    dve.tensor_scalar(stat[:, 1, t:t + 1], stat[:, 0, t:t + 1], 1.0 / D, EPS, ALU.mult, ALU.add).then_inc(s_ms, 1)
                if t >= 1:
                    finish(t - 1)

        @block.gpsimd
        def _(pool):
            pool.memset(power[:], -0.5).then_inc(s_power, 1)
            pool.memset(acc, 0.0).then_inc(s_zero, 1)
            pool.wait_ge(s_power, 1)
            for t in range(T):
                pool.wait_ge(s_ms, t + 1)
                pool.tensor_tensor(stat[:, 2, t:t + 1], stat[:, 1, t:t + 1], power[:], ALU.pow).then_inc(s_rstd, 1)
                if t >= 1:
                    residual(pool, t - 1)

        @block.tensor
        def _(pe):
            def up(n, kind, c):
                pe.wait_ge(s_conv, n + 1)
                for half in range(2):
                    bank = ps_up[:, c, half * HALF:(half + 1) * HALF]
                    cols = slice(half * HALF, (half + 1) * HALF)
                    for k in range(KD):
                        hi = up_w(0, kind)[:, k, c * P:(c + 1) * P]
                        lo = up_w(1, kind)[:, k, c * P:(c + 1) * P]
                        pe.matmul(bank, hi, h_hi[:, k, cols], start=(k == 0), stop=False)
                        pe.matmul(bank, hi, h_lo[:, k, cols], start=False, stop=False)
                        op = pe.matmul(bank, lo, h_hi[:, k, cols], start=False, stop=(k == KD - 1))
                op.then_inc(s_pair, 1)

            def down(g):
                last = isinstance(g, int) and g == FG
                kind = GATE if last else DOWN
                pe.wait_ge(s_wlo, LAST_DOWN if last else n_down(g))
                pe.wait_ge(s_ylo, 2 * g)
                for j in range(2 * T):
                    t, half = j // 2, j % 2
                    pe.wait_ge(s_acc, g * 16 + (j - 15))
                    for k in range(2):
                        y = slice(t * P, (t + 1) * P)
                        cols = slice(half * HALF, (half + 1) * HALF)
                        bank = ps_dn[:, j % 4]
                        pe.matmul(bank, y_of(0, last)[:, k, y], dn_w(0, kind)[:, k, cols], start=(k == 0), stop=False)
                        pe.matmul(bank, y_of(0, last)[:, k, y], dn_w(1, kind)[:, k, cols], start=False, stop=False)
                        op = pe.matmul(bank, y_of(1, last)[:, k, y], dn_w(0, kind)[:, k, cols], start=False, stop=(k == 1))
                    op.then_inc(s_dn, 1)

            def ups(g):
                for kind, n in ((GATE, n_gate(g)), (VALUE, n_value(g))):
                    pe.wait_ge(s_wlo, n)
                    for c in range(2):
                        up(4 * g + 2 * kind + c, kind, c)

            def step(g, last):
                ups(g)
                down(g)

            pe.sem_inc(s_dn, 1)
            pe.wait_ge(s_ident, 16)
            pe.wait_ge(s_rows, 48)
            nb = NT + 2 * FT - P
            pe.transpose(ps_dn[:, 0, 0:P], rows_a[:], ident[:])
            pe.transpose(ps_dn[:, 0, P:P + nb], rows_b[:], ident[0:nb, 0:nb]).then_inc(s_taps_ps, 1)
            for kind in (GATE, VALUE):
                pe.wait_ge(s_wlo, kind + 1)
                for c in range(2):
                    up(2 * kind + c, kind, c)
            pe.wait_ge(s_taps, 1)
            steps(pe, step)
            down(FG)


_INS = ["x", "g_pre_mix", "w_in", "gdn_conv_w", "gdn_A_log", "gdn_dt_bias", "gdn_norm_w", "attn_sinks", "w_out",
        "g_post_mix", "g_pre_ffn", "w_up", "ffn_conv_w", "ffn_conv_b", "w_down", "g_post_ffn"]


def kernel(**inputs):
    import concourse.bacc as bacc
    from concourse.bass_utils import run_bass_kernel_spmd

    nc = bacc.Bacc("TRN2", target_bir_lowering=False, num_devices=1)
    arrays, io = {}, {}
    for name in _INS:
        a = np.ascontiguousarray(inputs[name])
        arrays[f"in_{name}"] = a
        io[name] = nc.dram_tensor(f"in_{name}", a.shape, mybir.dt.from_np(a.dtype), kind="ExternalInput").ap()
    arrays["in_tables"] = tables()
    io["tables"] = nc.dram_tensor("in_tables", (P, T_W), F32, kind="ExternalInput").ap()
    SCR = "Internal"
    io["rows"] = nc.dram_tensor("rows", (T, P, ROW), F32, kind=SCR).ap()
    io["qkv"] = nc.dram_tensor("qkv", (T, P, A_TILES, P), F32, kind=SCR).ap()
    io["out"] = nc.dram_tensor("out", (1, S, D), F32, kind="ExternalOutput").ap()
    io["res"] = nc.dram_tensor("res", (T, P, D), F32, kind=SCR).ap()
    project_block(nc, io)
    with ExitStack() as ctx:
        h_t = ctx.enter_context(nc.sbuf_tensor("h_t", [P, KD, S], F32))
        split = ctx.enter_context(nc.sbuf_tensor("split", [P, 2, KD, S], F32R))
        stage = ctx.enter_context(nc.sbuf_tensor("stage", [P, 2, 2 * P * KD], F32))
        s_stage = [ctx.enter_context(nc.semaphore(f"s_stage{n}")) for n in range(2)]
        mix_block(nc, io, h_t, split, stage, s_stage)
        ffn_block(nc, io, h_t, split, stage, s_stage)
    r = run_bass_kernel_spmd(nc, [arrays], core_ids=[0])
    return r.results[0]["out"]
```

```python
from contextlib import ExitStack

import numpy as np

import concourse.bass as bass
from concourse import mybir

P = 128
F32 = mybir.dt.float32
F32R = mybir.dt.float32r
BF16 = mybir.dt.bfloat16
ALU = mybir.AluOpType
ACT = mybir.ActivationFunctionType
AX_X = mybir.AxisListType.X

EPS = 1e-6
D = 1024
S = 1024
T = S // P
KD = D // P
HALF = 512
GH, DK = 4, 128
QH, KVH, HD = 8, 2, 64
CHUNK = 64
ROT = HD // 4
ROPE_THETA = 500000.0
GTAPS, FTAPS = 4, 3
DFF = 2816
A_CH = 3 * GH * DK
A_TILES = A_CH // P
Z0, AB0, Q0 = 0, GH * DK, GH * DK + 2 * GH
K0 = Q0 + QH * HD
V0 = K0 + KVH * HD
ROW = V0 + KVH * HD
GROUPS = [(0, HALF), (HALF, HALF), (2 * HALF, ROW - 2 * HALF)]
NEG = -1e30

T_ID, T_TRI, T_STRICT = 0, P, 2 * P
LEVELS = [1, 2, 4, 8, 16, 32, 64]
T_ONES = 3 * P
T_LEVEL = 4 * P
T_LEVEL0T = T_LEVEL + len(LEVELS) * P
T_CUR, T_PREV = T_LEVEL0T + P, T_LEVEL0T + 2 * P
T_ROPE = T_PREV + P
T_W = T_ROPE + T * 2 * (ROT // 2)


def tables():
    i, j = np.arange(P)[:, None], np.arange(P)[None, :]
    t = np.zeros((P, T_W), np.float32)
    t[:, T_ID:T_ID + P] = i == j
    t[:, T_TRI:T_TRI + P] = i <= j
    t[:, T_STRICT:T_STRICT + P] = j < i
    for n, s in enumerate(LEVELS):
        m = (i // (2 * s) == j // (2 * s)) & ((i // s) % 2 == 1) & ((j // s) % 2 == 0)
        t[:, T_LEVEL + n * P:T_LEVEL + (n + 1) * P] = -1.0 * m
        if n == 0:
            t[:, T_LEVEL0T:T_LEVEL0T + P] = -1.0 * m.T
    t[:, T_CUR:T_CUR + P] = np.where(j // CHUNK <= i // CHUNK, 0.0, NEG)
    t[:, T_PREV:T_PREV + P] = np.where((i // CHUNK == 0) & (j // CHUNK == 1), 0.0, NEG)
    t[:, T_ONES:T_ONES + P] = 1.0
    pos = np.arange(S, dtype=np.float32)
    inv = (np.float32(ROPE_THETA) ** (-np.arange(0, ROT, 2, dtype=np.float32) / np.float32(ROT))).astype(np.float32)
    ang = (pos[:, None] * inv[None, :]).astype(np.float32).reshape(T, P, ROT // 2)
    r = t[:, T_ROPE:].reshape(P, T, 2, ROT // 2)
    r[:, :, 0] = np.cos(ang).transpose(1, 0, 2)
    r[:, :, 1] = np.sin(ang).transpose(1, 0, 2)
    return t


def project_block(nc, io):
    SLOTS = 4
    with ExitStack() as ctx:
        sb = lambda name, shape, dt=F32: ctx.enter_context(nc.sbuf_tensor(name, shape, dt))
        sem = lambda name: ctx.enter_context(nc.semaphore(name))

        h_hi = sb("h_hi", [P, KD, S], F32R)
        h_lo = sb("h_lo", [P, KD, S], F32R)
        wbuf = sb("wbuf", [P, 2 * KD * ROW], F32R)
        raw = sb("raw", [P, SLOTS, KD // 2 * GROUPS[2][1]])
        tile_hi = sb("tile_hi", [P, 2, KD, P], F32R)
        tile_lo = sb("tile_lo", [P, 2, KD, P], F32R)
        xin = sb("xin", [P, 2, D])
        h = sb("h", [P, D])
        junk = sb("junk", [P, D], BF16)
        row = sb("row", [P, ROW])
        gain = sb("gain", [P, D])
        ident = sb("ident", [P, P])
        rope = sb("rope", [P, T, 2, ROT // 2])
        rot = sb("rot", [P, 4, QH + KVH, ROT // 2])
        stat = sb("stat", [P, 2, 4])
        power = sb("power", [P, 1])
        convrows = sb("convrows", [GTAPS * A_TILES, P])
        taps = sb("taps", [P, GTAPS * A_TILES])
        conv = xin

        ps_t = ctx.enter_context(nc.psum_tensor("ps_t", [P, 2, HALF], F32))
        ps_g = ctx.enter_context(nc.psum_tensor("ps_g", [P, 6, HALF], F32))

        s_x = [sem("s_x0"), sem("s_x1")]
        s_const, s_gain, s_rope, s_conv_rows = sem("s_const"), sem("s_gain"), sem("s_rope"), sem("s_conv_rows")
        s_raw = [sem(f"s_raw{n}") for n in range(SLOTS)]
        s_slab = [sem("s_slab0"), sem("s_slab1")]
        s_whi, s_wlo = sem("s_whi"), sem("s_wlo")
        s_power = sem("s_power")
        s_taps_ps, s_taps = sem("s_taps_ps"), sem("s_taps")
        s_sq, s_ms, s_rstd = sem("s_sq"), sem("s_ms"), sem("s_rstd")
        s_h, s_tr = sem("s_h"), sem("s_tr")
        s_hi, s_lo, s_big = sem("s_hi"), sem("s_lo"), sem("s_big")
        s_mm = sem("s_mm")
        s_z, s_mid, s_last = sem("s_z"), sem("s_mid"), sem("s_last")
        s_rot4, s_rot, s_row_out = sem("s_rot4"), sem("s_rot"), sem("s_row_out")
        s_pair, s_first, s_tap, s_conv = sem("s_pair"), sem("s_first"), sem("s_tap"), sem("s_conv")
        s_silu = sem("s_silu")
        s_qkv_out = [sem("s_qkv_out0"), sem("s_qkv_out1")]

        w_in = io["w_in"].rearrange("o (k p) n -> p (o k) n", p=P)
        rows_flat = io["rows"].rearrange("t p n -> (t p n)")
        x_tiles = io["x"].rearrange("o (t p) d -> (o t) p d", p=P)

        chunks = [(g, k, 2) for g in range(2) for k in range(0, KD, 2)] + [(2, 0, KD // 2), (2, KD // 2, KD // 2)]
        ready = [4, 8, 10]
        base = [0, 2 * KD * HALF, 4 * KD * HALF]

        def group_w(g, part):
            n = GROUPS[g][1]
            a = base[g] + part * KD * n
            return wbuf[:, a:a + KD * n].rearrange("p (k n) -> p k n", k=KD)

        def raw_chunk(c):
            g, _, nk = chunks[c]
            n = GROUPS[g][1]
            return raw[:, c % SLOTS, 0:nk * n].rearrange("p (k n) -> p k n", k=nk)

        def slab_w(slot, part):
            a = slot * 4 * P * KD + part * 2 * P * KD
            return wbuf[:, a:a + 2 * P * KD].rearrange("p (k n) -> p k n", k=KD)

        NCH = len(chunks)
        SLABS = A_TILES // 2

        def raw_slab(slot):
            both = raw[:, 2 * slot:2 * slot + 2].rearrange("p a n -> p (a n)")
            return both[:, 0:2 * P * KD].rearrange("p (k n) -> p k n", k=KD)

        def raw_count(n):
            return 16 * (n // SLOTS + 1)

        block = ctx.enter_context(nc.Block("project"))

        def tiles(eng, step, first=True):
            if first:
                step(0, 0, 0)
            with eng.Fori(0, T // 2 - 1) as i:
                step(i * 2 + 1, 1, i)
                step(i * 2 + 2, 0, i)
            step(T - 1, 1, T // 2 - 1)

        def slabs(eng, step):
            with eng.Fori(0, SLABS // 2 - 1) as i:
                step(i * 2, 0, i, False)
                step(i * 2 + 1, 1, i, False)
            step(SLABS - 2, 0, SLABS // 2 - 1, False)
            step(SLABS - 1, 1, SLABS // 2 - 1, True)

        @block.sync
        def _(sp):
            for q in s_qkv_out:
                sp.sem_inc(q, 16)
            sp.dma_start(xin[:, 0], x_tiles[0]).then_inc(s_x[0], 16)
            sp.dma_start(gain[:], io["g_pre_mix"][0:1, :].broadcast_to([P, D])).then_inc(s_gain, 16)
            sp.dma_start(ident[:], io["tables"][:, T_ID:T_ID + P]).then_inc(s_const, 16)

            def load_chunk(c):
                g, k0, nk = chunks[c]
                c0, n = GROUPS[g]
                if c >= SLOTS:
                    sp.wait_ge(s_whi, c - SLOTS + 1)
                    sp.wait_ge(s_wlo, c - SLOTS + 1)
                sp.dma_start(raw_chunk(c), w_in[:, k0:k0 + nk, A_CH + c0:A_CH + c0 + n]).then_inc(s_raw[c % SLOTS], 16)

            for c in range(SLOTS):
                load_chunk(c)
            sp.dma_start(xin[:, 1], x_tiles[1]).then_inc(s_x[1], 16)
            sp.dma_start(rope[:].rearrange("p t c r -> p (t c r)"), io["tables"][:, T_ROPE:T_W]).then_inc(s_rope, 16)
            for c in range(SLOTS, NCH):
                load_chunk(c)

            def reg(v):
                return v if isinstance(v, int) else sp.snap(v)

            def load_slab(s, slot):
                before = NCH if isinstance(s, int) and s < 2 else reg(s + NCH - 1)
                src = w_in[:, :, bass.ds(reg(s * (2 * P)), 2 * P)]
                sp.wait_ge(s_whi, before)
                sp.wait_ge(s_wlo, before)
                sp.dma_start(raw_slab(slot), src).then_inc(s_slab[slot], 16)

            load_slab(0, 0)
            load_slab(1, 1)

            def tile(t, par, i):
                this, after = reg(t), reg(t + 1)
                row_at = reg((t - 1) * (P * ROW))
                sp.wait_ge(s_h, this)
                sp.dma_start(xin[:, 1 - par], x_tiles[bass.ds(after, 1)].rearrange("o p d -> (o p) d")).then_inc(
                    s_x[1 - par], 16)
                store(row_at, after, this)

            def store(row_at, moved, rotated):
                sp.wait_ge(s_z, moved)
                sp.wait_ge(s_rot, rotated)
                dst = rows_flat[bass.ds(row_at, P * ROW)].rearrange("(p n) -> p n", n=ROW)
                sp.dma_start(dst, row[:]).then_inc(s_row_out, 16)

            with sp.Fori(0, T // 2 - 1) as i:
                tile(i * 2 + 1, 1, i)
                tile(i * 2 + 2, 0, i)
            sp.dma_start(convrows[:], io["gdn_conv_w"].rearrange("o k (c p) -> (o k c) p", p=P)).then_inc(s_conv_rows, 16)
            for t in range(T - 2, T):
                store(t * P * ROW, t + 2, t + 1)

            def slab(s, par, i, last):
                if not isinstance(s, int):
                    load_slab(s + 2, par)
                for c in range(1 if last else 2):
                    tile_c, done = reg(s * 2 + c), reg(s * 2 + c + 1)
                    sp.wait_ge(s_silu, done)
                    dst = io["qkv"][:, :, bass.ds(tile_c, 1), :].rearrange("t p o s -> p (t o) s")
                    sp.dma_start(dst, conv[:, c].rearrange("p (t s) -> p t s", t=T)).then_inc(s_qkv_out[c], 16)

            slabs(sp, slab)
            for half in range(2):
                sp.wait_ge(s_silu, A_TILES + half)
                of = slice(half * (T // 2), (half + 1) * (T // 2))
                dst = io["qkv"][of, :, A_TILES - 1, :].rearrange("t p s -> p t s")
                sp.dma_start(dst, conv[:, 1, half * HALF:(half + 1) * HALF].rearrange("p (t s) -> p t s", s=P)).then_inc(
                    s_qkv_out[1], 16)
            sp.wait_ge(s_row_out, 16 * T)
            sp.wait_ge(s_qkv_out[0], 16 * (A_TILES // 2 + 1))
            sp.wait_ge(s_qkv_out[1], 16 * (A_TILES // 2 + 2))

        @block.gpsimd
        def _(pool):
            pool.memset(power[:], -0.5).then_inc(s_power, 1)
            pool.wait_ge(s_power, 1)

            def rstd(t, par):
                pool.wait_ge(s_ms, t + 1)
                pool.tensor_tensor(stat[:, par, 2:3], stat[:, par, 1:2], power[:], ALU.pow).then_inc(s_rstd, 1)

            def tile(t, par, i):
                if not (isinstance(t, int) and t == T - 1):
                    rstd(t + 1, 1 - par)
                pool.wait_ge(s_hi, 2 * (t + 1))
                pool.wait_ge(s_lo, 2 * (t + 1))
                pool.tensor_copy(h_hi[:, :, bass.ds(t * P, P)], tile_hi[:, par].bitcast(F32)).then_inc(s_big, 1)
                pool.tensor_copy(h_lo[:, :, bass.ds(t * P, P)], tile_lo[:, par].bitcast(F32)).then_inc(s_big, 1)

            rstd(0, 0)
            tiles(pool, tile)

        @block.scalar
        def _(act):
            def front(t, par, load):
                square(t, par, load)
                keep_hi(t, par)

            def square(t, par, load):
                act.wait_ge(s_x[par], 16 * load)
                act.activation(junk[:], xin[:, par], ACT.Square, accum_out=stat[:, par, 0:1]).then_inc(s_sq, 1)

            def keep_hi(t, par):
                if not (isinstance(t, int) and t < 2):
                    act.wait_ge(s_mm, 3 * (t - 1))
                    act.wait_ge(s_big, 2 * (t - 1))
                for b in range(2):
                    act.wait_ge(s_tr, 2 * t + b + 1)
                    act.copy(tile_hi[:, par, 4 * b:4 * b + 4], ps_t[:, b].rearrange("p (k s) -> p k s", k=4)).then_inc(s_hi, 1)

            def split(s, par, loads):
                act.wait_ge(s_slab[par], 16 * loads)
                act.copy(slab_w(par, 0), raw_slab(par)).then_inc(s_whi, 1)

            def tile(t, par, i):
                if not (isinstance(t, int) and t in (0, T - 1)):
                    front(t + 1, 1 - par, i + 2)
                act.wait_ge(s_mm, 3 * t + 1)
                act.wait_ge(s_row_out, 16 * t)
                act.activation(row[:, 0:HALF], ps_g[:, 3 * par], ACT.Silu).then_inc(s_z, 1)
                if isinstance(t, int) and t == T - 1:
                    split(0, 0, 1)
                act.wait_ge(s_mm, 3 * t + 3)
                act.copy(row[:, 2 * HALF:ROW], ps_g[:, 3 * par + 2, 0:GROUPS[2][1]]).then_inc(s_last, 1)

            front(0, 0, 1)
            for c in range(NCH):
                g, k0, nk = chunks[c]
                act.wait_ge(s_raw[c % SLOTS], raw_count(c))
                act.copy(group_w(g, 0)[:, k0:k0 + nk], raw_chunk(c)).then_inc(s_whi, 1)
                if c == ready[0] - 1:
                    square(1, 1, 1)
                if c == ready[1] - 1:
                    keep_hi(1, 1)
            tiles(act, tile)

            def slab(s, par, i, last):
                if not last:
                    act.wait_ge(s_pair, 2 * s + 2)
                    split(s + 1, 1 - par, i + 1 + par)
                for c in range(1 if last else 2):
                    act.wait_ge(s_pair, 2 * s + c + 3)
                    act.wait_ge(s_qkv_out[c], 16 * s + 16)
                    act.activation(conv[:, c], ps_g[:, 2 * c:2 * c + 2].rearrange("p b n -> p (b n)"), ACT.Identity,
                                   scale=taps[:, bass.ds(2 * s + (c + (GTAPS - 1) * A_TILES), 1)]).then_inc(s_first, 1)
                for c in range(1 if last else 2):
                    act.wait_ge(s_conv, 2 * s + c + 3)
                    act.activation(conv[:, c], conv[:, c], ACT.Silu).then_inc(s_silu, 1)
                if last:
                    act.wait_ge(s_qkv_out[1], 16 * s + 16)
                    for half in range(2):
                        act.wait_ge(s_pair, 2 * s + 4 + half)
                        cols = slice(half * HALF, (half + 1) * HALF)
                        act.activation(conv[:, 1, cols], ps_g[:, 2 + half], ACT.Identity,
                                       scale=taps[:, GTAPS * A_TILES - 1:GTAPS * A_TILES]).then_inc(s_first, 1)
                    for half in range(2):
                        cols = slice(half * HALF, (half + 1) * HALF)
                        act.wait_ge(s_conv, 2 * s + 4 + half)
                        act.activation(conv[:, 1, cols], conv[:, 1, cols], ACT.Silu).then_inc(s_silu, 1)

            act.wait_ge(s_taps, 1)
            slabs(act, slab)

        @block.vector
        def _(dve):
            dve.sem_inc(s_conv, 2)
            for q in (s_z, s_mid, s_last):
                dve.sem_inc(q, 1)
            dve.wait_ge(s_gain, 16)

            def front(t, par):
                norm(t, par)
                keep_lo(t, par)

            def norm(t, par):
                st = stat[:, par]
                dve.wait_ge(s_sq, t + 1)
                dve.tensor_scalar(st[:, 1:2], st[:, 0:1], 1.0 / D, EPS, ALU.mult, ALU.add).then_inc(s_ms, 1)
                dve.wait_ge(s_rstd, t + 1)
                if not (isinstance(t, int) and t == 0):
                    dve.wait_ge(s_tr, 2 * t)
                dve.scalar_tensor_tensor(h[:], xin[:, par], st[:, 2:3], gain[:], ALU.mult, ALU.mult).then_inc(s_h, 1)

            def keep_lo(t, par):
                for b in range(2):
                    dve.wait_ge(s_hi, 2 * t + b + 1)
                    k = slice(4 * b, 4 * b + 4)
                    dve.tensor_tensor(tile_lo[:, par, k], ps_t[:, b].rearrange("p (k s) -> p k s", k=4),
                                      tile_hi[:, par, k].bitcast(F32), ALU.subtract).then_inc(s_lo, 1)

            heads = row[:, Q0:V0].rearrange("p (h d) -> p h d", d=HD)
            x1, x2 = heads[:, :, 0:ROT // 2], heads[:, :, ROT // 2:ROT]

            def split(s, par):
                dve.wait_ge(s_whi, s + NCH + 1)
                dve.tensor_tensor(slab_w(par, 1), raw_slab(par), slab_w(par, 0).bitcast(F32), ALU.subtract).then_inc(s_wlo, 1)

            def tile(t, par, i):
                if not (isinstance(t, int) and t in (0, T - 1)):
                    front(t + 1, 1 - par)
                dve.wait_ge(s_mm, 3 * t + 2)
                dve.wait_ge(s_row_out, 16 * t)
                dve.tensor_copy(row[:, HALF:2 * HALF], ps_g[:, 3 * par + 1]).then_inc(s_mid, 1)
                if isinstance(t, int) and t == T - 1:
                    split(0, 0)
                dve.wait_ge(s_mid, t + 2)
                dve.wait_ge(s_last, t + 2)
                cos = rope[:, bass.ds(t, 1), 0, :].broadcast_to([P, QH + KVH, ROT // 2])
                sin = rope[:, bass.ds(t, 1), 1, :].broadcast_to([P, QH + KVH, ROT // 2])
                for n, (a, b) in enumerate([(x1, cos), (x2, sin), (x2, cos), (x1, sin)]):
                    dve.tensor_tensor(rot[:, n], a, b, ALU.mult).then_inc(s_rot4, 1)
                dve.wait_ge(s_rot4, 4 * (t + 1))
                dve.tensor_tensor(x1, rot[:, 0], rot[:, 1], ALU.subtract)
                dve.tensor_tensor(x2, rot[:, 2], rot[:, 3], ALU.add).then_inc(s_rot, 1)

            front(0, 0)
            for c in range(NCH):
                g, k0, nk = chunks[c]
                dve.wait_ge(s_whi, c + 1)
                dve.tensor_tensor(group_w(g, 1)[:, k0:k0 + nk], raw_chunk(c),
                                  group_w(g, 0)[:, k0:k0 + nk].bitcast(F32), ALU.subtract).then_inc(s_wlo, 1)
                if c == ready[0] - 1:
                    norm(1, 1)
                if c == ready[1] - 1:
                    keep_lo(1, 1)
            dve.wait_ge(s_rope, 16)
            tiles(dve, tile)

            def slab(s, par, i, last):
                if not last:
                    split(s + 1, 1 - par)
                for c in range(1 if last else 2):
                    src = ps_g[:, 2 * c:2 * c + 2].rearrange("p b n -> p (b n)")
                    dve.wait_ge(s_first, 2 * s + c + 1)
                    for k in range(1, GTAPS):
                        op = dve.scalar_tensor_tensor(
                            conv[:, c, k:S], src[:, 0:S - k], taps[:, bass.ds(2 * s + (c + (GTAPS - 1 - k) * A_TILES), 1)],
                            conv[:, c, k:S], ALU.mult, ALU.add)
                        if k < GTAPS - 1:
                            op.then_inc(s_tap, 1)
                            dve.wait_ge(s_tap, (2 * s + c) * (GTAPS - 2) + k)
                        else:
                            op.then_inc(s_conv, 1)
                if last:
                    src = ps_g[:, 2:4].rearrange("p b n -> p (b n)")
                    for half in range(2):
                        dve.wait_ge(s_first, 2 * s + 2 + half)
                        for k in range(1, GTAPS):
                            a, b = max(k, half * HALF), (half + 1) * HALF
                            tap = (GTAPS - k) * A_TILES - 1
                            op = dve.scalar_tensor_tensor(conv[:, 1, a:b], src[:, a - k:b - k], taps[:, tap:tap + 1], conv[:, 1, a:b],
                                                          ALU.mult, ALU.add)
                            if k < GTAPS - 1:
                                op.then_inc(s_tap, 1)
                                dve.wait_ge(s_tap, (2 * s + 1 + half) * (GTAPS - 2) + k)
                            else:
                                op.then_inc(s_conv, 1)

            dve.wait_ge(s_taps_ps, 1)
            dve.tensor_copy(taps[:], ps_t[:, 0, 0:GTAPS * A_TILES]).then_inc(s_taps, 1)
            slabs(dve, slab)

        @block.tensor
        def _(pe):
            pe.sem_inc(s_pair, 2)
            pe.wait_ge(s_const, 16)

            def front(t, par):
                pe.wait_ge(s_h, t + 1)
                for b in range(2):
                    if not (isinstance(t, int) and t == 0):
                        pe.wait_ge(s_lo, 2 * t - 1 + b)
                    for k in range(4):
                        last = pe.transpose(ps_t[:, b, k * P:(k + 1) * P], h[:, (4 * b + k) * P:(4 * b + k + 1) * P], ident[:])
                    last.then_inc(s_tr, 1)

            def tile(t, par, i):
                pe.wait_ge(s_lo, 2 * (t + 1))
                for g, (c0, n) in enumerate(GROUPS):
                    pe.wait_ge(s_wlo, ready[g])
                    if not (isinstance(t, int) and t == 0):
                        pe.wait_ge((s_z, s_mid, s_last)[g], t)
                    bank = ps_g[:, 3 * par + g, 0:n]
                    for k in range(KD):
                        pe.matmul(bank, tile_hi[:, par, k], group_w(g, 0)[:, k], start=(k == 0), stop=False)
                        pe.matmul(bank, tile_hi[:, par, k], group_w(g, 1)[:, k], start=False, stop=False)
                        last = pe.matmul(bank, tile_lo[:, par, k], group_w(g, 0)[:, k], start=False, stop=(k == KD - 1))
                    last.then_inc(s_mm, 1)
                    if g == 0 and not (isinstance(t, int) and t == T - 1):
                        front(t + 1, 1 - par)

            front(0, 0)
            tiles(pe, tile)

            def slab(s, par, i, last):
                pe.wait_ge(s_wlo, s + NCH + 1)
                for c in range(2):
                    pe.wait_ge(s_conv, 2 * s + c + 1)
                    for half in range(2):
                        bank = ps_g[:, 2 * c + half]
                        cols = slice(half * HALF, (half + 1) * HALF)
                        for k in range(KD):
                            w_hi = slab_w(par, 0)[:, k, c * P:(c + 1) * P]
                            w_lo = slab_w(par, 1)[:, k, c * P:(c + 1) * P]
                            pe.matmul(bank, w_hi, h_hi[:, k, cols], start=(k == 0), stop=False)
                            pe.matmul(bank, w_hi, h_lo[:, k, cols], start=False, stop=False)
                            op = pe.matmul(bank, w_lo, h_hi[:, k, cols], start=False, stop=(k == KD - 1))
                        if last and c == 1 and half == 0:
                            op.then_inc(s_pair, 1)
                    op.then_inc(s_pair, 1)

            pe.wait_ge(s_big, 2 * T)
            pe.wait_ge(s_conv_rows, 16)
            n = GTAPS * A_TILES
            pe.transpose(ps_t[:, 0, 0:n], convrows[:], ident[0:n, 0:n]).then_inc(s_taps_ps, 1)
            pe.wait_ge(s_z, T + 1)
            pe.wait_ge(s_mid, T)
            pe.wait_ge(s_last, T)
            slabs(pe, slab)


class Tally:

    def __init__(self, nc, ctx, name, per=1, credit=0):
        self.sem, self.per, self.credit = ctx.enter_context(nc.semaphore(name)), per, credit

    def at(self, t, k):
        return t * self.per + (k + self.credit)


def after(eng, tally, t, k=None):
    value = tally.at(t, tally.per if k is None else k)
    if not isinstance(value, int) or value > tally.credit:
        eng.wait_ge(tally.sem, value)


class Kept:

    def __init__(self, nc, ctx):
        sb = lambda name, shape, dt=F32: ctx.enter_context(nc.sbuf_tensor(name, shape, dt))
        self.h_t = sb("h_t", [P, KD, S])
        self.split = sb("split", [P, 2, KD, S], F32R)
        self.stage = sb("stage", [P, 2, 2 * P * KD])
        self.x = sb("x_tile", [P, D])
        self.g_post = sb("g_post", [P, D])
        self.g_ffn = sb("g_ffn", [P, D])
        self.sums = ctx.enter_context(nc.psum_tensor("sums", [P, 4, HALF], F32))
        self.s_stage = [ctx.enter_context(nc.semaphore(f"s_stage{n}")) for n in range(2)]


def mix_block(nc, io, kept):
    with ExitStack() as ctx:
        sb = lambda name, shape, dt=F32: ctx.enter_context(nc.sbuf_tensor("m_" + name, shape, dt))
        sem = lambda name: ctx.enter_context(nc.semaphore("m_" + name))
        tally = lambda name, per=1, credit=0: Tally(nc, ctx, "m_" + name, per, credit)
        H = GH
        NG = 7
        I_G, I_CUM, I_BETA, I_NEG, I_OUT, I_IN, I_LAST = range(NG)

        h_t, stage, x, g_post, g_ffn = kept.h_t, kept.stage, kept.x, kept.g_post, kept.g_ffn
        w_hi, w_lo = kept.split[:, 0], kept.split[:, 1]
        left, right = stage[:, 0], stage[:, 1]
        qkv = left[:, 0:A_TILES * P].rearrange("p (c s) -> p c s", s=P)
        zw = left[:, A_TILES * P:(A_TILES + H) * P].rearrange("p (h c) -> p h c", c=P)
        row = right[:, 0:ROW]
        o = right[:, ROW:ROW + H * P].rearrange("p (h c) -> p h c", c=P)
        gates = sb("gates", [P, T, NG, H])
        gs = sb("gs", [P, 2, NG, H])
        ab = sb("ab", [P, T, 2, H])
        g_tmp = right[:, ROW + H * P:ROW + H * P + 6 * T * H].rearrange("p (n t h) -> p n t h", n=6, h=H)
        a_log = sb("a_log", [P, H])
        dt_bias = sb("dt_bias", [P, H])
        a_exp = sb("a_exp", [P, H])
        power = sb("power", [P, 2 * H])
        squares = sb("squares", [P, 2 * H, P])
        g_tri = sb("g_tri", [P, H, P])
        norm2 = sb("norm2", [P, 2, 2, 2 * H])
        k_tok = sb("k_tok", [P, H, P])
        k_t = sb("k_t", [P, H, P])
        q_t = sb("q_t", [P, H, P])
        k_out = sb("k_out", [P, H, P])
        b_v = sb("b_v", [P, H, P])
        dec_t = sb("dec_t", [P, H, P])
        dec = sb("dec", [P, H, P])
        low = sb("low", [P, H, P])
        low_t = sb("low_t", [P, H, P])
        qk_t = sb("qk_t", [P, H, P])
        inv = sb("inv", [P, H, P])
        inv_t = sb("inv_t", [P, H, P])
        off = sb("off", [P, H, P])
        beta_low = squares[:, 0:H]
        state = sb("state", [P, H, P])
        resid = sb("resid", [P, H, P])
        v_new = sb("v_new", [P, H, P])
        o_stat = sb("o_stat", [P, 5, H])
        norm_w = sb("norm_w", [P, P])
        junk_o = sb("junk_o", [P, H, P], BF16)
        q_b = sb("q_b", [P, QH // 2, P])
        k_dup = sb("k_dup", [P, KVH, 2, HD])
        k_b = sb("k_b", [P, KVH, 2, P])
        v_b = sb("v_b", [P, 2, KVH * HD])
        scores = sb("scores", [P, 4, 2, P])
        p_t = sb("p_t", [P, 4, 2, P])
        masks = sb("masks", [P, 4, P])
        sinks = sb("sinks", [P, QH])
        c_stat = sb("c_stat", [P, 7, QH])
        mix_a = sb("mix_a", [P, H * P])
        mix_c = sb("mix_c", [P, 2, D - H * P])
        mix_hi = sb("mix_hi", [P, KD, P], F32R)
        mix_lo = sb("mix_lo", [P, KD, P], F32R)
        d_stat = sb("d_stat", [P, 6])
        y = sb("y", [P, D])
        table = sb("table", [P, T_CUR])
        tab = lambda at: table[:, at:at + P]
        ident, tri, strict, ones = tab(T_ID), tab(T_TRI), tab(T_STRICT), tab(T_ONES)
        over_heads = lambda m: m.unsqueeze(1).broadcast_to([P, H, P])
        over_cols = lambda s: s.unsqueeze(2).broadcast_to([P, H, P])
        flat = lambda m: m.rearrange("p a b -> p (a b)")

        ps = {n: ctx.enter_context(nc.psum_tensor("m_ps_" + n, [P, HALF], F32)) for n in ("a0", "a1", "a2", "c0")}
        ps_d = kept.sums[:, 0:2]
        ps["b0"], ps["b1"] = kept.sums[:, 2], kept.sums[:, 3]
        bank = lambda n: ps[n][:].rearrange("p (h c) -> p h c", c=P)

        fills = {"a0": 9, "a1": 9, "a2": 7, "b0": 3, "b1": 2, "c0": 12, "d0": 2, "d1": 2}
        frees = {"a0": 8, "a1": 8, "a2": 7, "b0": 2, "c0": 10, "d0": 2, "d1": 2}
        full = {n: tally(n + "_full", k, k if n[0] == "d" else 0) for n, k in fills.items()}
        free = {n: tally(n + "_free", k, k if n[0] == "d" else 0) for n, k in frees.items()}

        s_load, s_tab, s_ab, s_w = sem("load"), sem("tab"), sem("ab"), sem("w")
        s_whi, s_wlo, s_zero, s_gate = sem("whi"), sem("wlo"), sem("zero"), sem("gate")
        s_gv, s_ga, s_ps_g = sem("gate_vector"), sem("gate_scalar"), sem("gate_sums")
        s_order = sem("order")
        qkv_in, row_in = tally("qkv_in", 16), tally("row_in", 16)
        x_in, x_out = tally("x_in", 16, 16), tally("x_out", 16, 16)
        gs_set, tri_set, squared = tally("gs_set"), tally("tri_set"), tally("squared")
        n2, rn, khat, qt_set, kout_set = (tally(n) for n in ("n2", "rn", "khat", "qt_set", "kout_set"))
        clipped, dec_exp, dec_masked = tally("clipped", 2), tally("dec_exp", 2), tally("dec_masked", 2)
        beta_set, init, init_t = tally("beta_set"), tally("init", 2), tally("init_t", 2)
        st_set, o1_set, o_set = tally("st_set"), tally("o1_set"), tally("o_set")
        o_sq, o_n, o_ms, o_rstd, zw_set, mixa = tally("o_sq"), tally("o_n", 2), tally("o_ms"), tally("o_rstd", 2), tally("zw_set"), tally("mixa")
        kdup_set, vb_set = tally("kdup_set"), tally("vb_set")
        cmax, cneg, csub = tally("cmax", 2), tally("cneg", 2), tally("csub", 2)
        cexp, csink, cden, crec, mixb = tally("cexp", 2), tally("csink", 2), tally("cden", 2), tally("crec", 2), tally("mixb", 2)
        dhi, dsq, dms, drstd = (tally(n, 2, 2) for n in ("dhi", "dsq", "dms", "drstd"))
        dx, dh = (tally(n, 1, 1) for n in ("dx", "dh"))
        e_full, e_free = (tally(n, 2, 2) for n in ("e_full", "e_free"))

        LV = len(LEVELS) - 1

        def halves(m, n, which):
            s = LEVELS[n]
            return m.rearrange("p h (g two s) -> p h g two s", two=2, s=s)[:, :, :, which]

        def half_cols(m, h, n, which):
            s = LEVELS[n]
            return m[:, h].rearrange("p (g two s) -> p g two s", two=2, s=s)[:, :, which]

        def ps_half(n, which):
            s = LEVELS[n]
            return ps["a2"][:, 256 * which:256 * which + 256].rearrange("p (h g s) -> p h g s", h=H, s=s)

        w_rows = io["w_out"].rearrange("o (k p) n -> p (o k) n", p=P)
        qkv_flat = io["qkv"].rearrange("t p c s -> (t p c s)")
        rows_flat = io["rows"].rearrange("t p n -> (t p n)")
        x_flat = io["x"].rearrange("o s d -> (o s d)")
        res_flat = io["res"].rearrange("t p d -> (t p d)")

        def carry(eng):
            eng.sem_inc(s_order, 1)

        block = ctx.enter_context(nc.Block("mix"))

        def steps(eng, step):
            step(0, 0, True, True, False, False)
            step(1, 1, True, True, True, False)
            with eng.Fori(1, T // 2 - 1) as i:
                step(i * 2, 0, True, True, True, True)
                step(i * 2 + 1, 1, True, True, True, True)
            step(T - 2, 0, False, True, True, True)
            step(T - 1, 1, False, False, True, True)

        @block.sync
        def _(sp):
            def reg(v):
                return v if isinstance(v, int) else sp.snap(v)

            def ready(*needs):
                values = [(s, s.at(t, k)) for s, t, k in needs]
                for s, v in [(s, reg(v)) for s, v in values if not isinstance(v, int) or v > s.credit]:
                    sp.wait_ge(s.sem, v)
                    carry(sp)

            def load_qkv(u):
                at = reg(u * (P * A_TILES * P))
                ready((full["a1"], u - 1, 2), (qt_set, u - 1, 1), (squared, u - 1, 1))
                sp.dma_start(flat(qkv), qkv_flat[bass.ds(at, P * A_TILES * P)].rearrange("(p n) -> p n", p=P)).then_inc(
                    qkv_in.sem, 16)

            def load_row(t):
                at = reg(t * (P * ROW))
                ready((full["c0"], t - 1, 1), (zw_set, t - 1, 1), (kdup_set, t - 1, 1), (vb_set, t - 1, 1))
                sp.dma_start(row, rows_flat[bass.ds(at, P * ROW)].rearrange("(p n) -> p n", p=P)).then_inc(row_in.sem, 16)

            def load_x(v):
                at = reg(v * (P * D))
                ready((x_out, v - 1, 16), (dh, v - 1, 1))
                sp.dma_start(x[:], x_flat[bass.ds(at, P * D)].rearrange("(p n) -> p n", p=P)).then_inc(x_in.sem, 16)

            def store_x(v):
                at = reg(v * (P * D))
                ready((dx, v, 1))
                sp.dma_start(res_flat[bass.ds(at, P * D)].rearrange("(p n) -> p n", p=P), x[:]).then_inc(x_out.sem, 16)

            sp.sem_inc(x_in.sem, 16)
            sp.sem_inc(x_out.sem, 16)
            sp.dma_start(ab[:].rearrange("p t c h -> p t (c h)"), io["rows"][:, :, AB0:Q0].rearrange("t p n -> p t n")).then_inc(s_ab, 16)
            sp.dma_start(a_log[:], io["gdn_A_log"][0:1, :].broadcast_to([P, H])).then_inc(s_ab, 16)
            sp.dma_start(dt_bias[:], io["gdn_dt_bias"][0:1, :].broadcast_to([P, H])).then_inc(s_ab, 16)
            sp.dma_start(table[:, 0:T_LEVEL], io["tables"][:, 0:T_LEVEL]).then_inc(s_tab, 16)
            load_qkv(0)
            load_row(0)
            sp.dma_start(table[:, T_LEVEL:], io["tables"][:, T_LEVEL:T_CUR]).then_inc(s_load, 16)
            for m, at in enumerate((T_CUR, T_PREV, T_CUR)):
                sp.dma_start(masks[:, m], io["tables"][:, at:at + P]).then_inc(s_load, 16)
            sp.dma_start(norm_w[:], io["gdn_norm_w"][0:1, :].broadcast_to([P, P])).then_inc(s_load, 16)
            sp.dma_start(sinks[:], io["attn_sinks"][0:1, :].broadcast_to([P, QH])).then_inc(s_load, 16)
            sp.dma_start(g_post[:], io["g_post_mix"][0:1, :].broadcast_to([P, D])).then_inc(s_load, 16)
            sp.dma_start(g_ffn[:], io["g_pre_ffn"][0:1, :].broadcast_to([P, D])).then_inc(s_load, 16)
            sp.dma_start(h_t[:], w_rows).then_inc(s_w, 16)
            load_qkv(1)

            def step(t, par, n, a, d, e):
                if a:
                    load_row(t + 1)
                if n:
                    load_qkv(t + 2)
                if e:
                    store_x(t - 2)
                if d:
                    load_x(t - 1)

            steps(sp, step)
            store_x(T - 2)
            load_x(T - 1)
            last = T - 1
            ready((full["a1"], last, 2), (qt_set, last, 1), (squared, last, 1), (full["c0"], last, 1), (kdup_set, last, 1),
                  (vb_set, last, 1), (zw_set, last, 1), (o_sq, last, 1), (mixa, last, 1))
            for kind in range(2):
                src = io["w_up"].rearrange("o (k p) n -> p (o k) n", p=P)[:, :, kind * DFF:kind * DFF + 2 * P]
                sp.dma_start(stage[:, kind].rearrange("p (k n) -> p k n", k=KD), src).then_inc(kept.s_stage[kind], 16)
            sp.wait_ge(x_in.sem, 16 * (T + 1))
            sp.wait_ge(x_out.sem, 16 * T)

        LOADS = 16 * 8

        @block.gpsimd
        def _(pool):
            pool.memset(power[:], -0.5).then_inc(s_zero, 1)
            pool.memset(state[:], 0.0).then_inc(s_zero, 1)
            pool.memset(k_b[:], 0.0).then_inc(s_zero, 1)
            pool.memset(v_b[:], 0.0).then_inc(s_zero, 1)
            pool.memset(masks[:, 3], NEG).then_inc(s_zero, 1)
            pool.wait_ge(s_zero, 5)

            def a_gates(u, par):
                after(pool, st_set, u - 2)
                after(pool, o1_set, u - 2)
                carry(pool)
                pool.tensor_copy(gs[:, par].rearrange("p n h -> p (n h)"),
                                 gates[:, bass.ds(u, 1)].rearrange("p t n h -> p (t n h)")).then_inc(gs_set.sem, 1)
                after(pool, gs_set, u)
                after(pool, full["a1"], u - 1, 3)
                pool.tensor_tensor(g_tri[:], over_heads(tri), over_cols(gs[:, par, I_G]), ALU.mult).then_inc(tri_set.sem, 1)

            def a_rnorm(u, par):
                after(pool, n2, u)
                pool.tensor_tensor(norm2[:, par, 1], norm2[:, par, 0], power[:], ALU.pow).then_inc(rn.sem, 1)

            def a_kout(u, par):
                after(pool, khat, u)
                after(pool, full["b0"], u - 1, 3)
                pool.tensor_tensor(k_out[:], k_tok[:], over_cols(gs[:, par, I_OUT]), ALU.mult).then_inc(kout_set.sem, 1)

            def a_beta(u, par):
                after(pool, gs_set, u)
                after(pool, n2, u)
                pool.tensor_tensor(beta_low, over_heads(strict), over_cols(gs[:, par, I_BETA]), ALU.mult).then_inc(beta_set.sem, 1)

            def a_masks(u):
                after(pool, dec_exp, u, 1)
                after(pool, beta_set, u)
                pool.tensor_tensor(dec[:], dec[:], beta_low, ALU.mult).then_inc(dec_masked.sem, 1)
                after(pool, dec_exp, u, 2)
                pool.tensor_tensor(dec_t[:], dec_t[:], over_heads(tri), ALU.mult).then_inc(dec_masked.sem, 1)

            def a_init_t(u):
                after(pool, free["a1"], u, 3)
                after(pool, full["b0"], u - 1, 2)
                pool.tensor_tensor(inv_t[:], low_t[:], over_heads(tab(T_LEVEL0T)), ALU.mult).then_inc(init_t.sem, 1)
                after(pool, init_t, u, 1)
                pool.tensor_tensor(inv_t[:], inv_t[:], over_heads(ident), ALU.add).then_inc(init_t.sem, 1)

            def c_kdup(t):
                after(pool, row_in, t)
                after(pool, full["c0"], t - 1, 2)
                carry(pool)
                pool.tensor_copy(k_dup[:], row[:, K0:V0].rearrange("p (k d) -> p k d", d=HD).unsqueeze(2).broadcast_to(
                    [P, KVH, 2, HD])).then_inc(kdup_set.sem, 1)

            def c_vb(t, par):
                after(pool, full["c0"], t - 1, 12)
                carry(pool)
                pool.tensor_copy(v_b[:, par], row[:, V0:ROW]).then_inc(vb_set.sem, 1)

            def b_zw(t):
                after(pool, mixa, t - 1)
                pool.tensor_tensor(zw, row[:, 0:H * P].rearrange("p (h c) -> p h c", c=P), over_heads(norm_w[:]),
                                   ALU.mult).then_inc(zw_set.sem, 1)

            def b_scale(t, par):
                rq = norm2[:, par, 1, 0:H]
                after(pool, rn, t)
                pool.tensor_tensor(o_stat[:, 1], rq, rq, ALU.mult).then_inc(o_n.sem, 1)
                after(pool, o_sq, t)
                after(pool, o_n, t, 1)
                pool.tensor_tensor(o_stat[:, 2], o_stat[:, 1], o_stat[:, 0], ALU.mult).then_inc(o_n.sem, 1)

            def b_rstd(t, par):
                after(pool, o_ms, t)
                pool.tensor_tensor(o_stat[:, 4], o_stat[:, 3], power[:, 0:H], ALU.pow).then_inc(o_rstd.sem, 1)
                after(pool, o_rstd, t, 1)
                after(pool, mixa, t - 1)
                pool.tensor_tensor(o_stat[:, 4], o_stat[:, 4], norm2[:, par, 1, 0:H], ALU.mult).then_inc(o_rstd.sem, 1)

            def d_rstd(v, n):
                after(pool, dms, v, n)
                pool.tensor_tensor(d_stat[:, 3 * n - 1:3 * n], d_stat[:, 3 * n - 2:3 * n - 1], power[:, 0:1], ALU.pow).then_inc(drstd.sem, 1)

            def d_res(v):
                after(pool, free["d1"], v, 2)
                after(pool, x_in, v)
                pool.tensor_tensor(x[:], x[:], y[:], ALU.add).then_inc(dx.sem, 1)

            pool.wait_ge(s_tab, 16)
            pool.wait_ge(s_gate, 1)
            a_gates(0, 0)
            a_rnorm(0, 0)
            a_beta(0, 0)
            c_kdup(0)
            a_kout(0, 0)
            a_masks(0)
            pool.wait_ge(s_load, LOADS)
            a_init_t(0)
            c_vb(0, 0)
            a_rnorm(1, 1)
            a_gates(1, 1)
            b_zw(0)

            def step(t, par, n, a, d, e):
                if a:
                    a_beta(t + 1, 1 - par)
                if e:
                    d_rstd(t - 2, 1)
                if a:
                    c_kdup(t + 1)
                    a_kout(t + 1, 1 - par)
                    a_masks(t + 1)
                b_scale(t, par)
                b_rstd(t, par)
                if a:
                    a_init_t(t + 1)
                if e:
                    d_res(t - 2)
                    d_rstd(t - 2, 2)
                if a:
                    c_vb(t + 1, 1 - par)
                    b_zw(t + 1)
                if n:
                    a_rnorm(t + 2, par)
                    a_gates(t + 2, par)

            steps(pool, step)
            d_rstd(T - 2, 1)
            d_res(T - 2)
            d_rstd(T - 2, 2)

        @block.scalar
        def _(act):
            def a_square(u):
                after(act, qkv_in, u)
                after(act, dec_masked, u - 1, 1)
                act.activation(squares[:], qkv[:, 0:2 * H], ACT.Square).then_inc(squared.sem, 1)

            def a_q(u):
                after(act, full["b1"], u - 1, 1)
                act.copy(q_t[:], qkv[:, 0:H]).then_inc(qt_set.sem, 1)

            def a_kt(u):
                after(act, full["a0"], u, 2)
                after(act, full["b0"], u - 1, 1)
                act.copy(k_t[:], bank("a0")).then_inc(free["a0"].sem, 1)

            def a_exp_(u):
                after(act, clipped, u, 2)
                act.activation(dec[:], dec[:], ACT.Exp, scale=-1.0).then_inc(dec_exp.sem, 1)
                act.activation(dec_t[:], dec_t[:], ACT.Exp).then_inc(dec_exp.sem, 1)

            def a_lowt(u):
                after(act, full["a1"], u, 4)
                act.copy(low_t[:], bank("a1")).then_inc(free["a1"].sem, 1)

            def a_invt(u, n):
                after(act, full["a1"], u, 4 + n)
                act.copy(inv_t[:], bank("a1")).then_inc(free["a1"].sem, 1)

            def b_v_new(t):
                after(act, full["b0"], t, 2)
                after(act, full["b1"], t - 1, 2)
                act.copy(v_new[:], bank("b0")).then_inc(free["b0"].sem, 1)

            def b_square(t):
                after(act, o_set, t)
                after(act, o_ms, t - 1)
                for h in range(H):
                    op = act.activation(junk_o[:, h], o[:, h], ACT.Square, accum_out=o_stat[:, 0, h:h + 1])
                op.then_inc(o_sq.sem, 1)

            def c_qb(t):
                after(act, full["c0"], t, 1)
                act.copy(q_b[:], bank("c0")).then_inc(free["c0"].sem, 1)

            def c_kb(t, par):
                after(act, full["c0"], t, 2)
                act.copy(k_b[:, :, par], bank("c0")[:, 0:KVH]).then_inc(free["c0"].sem, 1)

            def c_exp(t, r):
                after(act, cneg, t, r + 1)
                after(act, mixb, t - 1, r + 1)
                for h in range(4):
                    op = act.activation(scores[:, h].rearrange("p a b -> p (a b)"), scores[:, h].rearrange("p a b -> p (a b)"), ACT.Exp,
                                        bias=c_stat[:, 2, 4 * r + h:4 * r + h + 1], accum_out=c_stat[:, 3, 4 * r + h:4 * r + h + 1])
                op.then_inc(cexp.sem, 1)
                after(act, csub, t, r + 1)
                act.activation(c_stat[:, 4, 4 * r:4 * r + 4], c_stat[:, 4, 4 * r:4 * r + 4], ACT.Exp).then_inc(csink.sem, 1)

            def c_pt(t, n):
                use = (5, 6, 10, 11)[n]
                after(act, full["c0"], t, use)
                act.copy(p_t[:, 2 * (n % 2):2 * (n % 2) + 2].rearrange("p h k c -> p (h k) c"), bank("c0")).then_inc(free["c0"].sem, 1)

            def d_hi(v):
                for b in range(2):
                    after(act, full[f"d{b}"], v, 1)
                    after(act, full["d1"], v - 1, 2)
                    act.copy(mix_hi[:, 4 * b:4 * b + 4], ps_d[:, b].rearrange("p (k c) -> p k c", c=P)).then_inc(dhi.sem, 1)

            def d_square(v, n):
                if n == 1:
                    after(act, e_full, v - 1)
                    after(act, full["d0"], v, 2)
                    after(act, full["d1"], v, 2)
                    src = ps_d.rearrange("p a b -> p (a b)")
                else:
                    after(act, dx, v)
                    src = x[:]
                act.activation(y[:], src, ACT.Square, accum_out=d_stat[:, 3 * n - 3:3 * n - 2]).then_inc(dsq.sem, 1)

            def d_out(v):
                act.wait_ge(s_wlo, KD)
                for b in range(2):
                    after(act, e_full, v, b + 1)
                    act.copy(h_t[:, 4 * b:4 * b + 4, bass.ds(v * P, P)], bank(f"b{b}")).then_inc(e_free.sem, 1)

            act.wait_ge(s_ab, 48)
            act.activation(a_exp[:], a_log[:], ACT.Exp).then_inc(s_ga, 1)
            act.activation(g_tmp[:, 3], ab[:, :, 1], ACT.Exp, scale=-1.0).then_inc(s_ga, 1)
            act.wait_ge(s_gv, 2)
            act.activation(g_tmp[:, 2], g_tmp[:, 1], ACT.Exp, scale=-1.0).then_inc(s_ga, 1)
            act.wait_ge(s_gv, 3)
            act.activation(g_tmp[:, 2], g_tmp[:, 2], ACT.Ln).then_inc(s_ga, 1)
            act.wait_ge(s_ps_g, 1)
            sums = ps["b0"][:, 0:2 * T * H].rearrange("p (c t h) -> p c t h", c=2, h=H)
            act.activation(gates[:, :, I_IN], sums[:, 0], ACT.Exp).then_inc(s_ga, 1)
            act.activation(gates[:, :, I_LAST], sums[:, 1], ACT.Exp).then_inc(s_ga, 1)
            act.wait_ge(s_gv, 9)
            act.activation(gates[:, :, I_OUT], g_tmp[:, 4], ACT.Exp).then_inc(s_ga, 1)
            a_square(0)
            a_q(0)
            c_qb(0)
            a_kt(0)
            c_kb(0, 0)
            a_exp_(0)
            a_lowt(0)
            c_exp(0, 0)
            a_invt(0, 1)
            c_pt(0, 0)
            c_pt(0, 1)
            a_invt(0, 2)
            a_square(1)
            a_invt(0, 3)
            c_exp(0, 1)
            a_invt(0, 4)
            c_pt(0, 2)
            a_invt(0, 5)
            c_pt(0, 3)
            act.wait_ge(s_w, 16)
            for k in range(KD):
                act.copy(w_hi[:, k], h_t[:, k]).then_inc(s_whi, 1)

            def step(t, par, n, a, d, e):
                if e:
                    d_square(t - 2, 1)
                b_v_new(t)
                if a:
                    a_q(t + 1)
                    c_qb(t + 1)
                if d:
                    d_hi(t - 1)
                if a:
                    a_kt(t + 1)
                    c_kb(t + 1, 1 - par)
                    a_exp_(t + 1)
                b_square(t)
                if a:
                    a_lowt(t + 1)
                    c_exp(t + 1, 0)
                    a_invt(t + 1, 1)
                    c_pt(t + 1, 0)
                if e:
                    d_square(t - 2, 2)
                if a:
                    c_pt(t + 1, 1)
                    a_invt(t + 1, 2)
                if n:
                    a_square(t + 2)
                if a:
                    a_invt(t + 1, 3)
                    c_exp(t + 1, 1)
                    a_invt(t + 1, 4)
                if e:
                    d_out(t - 2)
                if a:
                    c_pt(t + 1, 2)
                    a_invt(t + 1, 5)
                    c_pt(t + 1, 3)

            steps(act, step)
            d_square(T - 2, 1)
            d_hi(T - 1)
            d_square(T - 2, 2)
            d_out(T - 2)

        @block.vector
        def _(dve):
            def a_bv(u, par):
                after(dve, full["a1"], u, 2)
                after(dve, gs_set, u)
                after(dve, free["b0"], u - 1, 1)
                dve.tensor_tensor(b_v[:], bank("a1"), over_cols(gs[:, par, I_BETA]), ALU.mult).then_inc(free["a1"].sem, 1)

            def a_n2(u, par):
                after(dve, full["a1"], u, 1)
                after(dve, o_rstd, u - 2)
                dve.tensor_scalar(norm2[:, par, 0], ps["a1"][:, 0:2 * H], EPS, None, ALU.add).then_inc(n2.sem, 1)

            def a_khat(u, par):
                after(dve, rn, u)
                after(dve, full["a0"], u, 1)
                after(dve, kout_set, u - 1)
                dve.tensor_tensor(k_tok[:], bank("a0"), over_cols(norm2[:, par, 1, H:2 * H]), ALU.mult).then_inc(khat.sem, 1)

            def a_diff(u, par):
                after(dve, full["a1"], u, 3)
                dve.tensor_tensor(dec[:], bank("a1"), over_cols(gs[:, par, I_CUM]), ALU.subtract).then_inc(free["a1"].sem, 1)
                after(dve, free["a1"], u, 2)
                dve.tensor_scalar(dec_t[:], dec[:], 0.0, None, ALU.min).then_inc(clipped.sem, 1)
                after(dve, clipped, u, 1)
                dve.tensor_scalar(dec[:], dec[:], 0.0, None, ALU.max).then_inc(clipped.sem, 1)

            def a_low(u):
                after(dve, dec_masked, u, 1)
                after(dve, full["a0"], u, 3)
                dve.tensor_tensor(low[:], bank("a0"), dec[:], ALU.mult).then_inc(free["a0"].sem, 1)

            def a_qk(u):
                after(dve, dec_masked, u, 2)
                after(dve, full["a2"], u, 1)
                after(dve, full["b1"], u - 1, 2)
                dve.tensor_tensor(qk_t[:], bank("a2"), dec_t[:], ALU.mult).then_inc(free["a2"].sem, 1)

            def a_init(u):
                after(dve, free["a0"], u, 2)
                dve.tensor_tensor(off[:], low[:], over_heads(tab(T_LEVEL)), ALU.mult).then_inc(init.sem, 1)
                after(dve, init, u, 1)
                dve.tensor_tensor(inv[:], off[:], over_heads(ident), ALU.add).then_inc(init.sem, 1)

            def a_off(u, n):
                after(dve, full["a0"], u, 3 + n)
                if n == 1:
                    after(dve, init, u, 2)
                dve.tensor_tensor(off[:], bank("a0"), over_heads(tab(T_LEVEL + n * P)), ALU.mult).then_inc(free["a0"].sem, 1)

            def a_inv(u, n):
                after(dve, full["a2"], u, 1 + n)
                m, which = (inv, 0) if n < LV else (inv_t, 1)
                dve.tensor_tensor(halves(m[:], n, which), ps_half(n, which), halves(m[:], n, which), ALU.add).then_inc(
                    free["a2"].sem, 1)

            def b_resid(t, par):
                after(dve, full["b0"], t, 1)
                for h in range(H):
                    op = dve.scalar_tensor_tensor(resid[:, h], bank("b0")[:, h], gs[:, par, I_NEG, h:h + 1], b_v[:, h], ALU.mult, ALU.add)
                op.then_inc(free["b0"].sem, 1)

            def b_state(t, par):
                after(dve, full["b0"], t, 3)
                after(dve, full["b1"], t, 1)
                for h in range(H):
                    op = dve.scalar_tensor_tensor(state[:, h], state[:, h], gs[:, par, I_LAST, h:h + 1], bank("b0")[:, h], ALU.mult, ALU.add)
                op.then_inc(st_set.sem, 1)

            def b_o1(t, par):
                after(dve, full["b1"], t, 1)
                dve.tensor_tensor(o, bank("b1"), over_cols(gs[:, par, I_IN]), ALU.mult).then_inc(o1_set.sem, 1)

            def b_o(t):
                after(dve, full["b1"], t, 2)
                after(dve, o1_set, t)
                dve.tensor_tensor(o, bank("b1"), o, ALU.add).then_inc(o_set.sem, 1)

            def b_ms(t):
                after(dve, o_n, t, 2)
                dve.tensor_scalar(o_stat[:, 3], o_stat[:, 2], 1.0 / P, EPS * DK, ALU.mult, ALU.add).then_inc(o_ms.sem, 1)

            def b_mix(t):
                after(dve, o_rstd, t, 2)
                after(dve, zw_set, t)
                after(dve, full["d1"], t - 1, 1)
                for h in range(H):
                    op = dve.scalar_tensor_tensor(mix_a[:, h * P:(h + 1) * P], o[:, h], o_stat[:, 4, h:h + 1], zw[:, h], ALU.mult, ALU.mult)
                op.then_inc(mixa.sem, 1)

            def c_scores(t, par, n):
                after(dve, full["c0"], t, (3, 4, 8, 9)[n])
                carry(dve)
                at = 2 if isinstance(t, int) and t == 0 else par
                mask = masks[:, at:at + 2].rearrange("p a b -> p (a b)")
                for h in range(2):
                    slot = n % 2 + 2 * h
                    op = dve.tensor_tensor_reduce(scores[:, slot].rearrange("p a b -> p (a b)"),
                                                  ps["c0"][:, 256 * h:256 * h + 256], mask, HD ** -0.5, -3e38, ALU.add, ALU.max,
                                                  c_stat[:, 0, 4 * (n // 2) + slot:4 * (n // 2) + slot + 1])
                op.then_inc(free["c0"].sem, 1)

            def c_max(t, r):
                q = slice(4 * r, 4 * r + 4)
                after(dve, free["c0"], t, (4, 8)[r])
                dve.tensor_tensor(c_stat[:, 1, q], c_stat[:, 0, q], sinks[:, q], ALU.max).then_inc(cmax.sem, 1)
                after(dve, cmax, t, r + 1)
                dve.tensor_scalar(c_stat[:, 2, q], c_stat[:, 1, q], -1.0, None, ALU.mult).then_inc(cneg.sem, 1)
                dve.tensor_tensor(c_stat[:, 4, q], sinks[:, q], c_stat[:, 1, q], ALU.subtract).then_inc(csub.sem, 1)

            def c_out(t, par, r):
                q = slice(4 * r, 4 * r + 4)
                after(dve, cexp, t, r + 1)
                after(dve, csink, t, r + 1)
                dve.tensor_tensor(c_stat[:, 5, q], c_stat[:, 3, q], c_stat[:, 4, q], ALU.add).then_inc(cden.sem, 1)
                after(dve, cden, t, r + 1)
                dve.reciprocal(c_stat[:, 6, q], c_stat[:, 5, q]).then_inc(crec.sem, 1)
                after(dve, crec, t, r + 1)
                after(dve, full["c0"], t, (7, 12)[r])
                after(dve, full["d1"], t - 2, 1)
                cols = slice(r * 4 * HD, (r + 1) * 4 * HD)
                dve.tensor_tensor(mix_c[:, par, cols].rearrange("p (h d) -> p h d", d=HD), ps["c0"][:, 0:4 * HD].rearrange("p (h d) -> p h d", d=HD),
                                  c_stat[:, 6, q].unsqueeze(2).broadcast_to([P, 4, HD]), ALU.mult).then_inc(mixb.sem, 1)

            def d_lo(v):
                for b in range(2):
                    after(dve, dhi, v, b + 1)
                    after(dve, full["d1"], v - 1, 2)
                    dve.tensor_tensor(mix_lo[:, 4 * b:4 * b + 4], ps_d[:, b].rearrange("p (k c) -> p k c", c=P),
                                      mix_hi[:, 4 * b:4 * b + 4].bitcast(F32), ALU.subtract).then_inc(free[f"d{b}"].sem, 1)

            def d_ms(v, n):
                after(dve, dsq, v, n)
                dve.tensor_scalar(d_stat[:, 3 * n - 2:3 * n - 1], d_stat[:, 3 * n - 3:3 * n - 2], 1.0 / D, EPS, ALU.mult,
                                  ALU.add).then_inc(dms.sem, 1)

            def d_res(v):
                after(dve, drstd, v, 1)
                after(dve, e_full, v - 1)
                for b in range(2):
                    cols = slice(b * HALF, (b + 1) * HALF)
                    dve.scalar_tensor_tensor(y[:, cols], ps_d[:, b], d_stat[:, 2:3], g_post[:, cols], ALU.mult, ALU.mult).then_inc(
                        free[f"d{b}"].sem, 1)

            def d_norm(v):
                after(dve, drstd, v, 2)
                after(dve, free["d1"], v, 2)
                dve.scalar_tensor_tensor(y[:], x[:], d_stat[:, 5:6], g_ffn[:], ALU.mult, ALU.mult).then_inc(dh.sem, 1)

            for s in [full[n] for n in ("d0", "d1")] + [free[n] for n in ("d0", "d1")] + [dhi, dsq, dms, drstd, dx, dh, e_full, e_free]:
                dve.sem_inc(s.sem, s.credit)
            n_gv = [0]

            def gv(op):
                op.then_inc(s_gv, 1)
                n_gv[0] += 1
                dve.wait_ge(s_gv, n_gv[0])

            by_tile = lambda m: m.unsqueeze(1).broadcast_to([P, T, H])
            dve.wait_ge(s_ab, 48)
            gv(dve.tensor_tensor(g_tmp[:, 0], ab[:, :, 0], by_tile(dt_bias[:]), ALU.add))
            gv(dve.scalar_tensor_tensor(g_tmp[:, 1], g_tmp[:, 0], -1.0, g_tmp[:, 0], ALU.mult, ALU.max))
            dve.wait_ge(s_ga, 3)
            gv(dve.tensor_scalar(g_tmp[:, 2], g_tmp[:, 2], 1.0, None, ALU.add))
            gv(dve.tensor_scalar(g_tmp[:, 3], g_tmp[:, 3], 1.0, None, ALU.add))
            gv(dve.reciprocal(gates[:, :, I_BETA], g_tmp[:, 3]))
            dve.wait_ge(s_ga, 4)
            gv(dve.scalar_tensor_tensor(g_tmp[:, 5], g_tmp[:, 0], 0.0, g_tmp[:, 2], ALU.max, ALU.add))
            gv(dve.scalar_tensor_tensor(gates[:, :, I_G], g_tmp[:, 5], -1.0, by_tile(a_exp[:]), ALU.mult, ALU.mult))
            dve.wait_ge(s_ga, 6)
            sums = ps["b0"][:, 0:2 * T * H].rearrange("p (c t h) -> p c t h", c=2, h=H)
            gv(dve.tensor_copy(gates[:, :, I_CUM], sums[:, 0]))
            gv(dve.tensor_tensor(g_tmp[:, 4], sums[:, 1], gates[:, :, I_CUM], ALU.subtract))
            dve.wait_ge(s_ga, 7)
            dve.scalar_tensor_tensor(gates[:, :, I_NEG], gates[:, :, I_BETA], -1.0, gates[:, :, I_IN], ALU.mult, ALU.mult).then_inc(s_gate, 1)
            a_n2(0, 0)
            a_bv(0, 0)
            a_khat(0, 0)
            a_diff(0, 0)
            dve.wait_ge(s_load, LOADS)
            dve.wait_ge(s_zero, 5)
            c_scores(0, 0, 0)
            a_low(0)
            a_qk(0)
            a_init(0)
            c_scores(0, 0, 1)
            c_max(0, 0)
            a_off(0, 1)
            a_inv(0, 1)
            a_off(0, 2)
            a_inv(0, 2)
            a_off(0, 3)
            c_out(0, 0, 0)
            a_inv(0, 3)
            c_scores(0, 0, 2)
            a_off(0, 4)
            c_scores(0, 0, 3)
            c_max(0, 1)
            a_inv(0, 4)
            a_off(0, 5)
            a_inv(0, 5)
            a_off(0, 6)
            a_n2(1, 1)
            a_inv(0, 6)
            c_out(0, 0, 1)

            def w_split(k):
                dve.wait_ge(s_whi, k + 1)
                dve.tensor_tensor(w_lo[:, k], h_t[:, k], w_hi[:, k].bitcast(F32), ALU.subtract).then_inc(s_wlo, 1)

            def step(t, par, n, a, d, e):
                b_resid(t, par)
                if a:
                    a_bv(t + 1, 1 - par)
                if e:
                    d_ms(t - 2, 1)
                if a:
                    a_khat(t + 1, 1 - par)
                if e:
                    d_res(t - 2)
                b_o1(t, par)
                if a:
                    a_diff(t + 1, 1 - par)
                b_state(t, par)
                if d:
                    d_lo(t - 1)
                b_o(t)
                if a:
                    c_scores(t + 1, 1 - par, 0)
                    a_low(t + 1)
                    a_qk(t + 1)
                b_ms(t)
                if a:
                    a_init(t + 1)
                    c_scores(t + 1, 1 - par, 1)
                    c_max(t + 1, 0)
                    a_off(t + 1, 1)
                b_mix(t)
                if not d:
                    w_split(0)
                    w_split(1)
                if a:
                    a_inv(t + 1, 1)
                    a_off(t + 1, 2)
                    if not d:
                        w_split(2)
                    a_inv(t + 1, 2)
                if e:
                    d_ms(t - 2, 2)
                if a:
                    a_off(t + 1, 3)
                    if not d:
                        w_split(3)
                    c_out(t + 1, 1 - par, 0)
                    a_inv(t + 1, 3)
                if e:
                    d_norm(t - 2)
                if a:
                    c_scores(t + 1, 1 - par, 2)
                    a_off(t + 1, 4)
                    if not d:
                        w_split(4)
                    c_scores(t + 1, 1 - par, 3)
                    c_max(t + 1, 1)
                    a_inv(t + 1, 4)
                    if not d:
                        w_split(5)
                    a_off(t + 1, 5)
                    if not d:
                        w_split(6)
                    a_inv(t + 1, 5)
                    a_off(t + 1, 6)
                    if not d:
                        w_split(7)
                if n:
                    a_n2(t + 2, par)
                if a:
                    a_inv(t + 1, 6)
                    c_out(t + 1, 1 - par, 1)

            steps(dve, step)
            d_ms(T - 2, 1)
            d_res(T - 2)
            d_lo(T - 1)
            d_ms(T - 2, 2)
            d_norm(T - 2)

        @block.tensor
        def _(pe):
            def fill(name, t, k):
                after(pe, free[name], t if k > 1 else t - 1, k - 1 if k > 1 else None)

            def a_tr(u):
                after(pe, qkv_in, u)
                fill("a0", u, 1)
                for h in range(H):
                    op = pe.transpose(bank("a0")[:, h], qkv[:, H + h], ident)
                op.then_inc(full["a0"].sem, 1)
                after(pe, n2, u)
                for h in range(H):
                    op = pe.transpose(bank("a1")[:, h], qkv[:, 2 * H + h], ident)
                op.then_inc(full["a1"].sem, 1)

            def a_norms(u):
                after(pe, squared, u)
                after(pe, qkv_in, u)
                fill("a1", u, 1)
                for c in range(2 * H):
                    op = pe.matmul(ps["a1"][:, c:c + 1], squares[:, c], ones[:, 0:1], start=True, stop=True)
                op.then_inc(full["a1"].sem, 1)

            def a_sums(u):
                after(pe, tri_set, u)
                fill("a1", u, 2)
                pe.matmul(ps["a1"][:], ones, flat(g_tri[:]), start=True, stop=True).then_inc(full["a1"].sem, 1)

            def a_trk(u):
                after(pe, khat, u)
                for h in range(H):
                    op = pe.transpose(bank("a0")[:, h], k_tok[:, h], ident)
                op.then_inc(full["a0"].sem, 1)

            def a_kk(u):
                after(pe, free["a0"], u, 1)
                for h in range(H):
                    op = pe.matmul(bank("a0")[:, h], k_t[:, h], k_t[:, h], start=True, stop=True)
                op.then_inc(full["a0"].sem, 1)

            def a_kq(u):
                fill("a2", u, 1)
                after(pe, qt_set, u)
                for h in range(H):
                    op = pe.matmul(bank("a2")[:, h], k_t[:, h], q_t[:, h], start=True, stop=True)
                op.then_inc(full["a2"].sem, 1)

            def a_trl(u):
                after(pe, free["a0"], u, 2)
                fill("a1", u, 3)
                for h in range(H):
                    op = pe.transpose(bank("a1")[:, h], low[:, h], ident)
                op.then_inc(full["a1"].sem, 1)

            def a_off(u, n):
                if n == 1:
                    after(pe, init, u, 2)
                    after(pe, free["a1"], u, 3)
                else:
                    after(pe, free["a2"], u, n)
                for h in range(H):
                    op = pe.matmul(bank("a0")[:, h], low_t[:, h], inv[:, h], start=True, stop=True)
                op.then_inc(full["a0"].sem, 1)

            def a_inv(u, n):
                after(pe, free["a0"], u, 2 + n)
                if n == 1:
                    after(pe, init_t, u, 2)
                else:
                    after(pe, free["a1"], u, 2 + n)
                after(pe, free["a2"], u, n)
                for h in range(H):
                    if n < LV:
                        op = pe.matmul(ps_half(n, 0)[:, h], inv_t[:, h], half_cols(off[:], h, n, 0), start=True, stop=True)
                    else:
                        op = pe.matmul(ps_half(n, 1)[:, h], off[:, h], half_cols(inv_t[:], h, n, 1), start=True, stop=True)
                op.then_inc(full["a2"].sem, 1)

            def a_trinv(u, n):
                after(pe, free["a1"], u, 2 + n)
                after(pe, free["a2"], u, 1 + n)
                for h in range(H):
                    op = pe.transpose(bank("a1")[:, h], inv[:, h], ident)
                op.then_inc(full["a1"].sem, 1)

            def b_ks(t):
                after(pe, st_set, t - 1)
                after(pe, e_free, t - 3)
                for h in range(H):
                    op = pe.matmul(bank("b0")[:, h], k_t[:, h], state[:, h], start=True, stop=True)
                op.then_inc(full["b0"].sem, 1)

            def b_vnew(t):
                after(pe, free["b0"], t, 1)
                for h in range(H):
                    op = pe.matmul(bank("b0")[:, h], inv_t[:, h], resid[:, h], start=True, stop=True)
                op.then_inc(full["b0"].sem, 1)

            def b_o1(t):
                after(pe, o_set, t - 1)
                for h in range(H):
                    op = pe.matmul(bank("b1")[:, h], q_t[:, h], state[:, h], start=True, stop=True)
                op.then_inc(full["b1"].sem, 1)

            def b_ds(t):
                after(pe, free["b0"], t, 2)
                after(pe, kout_set, t)
                for h in range(H):
                    op = pe.matmul(bank("b0")[:, h], k_out[:, h], v_new[:, h], start=True, stop=True)
                op.then_inc(full["b0"].sem, 1)

            def b_o2(t):
                after(pe, o1_set, t)
                for h in range(H):
                    op = pe.matmul(bank("b1")[:, h], qk_t[:, h], v_new[:, h], start=True, stop=True)
                op.then_inc(full["b1"].sem, 1)

            def c_trq(t):
                after(pe, row_in, t)
                after(pe, mixb, t - 1, 2)
                for b in range(4):
                    op = pe.transpose(bank("c0")[:, b], row[:, Q0 + b * P:Q0 + (b + 1) * P], ident)
                op.then_inc(full["c0"].sem, 1)

            def c_trk(t):
                after(pe, kdup_set, t)
                after(pe, free["c0"], t, 1)
                for kv in range(KVH):
                    op = pe.transpose(bank("c0")[:, kv], k_dup[:, kv].rearrange("p a d -> p (a d)"), ident)
                op.then_inc(full["c0"].sem, 1)

            def c_scores(t, n):
                if n == 2:
                    after(pe, mixb, t, 1)
                else:
                    after(pe, free["c0"], t, (2, 3, None, 7)[n])
                for h in range(2):
                    part = slice(n % 2 * HD, (n % 2 + 1) * HD)
                    op = pe.matmul(ps["c0"][:, 256 * h:256 * h + 256], q_b[part, n // 2 * 2 + h], k_b[part, n // 2].rearrange("p a b -> p (a b)"),
                                   start=True, stop=True)
                op.then_inc(full["c0"].sem, 1)

            def c_trp(t, n):
                after(pe, cexp, t, n // 2 + 1)
                after(pe, free["c0"], t, (4, 5, 8, 9)[n])
                for j in range(4):
                    op = pe.transpose(bank("c0")[:, j], scores[:, 2 * (n % 2) + j // 2, j % 2], ident)
                op.then_inc(full["c0"].sem, 1)

            def c_pv(t, r):
                after(pe, free["c0"], t, (6, 10)[r])
                after(pe, vb_set, t)
                for h in range(4):
                    for kt in range(2):
                        op = pe.matmul(ps["c0"][:, h * HD:(h + 1) * HD], p_t[:, h, kt], v_b[:, kt, r * HD:(r + 1) * HD],
                                       start=(kt == 0), stop=(kt == 1))
                op.then_inc(full["c0"].sem, 1)

            def d_tr(v, par):
                after(pe, mixa, v)
                after(pe, mixb, v, 2)
                for b in range(2):
                    fill(f"d{b}", v, 1)
                    for j in range(4):
                        src = mix_c[:, par] if b else mix_a[:]
                        op = pe.transpose(ps_d[:, b, j * P:(j + 1) * P], src[:, j * P:(j + 1) * P], ident)
                    op.then_inc(full[f"d{b}"].sem, 1)

            def d_mm(v, half, ks):
                if half == 0 and ks[0] == 0:
                    pe.wait_ge(s_wlo, KD)
                    after(pe, free["d0"], v, 1)
                    after(pe, free["d1"], v, 1)
                cols = slice(half * HALF, (half + 1) * HALF)
                for k in ks:
                    pe.matmul(ps_d[:, half], mix_hi[:, k], w_hi[:, k, cols], start=(k == 0), stop=False)
                    pe.matmul(ps_d[:, half], mix_hi[:, k], w_lo[:, k, cols], start=False, stop=False)
                    op = pe.matmul(ps_d[:, half], mix_lo[:, k], w_hi[:, k, cols], start=False, stop=(k == KD - 1))
                if ks[-1] == KD - 1:
                    op.then_inc(full[f"d{half}"].sem, 1)

            def d_tr2(v, t):
                after(pe, st_set, t)
                after(pe, o_set, t)
                after(pe, dh, v)
                after(pe, e_free, v - 1)
                for b in range(2):
                    for j in range(4):
                        k = 4 * b + j
                        op = pe.transpose(bank(f"b{b}")[:, j], y[:, k * P:(k + 1) * P], ident)
                    op.then_inc(e_full.sem, 1)

            pe.wait_ge(s_tab, 16)
            pe.wait_ge(s_gv, 7)
            for c, m in enumerate((tri, ones)):
                op = pe.matmul(ps["b0"][:, c * T * H:(c + 1) * T * H].rearrange("p (t h) -> p t h", h=H), m, gates[:, :, I_G],
                               start=True, stop=True)
            op.then_inc(s_ps_g, 1)
            a_norms(0)
            a_tr(0)
            c_trq(0)
            pe.wait_ge(s_zero, 5)
            a_sums(0)
            a_trk(0)
            c_trk(0)
            a_kk(0)
            c_scores(0, 0)
            a_kq(0)
            c_scores(0, 1)
            a_trl(0)
            a_off(0, 1)
            a_inv(0, 1)
            a_off(0, 2)
            a_trinv(0, 1)
            c_trp(0, 0)
            a_inv(0, 2)
            c_trp(0, 1)
            a_off(0, 3)
            a_trinv(0, 2)
            c_pv(0, 0)
            a_inv(0, 3)
            c_scores(0, 2)
            a_off(0, 4)
            a_trinv(0, 3)
            c_scores(0, 3)
            a_inv(0, 4)
            a_off(0, 5)
            a_trinv(0, 4)
            a_inv(0, 5)
            c_trp(0, 2)
            a_off(0, 6)
            a_trinv(0, 5)
            a_norms(1)
            c_trp(0, 3)
            a_inv(0, 6)
            c_pv(0, 1)

            def step(t, par, n, a, d, e):
                A = (lambda f, *w: f(t + 1, *w)) if a else (lambda f, *w: None)
                D_ = (lambda f, *w: f(t - 1, *w)) if d else (lambda f, *w: None)
                after(pe, free["a2"], t)
                b_ks(t)
                A(a_tr)
                b_vnew(t)
                A(a_sums)
                D_(d_tr, 1 - par)
                A(c_trq)
                b_o1(t)
                A(a_trk)
                b_ds(t)
                A(c_trk)
                b_o2(t)
                A(a_kk)
                A(c_scores, 0)
                A(a_kq)
                D_(d_mm, 0, [0, 1])
                A(c_scores, 1)
                D_(d_mm, 0, [2, 3])
                A(a_trl)
                D_(d_mm, 0, [4, 5, 6])
                A(a_off, 1)
                D_(d_mm, 0, [7])
                A(a_inv, 1)
                D_(d_mm, 1, [0])
                A(a_off, 2)
                A(a_trinv, 1)
                A(c_trp, 0)
                A(a_inv, 2)
                A(c_trp, 1)
                D_(d_mm, 1, [1])
                A(a_off, 3)
                A(a_trinv, 2)
                A(c_pv, 0)
                A(a_inv, 3)
                A(c_scores, 2)
                A(a_off, 4)
                A(a_trinv, 3)
                D_(d_mm, 1, [2])
                A(c_scores, 3)
                A(a_inv, 4)
                D_(d_mm, 1, [3])
                A(a_off, 5)
                A(a_trinv, 4)
                if e:
                    d_tr2(t - 2, t)
                A(a_inv, 5)
                A(c_trp, 2)
                D_(d_mm, 1, [4])
                A(a_off, 6)
                A(a_trinv, 5)
                A(c_trp, 3)
                D_(d_mm, 1, [5, 6])
                if n:
                    a_norms(t + 2)
                A(a_inv, 6)
                D_(d_mm, 1, [7])
                A(c_pv, 1)

            steps(pe, step)
            d_tr(T - 1, 1)
            d_mm(T - 1, 0, list(range(KD)))
            d_tr2(T - 2, T - 1)
            d_mm(T - 1, 1, list(range(KD)))


FT = DFF // P
FG = FT // 2


def ffn_block(nc, io, kept):
    with ExitStack() as ctx:
        sb = lambda name, shape, dt=F32: ctx.enter_context(nc.sbuf_tensor(name, shape, dt))
        sem = lambda name: ctx.enter_context(nc.semaphore(name))

        NT = FTAPS * 2 * FT
        h_t, raw, s_raw, ps_dn = kept.h_t, kept.stage, kept.s_stage, kept.sums
        h_hi, h_lo = kept.split[:, 0], kept.split[:, 1]
        acc = h_t[:].rearrange("p k s -> p (k s)").rearrange("p (t d) -> p t d", t=T)
        slab = 2 * P * KD
        w_hi = sb("f_w_hi", [P, 3, slab], F32R)
        w_lo = sb("f_w_lo", [P, 3, slab], F32R)
        conv = sb("f_conv", [P, 4, S])
        y_hi = sb("f_y_hi", [P, 2, S], F32R)
        y_lo = sb("f_y_lo", [P, 2, S], F32R)
        last_y = conv[:, 2]
        junk, gain = kept.x, kept.g_post
        ident = sb("f_ident", [P, P])
        rows_a = sb("f_rows_a", [P, P])
        rows_b = sb("f_rows_b", [NT + 2 * FT - P, P])
        taps = sb("f_taps", [P, NT + 2 * FT])
        stat = sb("f_stat", [P, 3, T])
        power = sb("f_power", [P, 1])
        last = sb("f_last", [P, 2, 3])

        ps_up = ctx.enter_context(nc.psum_tensor("f_ps_up", [P, 2, S], F32))

        s_ident, s_rows, s_gain = sem("f_ident_in"), sem("f_rows_in"), sem("f_gain_in")
        s_taps_ps, s_taps = sem("f_taps_ps"), sem("f_taps_ready")
        s_zero = sem("f_zero")
        s_lsq, s_lms, s_lrstd, s_ly = sem("f_lsq"), sem("f_lms"), sem("f_lrstd"), sem("f_ly")
        s_lx, s_lh, s_ltr, s_lout = sem("f_lx"), sem("f_lh"), sem("f_ltr"), sem("f_lout")
        s_hhi, s_hlo = sem("f_hhi"), sem("f_hlo")
        s_whi, s_wlo = sem("f_whi"), sem("f_wlo")
        s_pair = sem("f_pair")
        s_first, s_tap, s_conv = sem("f_first"), sem("f_tap"), sem("f_convolved")
        s_gelu, s_prod = sem("f_gelu"), sem("f_prod")
        s_yhi, s_ylo = sem("f_yhi"), sem("f_ylo")
        s_dn, s_acc = sem("f_dn"), sem("f_acc")
        s_freed, s_power = sem("f_freed"), sem("f_power_set")
        s_sq, s_ms, s_rstd, s_norm, s_res = sem("f_sq"), sem("f_ms"), sem("f_rstd"), sem("f_norm"), sem("f_res")
        s_xr = [sem(f"f_xr{t}") for t in range(T)]
        s_out = sem("f_out")

        w_up = io["w_up"].rearrange("o (k p) n -> p (o k) n", p=P)
        w_down = io["w_down"].rearrange("o f d -> (o f d)")
        GATE, VALUE, DOWN = 0, 1, 2

        def n_gate(g):
            return 3 * g

        def n_value(g):
            return 3 * g + 1

        def n_down(g):
            return 3 * g + 2

        LAST_DOWN = n_down(FG) - 2

        def steps(eng, step):
            with eng.Fori(1, FG - 1) as g:
                step(g, False)
            step(FG - 1, True)

        def up_w(part, kind):
            return (w_hi, w_lo)[part][:, kind].rearrange("p (k n) -> p k n", k=KD)

        def dn_w(part, kind):
            return (w_hi, w_lo)[part][:, kind].rearrange("p (k n) -> p k n", k=2)

        def y_of(part, last):
            if last:
                return (w_hi, w_lo)[part][:, VALUE].rearrange("p (c s) -> p c s", c=2)
            return (y_hi, y_lo)[part][:]

        OTHERS = [slice(0, HALF), slice(HALF, S - P)]
        LAST_COLS = slice(S - P, S)
        PARTS = 2 * KD + 2
        LEAD = 2

        block = ctx.enter_context(nc.Block("ffn"))

        def res_tile(t):
            return raw[:, 1 - t // 2, t % 2 * D:(t % 2 + 1) * D] if t < 4 else conv[:, t - 4]

        def residual(eng, t):
            eng.wait_ge(s_norm, t + 1)
            eng.wait_ge(s_xr[t], 16)
            if t >= T - 2:
                eng.wait_ge(s_res, t)
            eng.tensor_tensor(res_tile(t), res_tile(t), acc[:, t], ALU.add).then_inc(s_res, 1)

        @block.sync
        def _(sp):
            def reg(v):
                return v if isinstance(v, int) else sp.snap(v)

            def up_src(kind, g):
                return w_up[:, :, bass.ds(reg(g * (2 * P) + kind * DFF), 2 * P)]

            def down_src(g):
                return w_down[bass.ds(reg(g * (2 * P * D)), 2 * P * D)].rearrange("(k p d) -> p k d", k=2, p=P)

            def load(slot, src, k):
                sp.dma_start(raw[:, slot].rearrange("p (k n) -> p k n", k=k), src).then_inc(s_raw[slot], 16)

            def free(n):
                sp.wait_ge(s_whi, n)
                sp.wait_ge(s_wlo, n)
                sp.sem_inc(s_freed, 1)

            sp.dma_start(ident[:], io["tables"][:, T_ID:T_ID + P]).then_inc(s_ident, 16)
            rows = io["ffn_conv_w"].rearrange("o k (c p) -> (o k c) p", p=P)
            sp.dma_start(rows_a[:], rows[0:P]).then_inc(s_rows, 16)
            sp.dma_start(rows_b[0:NT - P], rows[P:NT]).then_inc(s_rows, 16)
            sp.dma_start(rows_b[NT - P:], io["ffn_conv_b"].rearrange("o (c p) -> (o c) p", p=P)).then_inc(s_rows, 16)
            sp.wait_ge(s_lx, 1)
            sp.dma_start(io["res"][T - 1], kept.x[:]).then_inc(s_lout, 16)
            free(1)
            load(0, up_src(GATE, 1), KD)
            free(2)
            load(1, up_src(VALUE, 1), KD)
            sp.wait_ge(s_lh, 1)
            sp.dma_start(gain[:], io["g_post_ffn"][0:1, :].broadcast_to([P, D])).then_inc(s_gain, 16)
            free(3)
            load(0, down_src(0), 2)

            def step(g, last):
                if not last:
                    value_free, gate_free, down_free = reg(n_value(g)), reg(n_down(g)), reg(n_gate(g + 1))
                    gate_from, value_from, down_from = up_src(GATE, g + 1), up_src(VALUE, g + 1), down_src(g)
                    free(value_free)
                    load(1, value_from, KD)
                    free(gate_free)
                    load(0, gate_from, KD)
                    free(down_free)
                    load(0, down_from, 2)
                else:
                    free(n_down(g))
                    load(0, down_src(g), 2)

            steps(sp, step)
            sp.wait_ge(s_lout, 16)
            free(LAST_DOWN)
            for t in range(4):
                sp.dma_start(res_tile(t), io["res"][t]).then_inc(s_xr[t], 16)
            sp.wait_ge(s_ylo, 2 * FG)
            sp.wait_ge(s_yhi, 2 * FG)
            for t in range(4, T):
                sp.dma_start(res_tile(t), io["res"][t]).then_inc(s_xr[t], 16)
            for t in range(T):
                sp.wait_ge(s_res, t + 1)
                sp.dma_start(io["out"][0, t * P:(t + 1) * P, :], res_tile(t)).then_inc(s_out, 16)
            sp.wait_ge(s_out, 16 * T)

        @block.scalar
        def _(act):
            def split(n, kind, slot, loads):
                act.wait_ge(s_raw[slot], 16 * loads)
                act.copy(w_hi[:, kind], raw[:, slot]).then_inc(s_whi, 1)

            def first(n, q, ct):
                act.wait_ge(s_pair, n + 1)
                act.activation(conv[:, q], ps_up[:, q % 2], ACT.Identity, bias=taps[:, bass.ds(ct + NT, 1)],
                               scale=taps[:, bass.ds(ct + (FTAPS - 1) * 2 * FT, 1)]).then_inc(s_first, 1)

            def step(g, last, lead=False):
                if not lead:
                    act.wait_ge(s_dn, g * 16 - 15)
                    split(n_down(g), DOWN, 0, g * 2 + 1)
                    act.wait_ge(s_prod, 2 * g)
                for c in range(2):
                    first(4 * g + c, c, g * 2 + c)
                for c in range(2):
                    act.wait_ge(s_conv, 4 * g + c + 3)
                    act.activation(conv[:, c], conv[:, c], ACT.Gelu_apprx_tanh).then_inc(s_gelu, 1)
                if not last:
                    act.wait_ge(s_pair, 4 * g + 2)
                    split(n_gate(g + 1), GATE, 0, 2 * g + 2)
                else:
                    act.wait_ge(s_pair, 4 * g + 2)
                    split(LAST_DOWN, GATE, 0, 2 * FG)
                if not lead:
                    act.wait_ge(s_ylo, 2 * g)
                for c in range(2):
                    first(4 * g + 2 + c, 2 + c, g * 2 + (c + FT))
                if not last:
                    act.wait_ge(s_pair, 4 * g + 4)
                    split(n_value(g + 1), VALUE, 1, g + 2)
                for c in range(2):
                    act.wait_ge(s_prod, 2 * g + c + 1)
                    if last:
                        act.wait_ge(s_pair, 4 * g + 4)
                    elif not lead:
                        act.wait_ge(s_dn, 16 * g + 1)
                    act.copy(y_of(0, last)[:, c], conv[:, 2 + c]).then_inc(s_yhi, 1)

            def h_hi_part(part, k):
                act.copy(h_hi[:, k, OTHERS[part]], h_t[:, k, OTHERS[part]]).then_inc(s_hhi, 1)

            y_flat = ps_dn[:, 0:2].rearrange("p a b -> p (a b)")
            split(1, GATE, 0, 1)
            act.activation(last_y, y_flat, ACT.Square, accum_out=last[:, 0, 0:1]).then_inc(s_lsq, 1)
            for k in range(KD):
                h_hi_part(0, k)
            act.wait_ge(s_lx, 1)
            act.activation(last_y, kept.x[:], ACT.Square, accum_out=last[:, 1, 0:1]).then_inc(s_lsq, 1)
            for k in range(KD):
                h_hi_part(1, k)
            for b in range(2):
                act.wait_ge(s_ltr, b + 1)
                act.copy(h_hi[:, 4 * b:4 * b + 4, LAST_COLS], ps_dn[:, 2 + b].rearrange("p (k c) -> p k c", c=P)).then_inc(s_hhi, 1)
            split(2, VALUE, 1, 1)
            act.wait_ge(s_taps, 1)
            step(0, False, lead=True)
            steps(act, step)
            for t in range(T):
                act.wait_ge(s_acc, 16 * (FG - 1) + 2 * t + 2 + 4)
                act.activation(junk[:], acc[:, t], ACT.Square, accum_out=stat[:, 0, t:t + 1]).then_inc(s_sq, 1)

        @block.vector
        def _(dve):
            dve.sem_inc(s_conv, 2)
            dve.sem_inc(s_acc, 4)

            def split(n, kind, slot):
                dve.wait_ge(s_whi, n)
                dve.tensor_tensor(w_lo[:, kind], raw[:, slot], w_hi[:, kind].bitcast(F32), ALU.subtract).then_inc(s_wlo, 1)

            def convolve(n, q, ct):
                dve.wait_ge(s_first, n + 1)
                for k in range(1, FTAPS):
                    op = dve.scalar_tensor_tensor(conv[:, q, k:S], ps_up[:, q % 2, 0:S - k],
                                                  taps[:, bass.ds(ct + (FTAPS - 1 - k) * 2 * FT, 1)], conv[:, q, k:S],
                                                  ALU.mult, ALU.add)
                    if k == 1:
                        op.then_inc(s_tap, 1)
                        dve.wait_ge(s_tap, n + 1)
                    else:
                        op.then_inc(s_conv, 1)

            def accumulate(m, t, half):
                dve.wait_ge(s_dn, m + 2)
                cols = acc[:, t, half * HALF:(half + 1) * HALF]
                dve.tensor_tensor(cols, ps_dn[:, (2 * t + half) % 4], cols, ALU.add).then_inc(s_acc, 1)

            def step(g, last, lead=False):
                if not lead:
                    split(n_down(g), DOWN, 0)
                for c in range(2):
                    convolve(4 * g + c, c, g * 2 + c)
                split(LAST_DOWN if last else n_gate(g + 1), GATE, 0)
                for c in range(2):
                    convolve(4 * g + 2 + c, 2 + c, g * 2 + (c + FT))
                def low_part(c):
                    dve.wait_ge(s_yhi, 2 * g + c + 1)
                    dve.tensor_tensor(y_of(1, last)[:, c], conv[:, 2 + c], y_of(0, last)[:, c].bitcast(F32), ALU.subtract).then_inc(
                        s_ylo, 1)

                for j in range(2 * T):
                    if not lead:
                        accumulate(g * 16 + (j - 16), j // 2, j % 2)
                    if j in (3, 6):
                        c = (j - 3) // 3
                        dve.wait_ge(s_gelu, 2 * g + c + 1)
                        dve.wait_ge(s_conv, 4 * g + c + 5)
                        dve.tensor_tensor(conv[:, 2 + c], conv[:, c], conv[:, 2 + c], ALU.mult).then_inc(s_prod, 1)
                    if j == 9 and not last:
                        split(n_value(g + 1), VALUE, 1)
                    if j in (9, 12) and last:
                        low_part((j - 9) // 3)
                if not last:
                    for c in range(2):
                        low_part(c)

            def finish(t):
                if t == T - 1:
                    residual(dve, t - 1)
                dve.wait_ge(s_rstd, t + 1)
                dve.scalar_tensor_tensor(acc[:, t], acc[:, t], stat[:, 2, t:t + 1], gain[:], ALU.mult, ALU.mult).then_inc(s_norm, 1)
                if t == T - 1:
                    residual(dve, t)

            def h_lo_part(part, k):
                dve.wait_ge(s_hhi, KD * part + k + 1)
                cols = OTHERS[part]
                dve.tensor_tensor(h_lo[:, k, cols], h_t[:, k, cols], h_hi[:, k, cols].bitcast(F32), ALU.subtract).then_inc(s_hlo, 1)

            def last_mean(n):
                dve.wait_ge(s_lsq, n + 1)
                dve.tensor_scalar(last[:, n, 1:2], last[:, n, 0:1], 1.0 / D, EPS, ALU.mult, ALU.add).then_inc(s_lms, 1)

            split(1, GATE, 0)
            last_mean(0)
            for k in range(LEAD):
                h_lo_part(0, k)
            dve.wait_ge(s_lrstd, 1)
            for b in range(2):
                cols = slice(b * HALF, (b + 1) * HALF)
                dve.scalar_tensor_tensor(last_y[:, cols], ps_dn[:, b], last[:, 0, 2:3], kept.g_post[:, cols], ALU.mult,
                                         ALU.mult).then_inc(s_ly, 1)
            for k in range(LEAD, KD):
                h_lo_part(0, k)
            last_mean(1)
            dve.wait_ge(s_lrstd, 2)
            dve.scalar_tensor_tensor(last_y, kept.x[:], last[:, 1, 2:3], kept.g_ffn[:], ALU.mult, ALU.mult).then_inc(s_lh, 1)
            for k in range(KD):
                h_lo_part(1, k)
            for b in range(2):
                dve.wait_ge(s_hhi, 2 * KD + b + 1)
                k = slice(4 * b, 4 * b + 4)
                dve.tensor_tensor(h_lo[:, k, LAST_COLS], ps_dn[:, 2 + b].rearrange("p (k c) -> p k c", c=P),
                                  h_hi[:, k, LAST_COLS].bitcast(F32), ALU.subtract).then_inc(s_hlo, 1)
            dve.wait_ge(s_taps_ps, 1)
            dve.tensor_copy(taps[:], ps_up[:, 1, HALF:HALF + NT + 2 * FT]).then_inc(s_taps, 1)
            split(2, VALUE, 1)
            dve.wait_ge(s_taps, 1)
            step(0, False, lead=True)
            dve.wait_ge(s_zero, 1)
            steps(dve, step)
            dve.wait_ge(s_gain, 16)
            for t in range(T + 1):
                if t < T:
                    for half in range(2):
                        accumulate(16 * (FG - 1) + 2 * t + half, t, half)
                if t >= 1:
                    finish(t - 1)
                if t < T:
                    dve.wait_ge(s_sq, t + 1)
                    dve.tensor_scalar(stat[:, 1, t:t + 1], stat[:, 0, t:t + 1], 1.0 / D, EPS, ALU.mult, ALU.add).then_inc(s_ms, 1)

        @block.gpsimd
        def _(pool):
            pool.memset(power[:], -0.5).then_inc(s_power, 1)
            pool.wait_ge(s_power, 1)
            for n in range(2):
                pool.wait_ge(s_lms, n + 1)
                pool.tensor_tensor(last[:, n, 2:3], last[:, n, 1:2], power[:], ALU.pow).then_inc(s_lrstd, 1)
                if n == 0:
                    pool.wait_ge(s_ly, 2)
                    pool.tensor_tensor(kept.x[:], kept.x[:], last_y, ALU.add).then_inc(s_lx, 1)
            pool.wait_ge(s_hlo, PARTS)
            pool.memset(acc, 0.0).then_inc(s_zero, 1)
            for t in range(T):
                pool.wait_ge(s_ms, t + 1)
                pool.tensor_tensor(stat[:, 2, t:t + 1], stat[:, 1, t:t + 1], power[:], ALU.pow).then_inc(s_rstd, 1)
                if 1 <= t < T - 1:
                    residual(pool, t - 1)

        @block.tensor
        def _(pe):
            def up(n, kind, c, halves=(0, 1), each=None):
                pe.wait_ge(s_conv, n + 1)
                for half in halves:
                    bank = ps_up[:, c, half * HALF:(half + 1) * HALF]
                    cols = slice(half * HALF, (half + 1) * HALF)
                    for k in range(KD):
                        hi = up_w(0, kind)[:, k, c * P:(c + 1) * P]
                        lo = up_w(1, kind)[:, k, c * P:(c + 1) * P]
                        if each:
                            pe.wait_ge(s_hlo, each + k)
                        pe.matmul(bank, hi, h_hi[:, k, cols], start=(k == 0), stop=False)
                        pe.matmul(bank, hi, h_lo[:, k, cols], start=False, stop=False)
                        op = pe.matmul(bank, lo, h_hi[:, k, cols], start=False, stop=(k == KD - 1))
                if 1 in halves:
                    op.then_inc(s_pair, 1)

            def down(g):
                last = isinstance(g, int) and g == FG
                kind = GATE if last else DOWN
                pe.wait_ge(s_wlo, LAST_DOWN if last else n_down(g))
                pe.wait_ge(s_ylo, 2 * g)
                for j in range(2 * T):
                    t, half = j // 2, j % 2
                    pe.wait_ge(s_acc, g * 16 + (j - 15))
                    for k in range(2):
                        y = slice(t * P, (t + 1) * P)
                        cols = slice(half * HALF, (half + 1) * HALF)
                        bank = ps_dn[:, j % 4]
                        pe.matmul(bank, y_of(0, last)[:, k, y], dn_w(0, kind)[:, k, cols], start=(k == 0), stop=False)
                        pe.matmul(bank, y_of(0, last)[:, k, y], dn_w(1, kind)[:, k, cols], start=False, stop=False)
                        op = pe.matmul(bank, y_of(1, last)[:, k, y], dn_w(0, kind)[:, k, cols], start=False, stop=(k == 1))
                    op.then_inc(s_dn, 1)

            def ups(g):
                for kind, n in ((GATE, n_gate(g)), (VALUE, n_value(g))):
                    pe.wait_ge(s_wlo, n)
                    for c in range(2):
                        up(4 * g + 2 * kind + c, kind, c)

            def step(g, last):
                ups(g)
                down(g)

            pe.sem_inc(s_dn, 1)
            pe.wait_ge(s_ident, 16)
            pe.wait_ge(s_rows, 48)
            nb = NT + 2 * FT - P
            pe.transpose(ps_up[:, 1, HALF:HALF + P], rows_a[:], ident[:])
            pe.transpose(ps_up[:, 1, HALF + P:HALF + P + nb], rows_b[:], ident[0:nb, 0:nb]).then_inc(s_taps_ps, 1)
            pe.wait_ge(s_wlo, 1)
            up(0, GATE, 0, (0,), each=1)
            pe.wait_ge(s_lh, 1)
            for b in range(2):
                for j in range(4):
                    op = pe.transpose(ps_dn[:, 2 + b, j * P:(j + 1) * P], last_y[:, (4 * b + j) * P:(4 * b + j + 1) * P], ident[:])
                op.then_inc(s_ltr, 1)
            up(1, GATE, 1, (0,))
            pe.wait_ge(s_hlo, PARTS)
            up(0, GATE, 0, (1,))
            pe.wait_ge(s_taps, 1)
            up(1, GATE, 1, (1,))
            pe.wait_ge(s_wlo, 2)
            for c in range(2):
                up(2 + c, VALUE, c)
            steps(pe, step)
            down(FG)


_INS = ["x", "g_pre_mix", "w_in", "gdn_conv_w", "gdn_A_log", "gdn_dt_bias", "gdn_norm_w", "attn_sinks", "w_out",
        "g_post_mix", "g_pre_ffn", "w_up", "ffn_conv_w", "ffn_conv_b", "w_down", "g_post_ffn"]


def kernel(**inputs):
    import concourse.bacc as bacc
    from concourse.bass_utils import run_bass_kernel_spmd

    nc = bacc.Bacc("TRN2", target_bir_lowering=False, num_devices=1)
    arrays, io = {}, {}
    for name in _INS:
        a = np.ascontiguousarray(inputs[name])
        arrays[f"in_{name}"] = a
        io[name] = nc.dram_tensor(f"in_{name}", a.shape, mybir.dt.from_np(a.dtype), kind="ExternalInput").ap()
    arrays["in_tables"] = tables()
    io["tables"] = nc.dram_tensor("in_tables", (P, T_W), F32, kind="ExternalInput").ap()
    SCR = "Internal"
    io["rows"] = nc.dram_tensor("rows", (T, P, ROW), F32, kind=SCR).ap()
    io["qkv"] = nc.dram_tensor("qkv", (T, P, A_TILES, P), F32, kind=SCR).ap()
    io["out"] = nc.dram_tensor("out", (1, S, D), F32, kind="ExternalOutput").ap()
    io["res"] = nc.dram_tensor("res", (T, P, D), F32, kind=SCR).ap()
    project_block(nc, io)
    with ExitStack() as ctx:
        kept = Kept(nc, ctx)
        mix_block(nc, io, kept)
        ffn_block(nc, io, kept)
    r = run_bass_kernel_spmd(nc, [arrays], core_ids=[0])
    return r.results[0]["out"]
```
